# Optimizing a Trainium2 kernel written in Bass

```python
import jax, jax.numpy as jnp
from jax import lax
import numpy as np

D_MODEL = 1024
BATCH = 1
SEQ = 512
DEPTH = 1

GRID_W = 64
N_HEADS = 8
HEAD_DIM = 64
ATTN_WIDTH = N_HEADS * HEAD_DIM
CONV_WIDTH = D_MODEL // 2
CONV_K = 3
WIN_ROWS_MAX = 8
WIN_COLS = 16
Q_COL_BLOCK = 16
KEY_COL_SPAN = 32
D_FF = 4 * D_MODEL
EPS = 1e-6
NEG_INF = -1e30
PROJ_SPLITS = [ATTN_WIDTH, ATTN_WIDTH, ATTN_WIDTH, CONV_WIDTH, CONV_WIDTH, CONV_WIDTH, D_MODEL]
PROJ_WIDTH = 3 * ATTN_WIDTH + 3 * CONV_WIDTH + 2 * D_MODEL


def rms_norm(x, g):
    xf = x.astype(jnp.float32)
    xf = xf * lax.rsqrt(jnp.mean(xf * xf, axis=-1, keepdims=True) + EPS)
    return xf.astype(x.dtype) * g

def _na_indices(rows):
    kr = min(WIN_ROWS_MAX, rows)
    r = np.arange(rows)
    row_start = np.clip(r - kr // 2, 0, rows - kr)
    key_rows = row_start[:, None] + np.arange(kr)[None, :]
    rel_r = key_rows - r[:, None] + WIN_ROWS_MAX - 1
    ncb = GRID_W // Q_COL_BLOCK
    j = np.arange(ncb)
    cb_start = np.clip(j * Q_COL_BLOCK - WIN_COLS // 2, 0, GRID_W - KEY_COL_SPAN)
    key_cols = cb_start[:, None] + np.arange(KEY_COL_SPAN)[None, :]
    q_cols = j[:, None] * Q_COL_BLOCK + np.arange(Q_COL_BLOCK)[None, :]
    win_start = np.clip(q_cols - WIN_COLS // 2, 0, GRID_W - WIN_COLS)
    kc = key_cols[:, None, :]
    col_mask = (kc >= win_start[..., None]) & (kc < win_start[..., None] + WIN_COLS)
    rel_c = np.clip(kc - q_cols[..., None] + WIN_COLS - 1, 0, 2 * WIN_COLS - 2)
    key_tok = key_rows[:, None, :, None] * GRID_W + key_cols[None, :, None, :]
    key_tok = key_tok.reshape(rows, ncb, kr * KEY_COL_SPAN).astype(np.int32)
    mask = np.broadcast_to(col_mask[:, :, None, :], (ncb, Q_COL_BLOCK, kr, KEY_COL_SPAN))
    mask = mask.reshape(ncb, Q_COL_BLOCK, kr * KEY_COL_SPAN)
    return kr, key_tok, rel_r.astype(np.int32), rel_c.astype(np.int32), mask

def neighbourhood_attention(q, k, v, rpb):
    B, S, H, dh = q.shape
    rows = S // GRID_W
    kr, key_tok, rel_r, rel_c, mask = _na_indices(rows)
    ncb = GRID_W // Q_COL_BLOCK
    qb = q.reshape(B, rows, ncb, Q_COL_BLOCK, H, dh)
    kb = k[:, key_tok]
    vb = v[:, key_tok]
    s = jnp.einsum('brjqhd,brjkhd->bhrjqk', qb, kb).astype(jnp.float32) * (dh ** -0.5)
    bias = rpb[:, rel_r[:, None, None, :, None], rel_c[None, :, :, None, :]]
    bias = bias.reshape(H, rows, ncb, Q_COL_BLOCK, kr * KEY_COL_SPAN).astype(jnp.float32)
    s = jnp.where(jnp.asarray(mask), s + bias[None], NEG_INF)
    p = jax.nn.softmax(s, axis=-1).astype(v.dtype)
    o = jnp.einsum('bhrjqk,brjkhd->brjqhd', p, vb)
    return o.reshape(B, S, H * dh)

def short_gated_conv(cb, cc, ch, w):
    z = cc * ch
    zp = jnp.pad(z, ((0, 0), (1, 1), (0, 0)))
    conv = zp[:, :-2] * w[0] + zp[:, 1:-1] * w[1] + zp[:, 2:] * w[2]
    return cb * conv

def first_inputs(seed: int = 0) -> dict:
    key = jax.random.key(seed)
    ks = jax.random.split(key, 16)
    f32 = jnp.float32

    def nrm(k, shape, scale):
        return jax.random.normal(k, shape, f32) * scale

    return {
        "x": nrm(ks[0], (BATCH, SEQ, D_MODEL), 1.0),
        "norm1_g": 1.0 + nrm(ks[1], (DEPTH, D_MODEL), 0.02),
        "w_in": nrm(ks[2], (DEPTH, D_MODEL, PROJ_WIDTH), D_MODEL ** -0.5),
        "q_norm_g": 1.0 + nrm(ks[3], (DEPTH, HEAD_DIM), 0.02),
        "k_norm_g": 1.0 + nrm(ks[4], (DEPTH, HEAD_DIM), 0.02),
        "rpb": nrm(ks[5], (DEPTH, N_HEADS, 2 * WIN_ROWS_MAX - 1, 2 * WIN_COLS - 1), 0.5),
        "conv_w": nrm(ks[6], (DEPTH, CONV_K, CONV_WIDTH), CONV_K ** -0.5),
        "w_attn_branch": nrm(ks[7], (DEPTH, ATTN_WIDTH, D_MODEL), ATTN_WIDTH ** -0.5),
        "w_conv_branch": nrm(ks[8], (DEPTH, CONV_WIDTH, D_MODEL), CONV_WIDTH ** -0.5),
        "w_o": nrm(ks[9], (DEPTH, D_MODEL, D_MODEL), D_MODEL ** -0.5),
        "norm2_g": 1.0 + nrm(ks[10], (DEPTH, D_MODEL), 0.02),
        "w_mlp_in": nrm(ks[11], (DEPTH, D_MODEL, D_FF), D_MODEL ** -0.5),
        "w_mlp_out": nrm(ks[12], (DEPTH, D_FF, D_MODEL), D_FF ** -0.5),
    }

def first_block(x, norm1_g, w_in, q_norm_g, k_norm_g, rpb, conv_w, w_attn_branch,
              w_conv_branch, w_o, norm2_g, w_mlp_in, w_mlp_out):
    B, S, _ = x.shape
    split_pts = [int(p) for p in np.cumsum(PROJ_SPLITS)]
    for l in range(DEPTH):
        u = rms_norm(x, norm1_g[l])
        proj = u @ w_in[l]
        q, k, v, cb, cc, ch, ga, gb = jnp.split(proj, split_pts, axis=-1)
        q = rms_norm(q.reshape(B, S, N_HEADS, HEAD_DIM), q_norm_g[l])
        k = rms_norm(k.reshape(B, S, N_HEADS, HEAD_DIM), k_norm_g[l])
        v = v.reshape(B, S, N_HEADS, HEAD_DIM)
        y_a = neighbourhood_attention(q, k, v, rpb[l]) @ w_attn_branch[l]
        y_b = short_gated_conv(cb, cc, ch, conv_w[l]) @ w_conv_branch[l]
        merged = jax.nn.sigmoid(ga) * y_a + jax.nn.sigmoid(gb) * y_b
        x = x + merged @ w_o[l]
        h = rms_norm(x, norm2_g[l]) @ w_mlp_in[l]
        x = x + jnp.square(jax.nn.relu(h)) @ w_mlp_out[l]
    return x


DEPTH_2 = 2

N_A_LAYERS = DEPTH_2 // 2
N_B_LAYERS = DEPTH_2 - N_A_LAYERS

D_FF_2 = 2816
RMS_EPS = 1e-6

RWKV_HEAD = 64
RWKV_HEADS = D_MODEL // RWKV_HEAD
DECAY_LORA = 64
AAA_LORA = 64
GATE_LORA = 128
GN_EPS = 64e-5

ATT_HEAD = 64
Q_HEADS = D_MODEL // ATT_HEAD
KV_HEADS = 4
GROUP = Q_HEADS // KV_HEADS
WINDOW = 128
BLOCK = 128
KV_WIDTH = KV_HEADS * ATT_HEAD
MASK_VALUE = -1e30


def rms_norm_2(x, g):
    xf = x.astype(jnp.float32)
    y = xf * lax.rsqrt(jnp.mean(xf * xf, axis=-1, keepdims=True) + RMS_EPS)
    return (y * g.astype(jnp.float32)).astype(x.dtype)

def swiglu(x, w_in, w_out):
    gate, up = jnp.split(x @ w_in, 2, axis=-1)
    return (jax.nn.silu(gate) * up) @ w_out

def rwkv7_time_mix(x, mu, w_rkv, w_o, w0, w1, w2, a0, a1, a2, g1, g2,
                   k_k, k_a, r_k, gn_g, gn_b):
    B, T, C = x.shape
    H, N = RWKV_HEADS, RWKV_HEAD
    f32 = jnp.float32
    x_prev = jnp.pad(x, ((0, 0), (1, 0), (0, 0)))[:, :-1]
    xx = x_prev - x
    xr, xw, xk, xv, xa, xg = [x + xx * mu[i] for i in range(6)]

    r = xr @ w_rkv[0]
    k = xk @ w_rkv[1]
    v = xv @ w_rkv[2]
    w = -jax.nn.softplus(-(w0 + jnp.tanh(xw @ w1) @ w2)) - 0.5
    decay = jnp.exp(-jnp.exp(w.astype(f32)))
    a = jax.nn.sigmoid(a0 + (xa @ a1) @ a2)
    g = jax.nn.sigmoid(xg @ g1) @ g2

    heads = lambda t: t.reshape(B, T, H, N).astype(f32)
    kk = heads(k * k_k)
    kk = kk / jnp.maximum(jnp.linalg.norm(kk, axis=-1, keepdims=True), 1e-12)
    k = k * (1.0 + (a - 1.0) * k_a)
    r_h, k_h, v_h, a_h, w_h = heads(r), heads(k), heads(v), heads(a), heads(decay)
    b_h = kk * a_h

    def step(S, inp):
        r_t, w_t, k_t, v_t, kk_t, b_t = inp
        sa = jnp.einsum('bhij,bhj->bhi', S, -kk_t)
        S = (S * w_t[:, :, None, :] + sa[..., None] * b_t[:, :, None, :]
             + v_t[..., None] * k_t[:, :, None, :])
        y = jnp.einsum('bhij,bhj->bhi', S, r_t)
        return S, y

    xs = tuple(jnp.moveaxis(t, 1, 0) for t in (r_h, w_h, k_h, v_h, kk, b_h))
    S0 = jnp.zeros((B, H, N, N), f32)
    _, y = lax.scan(step, S0, xs)
    y = jnp.moveaxis(y, 0, 1)

    mean = jnp.mean(y, axis=-1, keepdims=True)
    var = jnp.mean(jnp.square(y - mean), axis=-1, keepdims=True)
    y = ((y - mean) * lax.rsqrt(var + GN_EPS)).reshape(B, T, C)
    y = y * gn_g.astype(f32) + gn_b.astype(f32)
    bonus = jnp.sum(r_h * k_h * r_k.astype(f32), axis=-1, keepdims=True) * v_h
    y = (y + bonus.reshape(B, T, C)).astype(x.dtype)
    return (y * g) @ w_o

def swa_sinks(xq, k_sh, v_sh, w_q, b_q, w_o, b_o, sinks):
    B, T, _ = xq.shape
    NB = T // BLOCK
    q = (xq @ w_q + b_q).reshape(B, NB, BLOCK, KV_HEADS, GROUP, ATT_HEAD)

    def banded(t):
        t = t.reshape(B, NB, BLOCK, KV_HEADS, ATT_HEAD)
        prev = jnp.pad(t, ((0, 0), (1, 0), (0, 0), (0, 0), (0, 0)))[:, :-1]
        return jnp.concatenate([prev, t], axis=2)

    kb, vb = banded(k_sh), banded(v_sh)
    s = jnp.einsum('bnqkgd,bnskd->bnkgqs', q, kb).astype(jnp.float32) * (ATT_HEAD ** -0.5)
    blk = jnp.arange(NB)[:, None, None] * BLOCK
    q_pos = blk + jnp.arange(BLOCK)[None, :, None]
    k_pos = blk - BLOCK + jnp.arange(2 * BLOCK)[None, None, :]
    valid = (k_pos >= 0) & (k_pos <= q_pos) & (q_pos - k_pos < WINDOW)
    s = jnp.where(valid[None, :, None, None], s, MASK_VALUE)
    sink = jnp.broadcast_to(
        sinks.astype(jnp.float32).reshape(1, 1, KV_HEADS, GROUP, 1, 1), s.shape[:-1] + (1,))
    p = jax.nn.softmax(jnp.concatenate([s, sink], axis=-1), axis=-1)[..., :-1]
    o = jnp.einsum('bnkgqs,bnskd->bnqkgd', p.astype(vb.dtype), vb)
    o = o.reshape(B, T, Q_HEADS * ATT_HEAD)
    return o @ w_o + b_o

def second_inputs(seed: int = 0) -> dict:
    key = jax.random.key(seed)
    ks = iter(jax.random.split(key, 32))
    D, NA, NBL = D_MODEL, N_A_LAYERS, N_B_LAYERS
    f32 = jnp.float32

    def nrm(shape, scale):
        return scale * jax.random.normal(next(ks), shape, f32)

    def uni(shape, lo, hi):
        return jax.random.uniform(next(ks), shape, f32, lo, hi)

    return {
        "x": nrm((BATCH, SEQ, D), 1.0),
        "norm_g": 1.0 + nrm((DEPTH_2, 6, D), 0.05),
        "ffn_w_in": nrm((DEPTH_2, 2, D, 2 * D_FF_2), D ** -0.5),
        "ffn_w_out": nrm((DEPTH_2, 2, D_FF_2, D), D_FF_2 ** -0.5),
        "rwkv_mu": uni((NA, 6, D), 0.0, 1.0),
        "rwkv_w_rkv": nrm((NA, 3, D, D), D ** -0.5),
        "rwkv_w_o": nrm((NA, D, D), D ** -0.5),
        "rwkv_w0": uni((NA, D), -6.0, -1.0),
        "rwkv_w1": nrm((NA, D, DECAY_LORA), D ** -0.5),
        "rwkv_w2": nrm((NA, DECAY_LORA, D), 0.1 * DECAY_LORA ** -0.5),
        "rwkv_a0": nrm((NA, D), 0.1),
        "rwkv_a1": nrm((NA, D, AAA_LORA), D ** -0.5),
        "rwkv_a2": nrm((NA, AAA_LORA, D), 0.1 * AAA_LORA ** -0.5),
        "rwkv_g1": nrm((NA, D, GATE_LORA), D ** -0.5),
        "rwkv_g2": nrm((NA, GATE_LORA, D), GATE_LORA ** -0.5),
        "rwkv_k_k": 0.85 + nrm((NA, D), 0.05),
        "rwkv_k_a": 1.0 + nrm((NA, D), 0.05),
        "rwkv_r_k": nrm((NA, RWKV_HEADS, RWKV_HEAD), 0.1),
        "rwkv_gn_g": 1.0 + nrm((NA, D), 0.05),
        "rwkv_gn_b": nrm((NA, D), 0.02),
        "kv_norm_g": 1.0 + nrm((D,), 0.05),
        "w_kv": nrm((D, 2 * KV_WIDTH), D ** -0.5),
        "b_kv": nrm((2 * KV_WIDTH,), 0.02),
        "attn_w_q": nrm((NBL, D, Q_HEADS * ATT_HEAD), D ** -0.5),
        "attn_b_q": nrm((NBL, Q_HEADS * ATT_HEAD), 0.02),
        "attn_w_o": nrm((NBL, Q_HEADS * ATT_HEAD, D), (Q_HEADS * ATT_HEAD) ** -0.5),
        "attn_b_o": nrm((NBL, D), 0.02),
        "attn_sinks": nrm((NBL, Q_HEADS), 1.0),
    }

def second_block(x, norm_g, ffn_w_in, ffn_w_out,
              rwkv_mu, rwkv_w_rkv, rwkv_w_o, rwkv_w0, rwkv_w1, rwkv_w2,
              rwkv_a0, rwkv_a1, rwkv_a2, rwkv_g1, rwkv_g2, rwkv_k_k, rwkv_k_a,
              rwkv_r_k, rwkv_gn_g, rwkv_gn_b,
              kv_norm_g, w_kv, b_kv,
              attn_w_q, attn_b_q, attn_w_o, attn_b_o, attn_sinks):
    B, T, _ = x.shape
    h = x
    k_sh = v_sh = None
    for layer in range(DEPTH_2):
        g = norm_g[layer]
        h = h + 0.5 * rms_norm_2(swiglu(rms_norm_2(h, g[0]), ffn_w_in[layer, 0], ffn_w_out[layer, 0]), g[1])
        u = rms_norm_2(h, g[2])
        if layer < N_A_LAYERS:
            i = layer
            m = rwkv7_time_mix(u, rwkv_mu[i], rwkv_w_rkv[i], rwkv_w_o[i], rwkv_w0[i],
                               rwkv_w1[i], rwkv_w2[i], rwkv_a0[i], rwkv_a1[i], rwkv_a2[i],
                               rwkv_g1[i], rwkv_g2[i], rwkv_k_k[i], rwkv_k_a[i],
                               rwkv_r_k[i], rwkv_gn_g[i], rwkv_gn_b[i])
        else:
            j = layer - N_A_LAYERS
            m = swa_sinks(u, k_sh, v_sh, attn_w_q[j], attn_b_q[j], attn_w_o[j],
                          attn_b_o[j], attn_sinks[j])
        h = h + rms_norm_2(m, g[3])
        h = h + 0.5 * rms_norm_2(swiglu(rms_norm_2(h, g[4]), ffn_w_in[layer, 1], ffn_w_out[layer, 1]), g[5])
        if layer == N_A_LAYERS - 1:
            kv = rms_norm_2(h, kv_norm_g) @ w_kv + b_kv
            k_sh = kv[..., :KV_WIDTH].reshape(B, T, KV_HEADS, ATT_HEAD)
            v_sh = kv[..., KV_WIDTH:].reshape(B, T, KV_HEADS, ATT_HEAD)
    return h


def setup_inputs(seed=0):
    out = dict(first_inputs(seed))
    for name, value in second_inputs(seed + 1).items():
        if name != "x":
            out[name + "_2"] = value
    return out


def reference(
    x, norm1_g, w_in, q_norm_g, k_norm_g, rpb, conv_w, w_attn_branch, w_conv_branch, w_o,
    norm2_g, w_mlp_in, w_mlp_out, norm_g_2, ffn_w_in_2, ffn_w_out_2, rwkv_mu_2, rwkv_w_rkv_2,
    rwkv_w_o_2, rwkv_w0_2, rwkv_w1_2, rwkv_w2_2, rwkv_a0_2, rwkv_a1_2, rwkv_a2_2, rwkv_g1_2,
    rwkv_g2_2, rwkv_k_k_2, rwkv_k_a_2, rwkv_r_k_2, rwkv_gn_g_2, rwkv_gn_b_2, kv_norm_g_2,
    w_kv_2, b_kv_2, attn_w_q_2, attn_b_q_2, attn_w_o_2, attn_b_o_2, attn_sinks_2,
):
    x = first_block(
        x, norm1_g, w_in, q_norm_g, k_norm_g, rpb, conv_w, w_attn_branch, w_conv_branch, w_o,
        norm2_g, w_mlp_in, w_mlp_out,
    )
    return second_block(
        x, norm_g_2, ffn_w_in_2, ffn_w_out_2, rwkv_mu_2, rwkv_w_rkv_2, rwkv_w_o_2, rwkv_w0_2,
        rwkv_w1_2, rwkv_w2_2, rwkv_a0_2, rwkv_a1_2, rwkv_a2_2, rwkv_g1_2, rwkv_g2_2, rwkv_k_k_2,
        rwkv_k_a_2, rwkv_r_k_2, rwkv_gn_g_2, rwkv_gn_b_2, kv_norm_g_2, w_kv_2, b_kv_2,
        attn_w_q_2, attn_b_q_2, attn_w_o_2, attn_b_o_2, attn_sinks_2,
    )


_drawn_inputs = setup_inputs


def setup_inputs(seed=0):
    import zlib

    import numpy as np

    out = dict(_drawn_inputs(seed))
    spreads = {}
    factors = {'q_norm_g': 8.0,
     'k_norm_g': 8.0,
     'rwkv_w1_2': 8.0,
     'rwkv_w2_2': 8.0,
     'rwkv_gn_b_2': 3.492,
     'attn_b_q_2': 8.0}
    for name, (base, spread) in spreads.items():
        noise = np.random.default_rng([zlib.crc32(name.encode()), seed]).standard_normal(out[name].shape)
        drawn = base * np.exp(spread * noise) if base else spread * noise
        out[name] = __import__('jax').numpy.asarray(drawn.astype(out[name].dtype))
    for name, factor in factors.items():
        out[name] = (out[name] * factor).astype(out[name].dtype)
    return out
```

```python
from contextlib import ExitStack

import numpy as np
from concourse import mybir
from concourse.alu_op_type import AluOpType as ALU

F32 = mybir.dt.float32
F32R = mybir.dt.float32r
ACT = mybir.ActivationFunctionType
AX_X = mybir.AxisListType.X

P = 128
T = 512
D = 1024
NT = D // P
SLAB = 2048
EPS = 1e-6
GN_EPS = 64e-5
DECAY = float(np.exp(-0.5))
CH = 64
NCH = T // CH
FFN_TILES = 22
FFN_CHUNKS = (8, 8, 6)
MASKED = -1e30

_PARTS = [("qkvconv", 12), ("attn_branch", 2), ("conv_branch", 2), ("gates", 8), ("w_o", 4)]
for _c in range(4):
    _PARTS += [(f"mlp_in{_c}", 4), (f"mlp_out{_c}", 4)]


def _ffn_parts(f):
    out = []
    for c, n in enumerate(FFN_CHUNKS):
        out += [(f"ffn{f}_in{c}", n), (f"ffn{f}_out{c}", 4)]
    return out


_PARTS += _ffn_parts(0) + [("lora", 2), ("r", 4), ("k", 4), ("v", 4), ("rwkv_o", 4)] + _ffn_parts(1)
_PARTS += [("kv", 2)] + _ffn_parts(2) + [("q2", 4), ("o2", 4)] + _ffn_parts(3)
FIRST = {}
_n = 0
for _name, _k in _PARTS:
    FIRST[_name] = _n
    _n += _k
SLABS = _n

VEC = {}
_v = 0
for _name, _k in ([("norm1_g", 8), ("norm2_g", 8)] + [(f"norm_g{i}", 8) for i in range(12)]
                  + [(f"mu{i}", 8) for i in range(6)]
                  + [(n, 8) for n in ("w0", "a0", "k_k", "k_a", "r_k", "gn_g", "gn_b", "kv_norm_g", "b_q", "b_o")]
                  + [("b_kv", 4), ("q_norm_g", 1), ("k_norm_g", 1), ("conv_w", 12)]):
    VEC[_name] = _v
    _v += _k
NVEC = _v

CST = {}
_c0 = 0
for _name, _k in [("ident", 128), ("ones", 128), ("blk64", 128), ("blk1", 128), ("sel", 128), ("mean", 1),
                  ("strict", 64), ("incl", 64), ("eye", 64), ("first", 64), ("firstT", 64),
                  ("lev0", 64), ("lev1", 64), ("lev2", 64), ("lev3", 64), ("lev4", 64), ("sinks", 16)]:
    CST[_name] = _c0
    _c0 += _k
NCST = _c0


def constants():
    c = np.zeros((P, NCST), np.float32)
    i = np.arange(P)
    c[:, CST["ident"]:CST["ident"] + 128] = np.eye(P)
    c[:, CST["ones"]:CST["ones"] + 128] = 1
    blk = (i[:, None] // 64 == i[None, :] // 64)
    c[:, CST["blk64"]:CST["blk64"] + 128] = blk / 64
    c[:, CST["blk1"]:CST["blk1"] + 128] = blk
    for j in range(8):
        c[i, CST["sel"] + 16 * j + 2 * j + i // 64] = 1
    c[:, CST["mean"]] = 1 / D
    r, k = (i % 64)[:, None], np.arange(64)[None, :]
    c[:, CST["strict"]:CST["strict"] + 64] = r < k
    c[:, CST["incl"]:CST["incl"] + 64] = r <= k
    c[:, CST["eye"]:CST["eye"] + 64] = r == k
    c[:, CST["first"]:CST["first"] + 64] = -((r % 2 == 1) & (k == r - 1)).astype(np.float32)
    c[:, CST["firstT"]:CST["firstT"] + 64] = -((k % 2 == 1) & (r == k - 1)).astype(np.float32)
    for n, s in enumerate((2, 4, 8, 16, 32)):
        c[:, CST[f"lev{n}"]:CST[f"lev{n}"] + 64] = -(((r // s) % 2 == 1) & (k // s == r // s - 1)).astype(np.float32)
    return c


def spread_rows():
    return (np.arange(16)[:, None] == np.arange(1024)[None, :] // 64).astype(np.float32)


def scan_restart():
    return np.broadcast_to((np.arange(T) % CH != 0).astype(np.float32), (P, T)).copy()


NA_CLASS = (0, 1, 1, 2)
NA_KEY0 = (0, 8, 24, 32)


def na_tables():
    r, cc = np.divmod(np.arange(P), 16)
    kr, kc = np.divmod(np.arange(256), 32)
    mask = np.zeros((P, 3, 256), np.float32)
    rel_r = kr[None, :] - r[:, None] + 7
    rel_c = np.zeros((P, 3, 256), np.int64)
    for n, j in enumerate((0, 1, 3)):
        q = 16 * j + cc
        key = NA_KEY0[j] + kc
        start = np.clip(q - 8, 0, 48)
        ok = (key[None, :] >= start[:, None]) & (key[None, :] < start[:, None] + 16)
        mask[:, n, :] = np.where(ok, 0, MASKED)
        rel_c[:, n, :] = np.clip(key[None, :] - q[:, None] + 15, 0, 30)
    return mask, rel_r, rel_c


def swa_masks():
    q, s = np.arange(P)[:, None], np.arange(256)[None, :]
    ok = (s - 128 <= q) & (s > q)
    return np.stack([np.where(ok & (s >= 128), 0, MASKED), np.where(ok, 0, MASKED)], 1).astype(np.float32)


def build(nc, x_in, stream, vec_in, cst_in, spread_in, restart_in, bias_in, mask_in, swa_in,
          x_out):
    ctx = ExitStack()
    with ctx:
        def sb(name, shape, dt=F32):
            return ctx.enter_context(nc.sbuf_tensor(name, shape, dt))

        def sem(name):
            return ctx.enter_context(nc.semaphore(name))

        w_raw = sb("w_raw", [P, 2, SLAB])
        w_hi = sb("w_hi", [P, 2, SLAB], F32R)
        w_lo = sb("w_lo", [P, 2, SLAB], F32R)
        x = sb("x_res", [P, NT, T])
        ybuf = sb("ybuf", [P, NT, T + 2])
        work = sb("work", [P, 24, T])
        scratch = sb("scratch", [P, 4, T])
        vecs = sb("vecs", [P, NVEC])
        cst = sb("cst", [P, NCST])
        gains8 = sb("gains8", [P, 1])
        omu = sb("omu", [P, 48])
        oma = sb("oma", [P, 8])
        small = sb("small", [P, 32])
        area = sb("area", [P, 32, T])
        base = nc.sbuf_base - 32 * T * 4
        act_hi = nc.alloc_sbuf_tensor_at("act_hi", [P, NT, T], F32R, offset=base)
        act_lo = nc.alloc_sbuf_tensor_at("act_lo", [P, NT, T], F32R, offset=base + 8 * T * 4)
        hid_hi = nc.alloc_sbuf_tensor_at("hid_hi", [P, NT, T], F32R, offset=base + 16 * T * 4)
        hid_lo = nc.alloc_sbuf_tensor_at("hid_lo", [P, NT, T], F32R, offset=base + 24 * T * 4)
        ps = ctx.enter_context(nc.psum_tensor("ps", [P, 8, 512], F32))
        spill = nc.dram_tensor("spill", [8, P, NT, T], F32).ap()
        R_, K_, V_, LW_, A_, G_, Y_, BON_ = range(8)

        S = {n: sem(n) for n in (
            "consts_loaded", "x_loaded", "bias_loaded", "raw0_loaded", "raw1_loaded", "hi_made", "lo_made", "slab_mm",
            "banks0_free", "banks1_free",
            "sq_made", "sum_mm", "mean_made", "root_made", "diag_made", "rstd_mm", "u_made", "uhi_made", "ulo_made",
            "post_done",
            "gate_made", "hid_made", "tile_made",
            "qk_sq", "qk_sum", "qk_mean", "qk_root", "qk_recip", "qk_bcast", "qk_done",
            "at_s", "at_vblk", "at_vt", "at_max", "at_exp", "at_vtok", "at_p", "at_pt", "at_ptsb", "at_o", "at_osb",
            "branch_made", "merged_made", "conv_done", "out_stored",
            "t_made", "mix_made", "mix_hi", "mix_lo", "lora_mm", "lora_lo", "lora_out", "spilled",
            "duo_loaded", "duo_vec", "kk_sq", "kk_sum", "kk_max", "kk_root", "kk_recip", "act_prep", 
            "dve_prep", "job0_mm", "job1_mm", "job0_out", "job1_out",
            "rhs_mm", "rhs_out", "sa_mm", "sa_out", "st_mm", "st_out", "st_out1", "y_mm", "y_out",
            "gn_loaded", "gn_mean", "gn_d", "gn_sq", "gn_sum", "gn_var", "gn_root", "gn_recip", "gn_bcast",
            "gn_scaled", "gn_affine", "gn_gated", "gn_hi", "gn_lo", "swa_loaded", "vtok_mm", "vtok_out",
            "pe_waited", "spread_loaded", "dve_free", "gate_made2", "merged_hi",
        )}
        raw_loaded = (S["raw0_loaded"], S["raw1_loaded"])
        banks_free = (S["banks0_free"], S["banks1_free"])

        def c(name, a=0, n=None, p0=0, p1=P):
            n = n if n is not None else {"ident": 128, "ones": 128, "blk64": 128, "blk1": 128, "sel": 16}.get(name, 64)
            return cst[p0:p1, CST[name] + a:CST[name] + a + n]

        def vec(name, k=0):
            return vecs[:, VEC[name] + k:VEC[name] + k + 1]

        def pairs(t):
            return t[:, :, 0:T].rearrange("p (a b) t -> p a b t", b=2)

        def banks(a, n=2):
            return ps[:, a:a + n, :]

        yflat = ybuf[:].rearrange("p k t -> p (k t)")
        spread, rows16, restart = yflat[:, 0:1024], yflat[0:16, 1024:1536], yflat[:, 1536:2048]
        rows16b = scratch[0:16, 3, :]
        rows16b_duo = work[0:16, 22, :]
        MIX = (1, 4, 5, 0, 2, 3)

        def u_now(k):
            return ybuf[:, k, 1:T + 1]

        sinks = cst[:, NCST - 16:NCST]
        p_buf = yflat[:, 2048:3072].rearrange("p (b h k) -> p b h k", b=2, h=2)
        pt_buf = yflat[:, 3072:4096].rearrange("p (b h a k) -> p b h a k", b=2, h=2, a=2)
        vb_buf = scratch[:, 2, :].rearrange("p (b k) -> p b k", b=2)
        vt_buf = scratch[:, 3, :].rearrange("p (b a k) -> p b a k", b=2, a=2)

        NORMS = ["first", "mlp"]
        for f in range(4):
            NORMS += [f"ffn{f}_pre", f"ffn{f}_post"]
            if f == 0:
                NORMS += ["mixer0_pre", "mixer0_post"]
            if f == 1:
                NORMS += ["kv"]
            if f == 2:
                NORMS += ["mixer1_pre", "mixer1_post"]
        NORM = {n: i for i, n in enumerate(NORMS)}
        PRE = [n for n in NORMS if not n.endswith("post")]
        PRE_NO = {n: i for i, n in enumerate(PRE)}
        SPLIT_NO = {n: i for i, n in enumerate(n for n in PRE if n != "mixer0_pre")}
        POST_NO = {n: i for i, n in enumerate([n for n in NORMS if n.endswith("post")])}
        GAIN = {"first": "norm1_g", "mlp": "norm2_g", "kv": "kv_norm_g",
                "ffn0_pre": "norm_g0", "ffn0_post": "norm_g1", "mixer0_pre": "norm_g2", "mixer0_post": "norm_g3",
                "ffn1_pre": "norm_g4", "ffn1_post": "norm_g5", "ffn2_pre": "norm_g6", "ffn2_post": "norm_g7",
                "mixer1_pre": "norm_g8", "mixer1_post": "norm_g9", "ffn3_pre": "norm_g10", "ffn3_post": "norm_g11"}

        PAIR_STEPS = {}
        _h = 1
        for cn in range(4):
            PAIR_STEPS[f"mlp{cn}"] = _h
            _h += 4
        for f in range(4):
            for cn, n in enumerate(FFN_CHUNKS):
                PAIR_STEPS[f"ffn{f}_{cn}"] = _h
                _h += n // 2
        STEPS = (16, 32)

        IN_R, IN_K, IN_V, IN_LW, IN_A = (work[:, 2 * n:2 * n + 2, :] for n in range(5))
        TMP = {}
        for n, name in enumerate(("X", "kk", "b", "k", "rk", "Y")):
            TMP[name] = [work[:, 10 + 2 * n + q, :] for q in range(2)]
        for n, name in enumerate(("R", "KK", "KabT", "KakT", "RkT", "RbT", "XT", "kT", "bT", "vT")):
            TMP[name] = [area[:, 2 * n + q, :] for q in range(2)]
        TMP["v"] = [work[:, 4 + q, :] for q in range(2)]
        y_sb, bonus_sb = work[:, 22:24, :], scratch[:, 2:4, :]
        aflat = area[:].rearrange("p k t -> p (k t)")
        at0 = 20 * T
        grown = [aflat[:, at0 + 520 * q:at0 + 520 * q + 520].rearrange("p (n t) -> p n t", t=65) for q in range(2)]
        state = aflat[:, at0 + 1056:at0 + 1056 + 256].rearrange("p (b k) -> p b k", b=2)
        rhs_sb = aflat[:, at0 + 1312:at0 + 1440]
        sa_sb = aflat[:, at0 + 1440:at0 + 1568]
        duo_vec = small[:, 12:20]
        JOBS = [("kk", None, None, None), ("KabT", "b", "KK", "strict"), ("X", "KK", "b", "first"),
                ("KakT", "k", "KK", "strict")]
        late = [("RkT", "k", "R", "incl"), ("RbT", "b", "R", "incl"), ("kT", "k", None, None), ("bT", "b", None, None),
                ("vT", "v", None, None), ("bonus", None, None, None)]
        for level in range(5):
            JOBS.append(("Y", "KabT", "X", f"lev{level}"))
            JOBS.append(late.pop(0))
            if level < 4:
                JOBS.append(("X+", "XT", "Y", None))
            JOBS.append(("XT+", "Y", "XT", None))
            if level == 0:
                JOBS.append(late.pop(0))
        at_job = {}
        JOB_NEEDS = []
        for j, (name, lhs, rhs, _) in enumerate(JOBS):
            needs = [at_job[w] for w in (lhs, rhs) if w in at_job]
            if name in ("Y", "X+", "XT+"):
                needs += [at_job[w] for w in ("Y", "X", "XT") if w in at_job and w in (lhs, rhs)]
            if j >= 4:
                needs.append(j - 4)
            JOB_NEEDS.append([max(needs)] if needs else [])
            at_job[{"X+": "X", "XT+": "XT", "X": "X"}.get(name, name)] = j
            if name == "X":
                at_job["XT"] = j
        job_mm, job_out = (S["job0_mm"], S["job1_mm"]), (S["job0_out"], S["job1_out"])

        def na_q(t, h):
            return work[64 * h:64 * h + 64, t // 4, 128 * (t % 4):128 * (t % 4) + 128]

        def na_k(t, h):
            k = work[64 * h:64 * h + 64, 4 + t // 4, :].rearrange("p (r c) -> p r c", c=64)
            return [k[:, :, NA_KEY0[t % 4]:NA_KEY0[t % 4] + 32]]

        def swa_q(t, h):
            return work[64 * h:64 * h + 64, t // 4, 128 * (t % 4):128 * (t % 4) + 128]

        def swa_k(t, h):
            b = t % 4
            return [work[64 * h:64 * h + 64, 20 + t // 16, 128 * n:128 * n + 128] for n in (max(b - 1, 0), b)]

        def swa_v(t, h, part):
            b = t % 4
            n = b if part else max(b - 1, 0)
            return work[:, 16 + n // 2, 256 * (n % 2) + 128 * (t // 16) + 64 * h:256 * (n % 2) + 128 * (t // 16) + 64 * h + 64]

        block = ctx.enter_context(nc.Block())

        @block.sync
        def _(sp):
            sp.dma_start(cst[:], cst_in).then_inc(S["consts_loaded"], 16)
            sp.dma_start(vecs[:], vec_in).then_inc(S["consts_loaded"], 16)
            sp.dma_start(x[:], x_in).then_inc(S["x_loaded"], 16)
            for s in range(2):
                sp.dma_start(w_raw[:, s, :], stream[s]).then_inc(raw_loaded[s], 16)
            sp.dma_start(work[:, 12:24, :], bias_in).then_inc(S["bias_loaded"], 16)
            sp.dma_start(area[:, 24:26, :].rearrange("p k t -> p (k t)")[:, 0:768], mask_in).then_inc(S["bias_loaded"], 16)
            with sp.Fori(1, SLABS // 2) as i:
                for s in range(2):
                    sp.wait_ge(S["lo_made"], i * 2 + (s - 1))
                    sp.dma_start(w_raw[:, s, :], stream[i * 2 + s]).then_inc(raw_loaded[s], 16)

        @block.gpsimd
        def _(pool):
            def split(first, end):
                if end <= first:
                    return
                with pool.Fori(first // 2, end // 2) as i:
                    for s in range(2):
                        pool.wait_ge(S["hi_made"], i * 2 + (s + 1))
                        nc.gpsimd.tensor_tensor(w_lo[:, s, :], w_raw[:, s, :], w_hi[:, s, :].bitcast(F32),
                                                ALU.subtract).then_inc(S["lo_made"], 1)

            split(0, SLABS)

        @block.tensor
        def _(pe):
            mm = nc.tensor.matmul

            def slab_start(first, i, s):
                pe.wait_ge(S["lo_made"], i * 2 + (first + s + 1))
                if first or not isinstance(i, int):
                    pe.wait_ge(banks_free[s], i + first // 2)

            def slab(first, i, s, hi, lo, k0=0, kt=8):
                slab_start(first, i, s)
                for m in range(2):
                    for k in range(kt):
                        a = k * 256 + m * 128
                        wh, wl = w_hi[:, s, a:a + 128], w_lo[:, s, a:a + 128]
                        out = ps[:, 2 * s + m, :]
                        mm(out, wh, hi[:, k0 + k, :], start=(k == 0), stop=False)
                        mm(out, wh, lo[:, k0 + k, :], start=False, stop=False)
                        inst = mm(out, wl, hi[:, k0 + k, :], start=False, stop=(k == kt - 1))
                inst.then_inc(S["slab_mm"], 1)

            def slabs(first, count, hi, lo, kt=8):
                if first == 0:
                    for s in range(2):
                        slab(0, 0, s, hi, lo)
                with pe.Fori(1 if first == 0 else 0, count // 2) as i:
                    for s in range(2):
                        slab(first, i, s, hi, lo, kt=kt)

            def wide_slab(first, s, hi, lo, k0):
                slab_start(first, 0, s)
                for m in range(4):
                    for k in range(4):
                        a = k * 512 + m * 128
                        wh, wl = w_hi[:, s, a:a + 128], w_lo[:, s, a:a + 128]
                        out = ps[:, 4 * s + m, :]
                        mm(out, wh, hi[:, k0 + k, :], start=(k == 0), stop=False)
                        mm(out, wh, lo[:, k0 + k, :], start=False, stop=False)
                        inst = mm(out, wl, hi[:, k0 + k, :], start=False, stop=(k == 3))
                inst.then_inc(S["slab_mm"], 1)

            def norm(name):
                r = NORM[name]
                for k in range(NT):
                    pe.wait_ge(S["sq_made"], NT * r + k + 1)
                    for t in range(4):
                        inst = mm(ps[:, 4, t:t + 1], scratch[:, k % 2, 128 * t:128 * t + 128], c("mean", n=1),
                                  start=(k == 0 and t == 0), stop=(k == NT - 1), skip_group_check=True)
                    inst.then_inc(S["sum_mm"], 1)
                pe.wait_ge(S["diag_made"], r + 1)
                mm(ps[:, 5, :], c("ones"), scratch[:, 2, :], start=True, stop=True).then_inc(S["rstd_mm"], 1)

            def pre(name):
                norm(name)
                pe.wait_ge(S["ulo_made"], NT * (SPLIT_NO[name] + 1))

            def hidden(key, first, n, kt):
                slabs(first, n, act_hi, act_lo)
                pe.wait_ge(S["hid_made"], PAIR_STEPS[key] + kt // 2)
                slabs(first + n, 4, hid_hi, hid_lo, kt=kt)

            def ffn(f):
                pre(f"ffn{f}_pre")
                for cn, kt in enumerate(FFN_CHUNKS):
                    hidden(f"ffn{f}_{cn}", FIRST[f"ffn{f}_in{cn}"], kt, kt)
                norm(f"ffn{f}_post")

            def attention(a, q_of, k_of, v_of):
                g0, steps = 16 * a, STEPS[a]
                for t in range(steps + 2):
                    if t < steps:
                        g = g0 + t
                        if t:
                            pe.wait_ge(S["at_max"], g)
                        for h in range(2):
                            for part, keys in enumerate(k_of(t, h)):
                                n = 256 // len(k_of(t, h))
                                inst = mm(ps[:, 6 + h, n * part:n * part + n], q_of(t, h), keys, start=True, stop=True)
                        inst.then_inc(S["at_s"], 1)
                        if a == 0:
                            if t:
                                pe.wait_ge(S["at_vtok"], g)
                            pe.wait_ge(S["at_vblk"], g + 1)
                            for part in range(2):
                                inst = nc.tensor.transpose(ps[:, 5, 128 * part:128 * part + 128],
                                                           vb_buf[:, t % 2, 128 * part:128 * part + 128], c("ident"))
                            inst.then_inc(S["at_vt"], 1)
                    if 1 <= t <= steps:
                        g = g0 + t - 1
                        pe.wait_ge(S["at_p"], g + 1)
                        if t > 1:
                            pe.wait_ge(S["at_ptsb"], g)
                        for h in range(2):
                            for part in range(2):
                                inst = nc.tensor.transpose(ps[:, 4, 256 * h + 128 * part:256 * h + 128 * part + 128],
                                                           p_buf[:, (t - 1) % 2, h, 128 * part:128 * part + 128], c("ident"))
                        inst.then_inc(S["at_pt"], 1)
                    if t >= 2:
                        g = g0 + t - 2
                        pe.wait_ge(S["at_ptsb"], g + 1)
                        if t > 2:
                            pe.wait_ge(S["at_osb"], g)
                        elif a == 0:
                            pe.wait_ge(S["at_vtok"], g + 1)
                        for h in range(2):
                            for part in range(2):
                                v = vt_buf[:, (t - 2) % 2, part, 64 * h:64 * h + 64] if a == 0 else v_of(t - 2, h, part)
                                inst = mm(ps[64 * h:64 * h + 64, 3, 0:128], v, pt_buf[:, (t - 2) % 2, h, part, :],
                                          start=(part == 0), stop=(part == 1))
                        inst.then_inc(S["at_o"], 1)

            def heads_chunks(out, lhs, rhs):
                for n in range(NCH):
                    for h in range(2):
                        a, b = 64 * h, 64 * h + 64
                        inst = mm(out[a:b, 64 * n:64 * n + 64], lhs(a, b, n), rhs(a, b, n), start=True, stop=True)
                return inst

            def waited():
                pe.sem_inc(S["pe_waited"], 1)

            def chunk_of(tile):
                return lambda a, b, n: tile[a:b, 64 * n:64 * n + 64]

            def rwkv_duo(g):
                for q in range(2):
                    pe.wait_ge(S["kk_sq"], g * 2 + (q + 1))
                    inst = mm(ps[0:16, 0, :], c("sel", 16 * q), scratch[:, q, :], start=(q == 0), stop=(q == 1))
                inst.then_inc(S["kk_sum"], 1)
                for j, (name, lhs, rhs, _) in enumerate(JOBS):
                    for q in range(2):
                        if j == 0:
                            pe.wait_ge(S["kk_recip"], g + 1)
                        if j == 1:
                            pe.wait_ge(S["dve_prep"], g * 2 + 2)
                        for need in JOB_NEEDS[j]:
                            pe.wait_ge(job_out[q], g * len(JOBS) + (need + 1))
                        out = ps[:, 4 * q + j % 4, :]
                        waited()
                        if name == "kk":
                            inst = mm(out, spread[0:16, 128 * q:128 * q + 128], rows16, start=True, stop=True)
                        elif name == "bonus":
                            inst = mm(out, c("blk1"), TMP["rk"][q], start=True, stop=True)
                        elif rhs is None:
                            inst = heads_chunks(out, chunk_of(TMP[lhs][q]), lambda a, b, n: c("eye", p0=a, p1=b))
                        else:
                            inst = heads_chunks(out, chunk_of(TMP[lhs][q]), chunk_of(TMP[rhs][q]))
                        inst.then_inc(job_mm[q], 1)
                for n in range(NCH):
                    old = state[:, n % 2]

                    def part(bank, at, lhs, rhs, start, stop):
                        for q in range(2):
                            for h in range(2):
                                a, b = 64 * h, 64 * h + 64
                                inst = mm(ps[a:b, bank, at(q):at(q) + 64], lhs(a, b, q), rhs(a, b, q), start=start and q == 0,
                                          stop=stop, skip_group_check=True)
                        return inst

                    def ch(name):
                        return lambda a, b, q: TMP[name][q][a:b, 64 * n:64 * n + 64]

                    def st(a, b, q):
                        return old[a:b, 64 * q:64 * q + 64]

                    def at(q):
                        return 64 * q

                    if n == 0:
                        for q in range(2):
                            pe.wait_ge(job_out[q], (g + 1) * len(JOBS))
                    pe.wait_ge(S["st_out"], g * (NCH + 1) + (n + 1))
                    pe.wait_ge(S["st_out1"], g * (NCH + 1) + (n + 1))
                    waited()
                    part(0, at, ch("KK"), st, True, False)
                    part(0, at, ch("KakT"), ch("vT"), False, True).then_inc(S["rhs_mm"], 1)
                    if n >= 2:
                        pe.wait_ge(S["y_out"], g * NCH + (n - 1))
                        waited()
                    part(3 + n % 2, at, st, ch("R"), True, False)
                    part(3 + n % 2, at, ch("vT"), ch("RkT"), False, False)
                    part(2, at, lambda a, b, q: c("eye", p0=a, p1=b), st, True, False)
                    part(2, at, ch("kT"), ch("vT"), False, False)
                    pe.wait_ge(S["rhs_out"], g * NCH + (n + 1))
                    waited()
                    part(1, at, ch("XT"), lambda a, b, q: rhs_sb[a:b, 64 * q:64 * q + 64], True, True).then_inc(S["sa_mm"], 1)
                    pe.wait_ge(S["sa_out"], g * NCH + (n + 1))
                    waited()
                    part(2, at, ch("bT"), lambda a, b, q: sa_sb[a:b, 64 * q:64 * q + 64], False, True).then_inc(S["st_mm"], 1)
                    part(3 + n % 2, at, lambda a, b, q: sa_sb[a:b, 64 * q:64 * q + 64], ch("RbT"), False, True).then_inc(S["y_mm"], 1)

            pe.wait_ge(S["consts_loaded"], 32)
            pre("first")
            slabs(0, 12, act_hi, act_lo)
            pe.wait_ge(S["conv_done"], 1)
            for j in range(8):
                pe.wait_ge(S["qk_sq"], j + 1)
                mm(ps[0:16, 4, :], c("sel", 16 * j), scratch[:, j % 2, :], start=(j == 0), stop=(j == 7)).then_inc(S["qk_sum"], 1)
            pe.wait_ge(S["qk_recip"], 1)
            pe.wait_ge(S["spread_loaded"], 16)
            for j in range(8):
                if j >= 2:
                    pe.wait_ge(S["qk_done"], j - 1)
                mm(ps[:, 6 + j % 2, :], spread[0:16, 128 * j:128 * j + 128], rows16, start=True, stop=True).then_inc(S["qk_bcast"], 1)
            pe.wait_ge(S["qk_done"], 8)
            attention(0, na_q, na_k, None)
            for s in range(2):
                pe.wait_ge(S["branch_made"], 1)
                wide_slab(FIRST["attn_branch"], s, hid_hi, hid_lo, 0)
            for s in range(2):
                wide_slab(FIRST["conv_branch"], s, hid_hi, hid_lo, 4)
            slabs(FIRST["gates"], 8, act_hi, act_lo)
            pe.wait_ge(S["merged_made"], 1)
            slabs(FIRST["w_o"], 4, act_hi, act_lo)
            pre("mlp")
            for cn in range(4):
                hidden(f"mlp{cn}", FIRST[f"mlp_in{cn}"], 4, 8)

            ffn(0)
            norm("mixer0_pre")
            n = FIRST["lora"]
            pe.wait_ge(S["lo_made"], n + 1)
            for j, (col, hi, lo) in enumerate(((0, act_hi, act_lo), (0, hid_hi, hid_lo), (128, act_hi, act_lo))):
                pe.wait_ge(S["mix_lo"], NT * (j + 1))
                for k in range(NT):
                    a = k * 256 + col
                    wh, wl = w_hi[:, 0, a:a + 128], w_lo[:, 0, a:a + 128]
                    mm(ps[:, j, :], wh, hi[:, k, :], start=(k == 0), stop=False)
                    mm(ps[:, j, :], wh, lo[:, k, :], start=False, stop=False)
                    inst = mm(ps[:, j, :], wl, hi[:, k, :], start=False, stop=(k == NT - 1))
                inst.then_inc(S["lora_mm"] if j < 2 else S["slab_mm"], 1)
            pe.wait_ge(S["lora_lo"], 1)
            pe.wait_ge(S["lo_made"], n + 2)
            for j in range(24):
                kind, m = divmod(j, NT)
                if j >= 4:
                    pe.wait_ge(S["lora_out"], j - 3)
                a = 128 * m + (1024 if kind == 2 else 0)
                wh, wl = w_hi[:, 1, a:a + 128], w_lo[:, 1, a:a + 128]
                out = ps[:, j % 4, :]
                mm(out, wh, hid_hi[:, kind, :], start=True, stop=False)
                mm(out, wh, hid_lo[:, kind, :], start=False, stop=False)
                inst = mm(out, wl, hid_hi[:, kind, :], start=False, stop=True)
                inst.then_inc(S["lora_mm"] if j < 23 else S["slab_mm"], 1)
            pe.wait_ge(S["banks1_free"], FIRST["r"] // 2)
            pe.wait_ge(S["mix_lo"], NT * 4)
            slabs(FIRST["r"], 4, act_hi, act_lo)
            pe.wait_ge(S["mix_lo"], NT * 5)
            slabs(FIRST["k"], 4, hid_hi, hid_lo)
            pe.wait_ge(S["mix_lo"], NT * 6)
            slabs(FIRST["v"], 4, act_hi, act_lo)
            pe.wait_ge(banks_free[0], FIRST["rwkv_o"] // 2)
            pe.wait_ge(banks_free[1], FIRST["rwkv_o"] // 2)
            with pe.Fori(0, 4) as g:
                rwkv_duo(g)
            for m in range(NT):
                pe.wait_ge(S["gn_loaded"], 48)
                if m >= 2:
                    pe.wait_ge(S["gn_d"], m - 1)
                mm(ps[:, 4 + m % 2, :], c("blk64"), work[:, m, :], start=True, stop=True).then_inc(S["gn_mean"], 1)
                if m:
                    pe.wait_ge(S["gn_sq"], m)
                    mm(ps[0:16, 6, :], c("sel", 16 * (m - 1)), scratch[:, (m - 1) % 2, :], start=(m == 1), stop=False).then_inc(S["gn_sum"], 1)
            pe.wait_ge(S["gn_sq"], NT)
            mm(ps[0:16, 6, :], c("sel", 16 * 7), scratch[:, 1, :], start=False, stop=True).then_inc(S["gn_sum"], 1)
            pe.wait_ge(S["gn_recip"], 1)
            for m in range(NT):
                if m >= 2:
                    pe.wait_ge(S["gn_scaled"], m - 1)
                mm(ps[:, 4 + m % 2, :], spread[0:16, 128 * m:128 * m + 128], rows16, start=True, stop=True).then_inc(S["gn_bcast"], 1)
            pe.wait_ge(S["gn_lo"], NT)
            slabs(FIRST["rwkv_o"], 4, act_hi, act_lo)
            norm("mixer0_post")
            ffn(1)
            pre("kv")
            slabs(FIRST["kv"], 2, act_hi, act_lo)
            ffn(2)
            pre("mixer1_pre")
            slabs(FIRST["q2"], 4, act_hi, act_lo)
            for s in range(2):
                pe.wait_ge(banks_free[s], FIRST["o2"] // 2)
            for b in range(4):
                for a in range(2):
                    inst = nc.tensor.transpose(ps[:, 4 + b // 2, 256 * (b % 2) + 128 * a:256 * (b % 2) + 128 * a + 128],
                                               work[:, 22 + a, 128 * b:128 * b + 128], c("ident"))
            inst.then_inc(S["vtok_mm"], 1)
            pe.wait_ge(S["vtok_out"], 1)
            attention(1, swa_q, swa_k, swa_v)
            pe.wait_ge(S["branch_made"], 2)
            slabs(FIRST["o2"], 4, act_hi, act_lo)
            norm("mixer1_post")
            ffn(3)

        @block.scalar
        def _(act):
            af = nc.scalar.activation

            def hi_next(first, i, s):
                act.wait_ge(raw_loaded[1 - s], (i + (first // 2 + s + 1 if s else first // 2 + 1)) * 16)
                if first + s or not isinstance(i, int):
                    act.wait_ge(S["slab_mm"], i * 2 + (first + s))
                nc.scalar.copy(w_hi[:, 1 - s, :], w_raw[:, 1 - s, :]).then_inc(S["hi_made"], 1)

            def slabs(first, count, body=None):
                def one(i, s, more=True):
                    if more:
                        hi_next(first, i, s)
                    if body is not None:
                        act.wait_ge(S["slab_mm"], i * 2 + (first + s + 1))
                        body(i, s)
                begin = first == 0
                end = first + count == SLABS
                if begin:
                    one(0, 0)
                    one(0, 1)
                if count // 2 - end:
                    with act.Fori(begin, count // 2 - end) as i:
                        one(i, 0)
                        one(i, 1)
                if end:
                    one(count // 2 - 1, 0)
                    one(count // 2 - 1, 1, more=False)

            def evacuated(end):
                for s in range(2):
                    act.wait_ge(banks_free[s], end // 2)

            def norm(name, src):
                r = NORM[name]
                posts = sum(n.endswith("post") for n in NORMS[:r])
                if src is x_of and posts:
                    act.wait_ge(S["post_done"], posts)
                for k in range(NT):
                    if k >= 2 or r:
                        act.wait_ge(S["sum_mm"], NT * r + k - 1 if k >= 2 else NT * r)
                    af(scratch[:, k % 2, :], src(k), ACT.Square).then_inc(S["sq_made"], 1)
                act.wait_ge(S["mean_made"], r + 1)
                af(small[:, 4:8], small[:, 0:4], ACT.Sqrt).then_inc(S["root_made"], 1)

            def pre(name, src):
                norm(name, src)
                for k in range(NT):
                    act.wait_ge(S["u_made"], NT * PRE_NO[name] + k + 1)
                    nc.scalar.copy(act_hi[:, k, :], work[:, k, :]).then_inc(S["uhi_made"], 1)

            def x_of(k):
                return x[:, k, :]

            def y_of(k):
                return ybuf[:, k, 0:T]

            def ffn(f):
                pre(f"ffn{f}_pre", x_of)
                for cn, n in enumerate(FFN_CHUNKS):
                    def gate(i, s):
                        if s == 0:
                            act.wait_ge(S["hid_made"], i + PAIR_STEPS[f"ffn{f}_{cn}"])
                            af(work[:, 8, :], ps[:, 0, :], ACT.Silu)
                            af(work[:, 9, :], ps[:, 1, :], ACT.Silu).then_inc(banks_free[0], 1)
                    first = FIRST[f"ffn{f}_in{cn}"]
                    with act.Fori(0, n // 2) as i:
                        hi_next(first, i, 0)
                        act.wait_ge(S["slab_mm"], i * 2 + (first + 1))
                        gate(i, 0)
                        hi_next(first, i, 1)
                    slabs(first + n, 4)
                evacuated(FIRST[f"ffn{f}_out2"] + 4)
                norm(f"ffn{f}_post", y_of)

            def attention(a, exp_out):
                g0, steps = 16 * a, STEPS[a]
                for t in range(steps + 2):
                    if t < steps:
                        g = g0 + t
                        if a == 0:
                            tile, j = divmod(t, 4)
                            if t >= 2:
                                act.wait_ge(S["at_vt"], g - 1)
                            v = work[:, 8 + tile, :].rearrange("p (r c) -> p r c", c=64)[:, :, NA_KEY0[j]:NA_KEY0[j] + 32]
                            nc.scalar.copy(vb_buf[:, t % 2, :].rearrange("p (r c) -> p r c", c=32), v).then_inc(S["at_vblk"], 1)
                        act.wait_ge(S["at_max"], g + 1)
                        for h in range(2):
                            inst = af(p_buf[:, t % 2, h, :], p_buf[:, t % 2, h, :], ACT.Exp,
                                      bias=small[:, 12 + 2 * (t % 2) + h:13 + 2 * (t % 2) + h],
                                      accum_out=small[:, 16 + 2 * (t % 2) + h:17 + 2 * (t % 2) + h])
                        if a == 1:
                            for h in range(2):
                                inst = af(small[:, 24 + 2 * (t % 2) + h:25 + 2 * (t % 2) + h],
                                          sinks[:, 2 * (t // 4) + h:2 * (t // 4) + h + 1], ACT.Exp,
                                          bias=small[:, 12 + 2 * (t % 2) + h:13 + 2 * (t % 2) + h])
                        inst.then_inc(S["at_exp"], 1)
                        if a == 0:
                            act.wait_ge(S["at_vt"], g + 1)
                            if t >= 2:
                                act.wait_ge(S["at_o"], g - 1)
                            nc.scalar.copy(vt_buf[:, t % 2, :, :], ps[:, 5, 0:256].rearrange("p (a k) -> p a k", a=2)).then_inc(S["at_vtok"], 1)
                    if 1 <= t <= steps:
                        g = g0 + t - 1
                        act.wait_ge(S["at_pt"], g + 1)
                        if t >= 3:
                            act.wait_ge(S["at_o"], g - 1)
                        nc.scalar.copy(pt_buf[:, (t - 1) % 2, :, :, :],
                                       ps[:, 4, :].rearrange("p (h a k) -> p h a k", h=2, a=2)).then_inc(S["at_ptsb"], 1)
                    if t >= 2:
                        g = g0 + t - 2
                        act.wait_ge(S["at_o"], g + 1)
                        tile, j = divmod(t - 2, 4)
                        nc.scalar.copy(work[:, tile, 128 * j:128 * j + 128], ps[:, 3, 0:128]).then_inc(S["at_osb"], 1)

            def mix(j, wait):
                dst = hid_hi if j in (1, 4) else act_hi
                for k in range(NT + 1):
                    if k < NT:
                        e = NT * j + k
                        if e >= 2:
                            act.wait_ge(S["mix_made"], e - 1)
                        af(scratch[:, k % 2, :], u_now(k), ACT.Copy, scale=omu[:, NT * MIX[j] + k:NT * MIX[j] + k + 1]).then_inc(S["t_made"], 1)
                    if k == 0:
                        wait()
                    if k:
                        e = NT * j + k - 1
                        act.wait_ge(S["mix_made"], e + 1)
                        nc.scalar.copy(dst[:, k - 1, :], scratch[:, 2 + (k - 1) % 2, :]).then_inc(S["mix_hi"], 1)

            def rwkv_act():
                norm("mixer0_pre", x_of)
                n0 = FIRST["lora"]
                hi_next(n0, 0, 0)
                act.wait_ge(S["u_made"], NT * (PRE_NO["mixer0_pre"] + 1))
                mix(0, lambda: None)
                mix(1, lambda: None)
                mix(2, lambda: act.wait_ge(S["lora_mm"], 1))
                act.wait_ge(S["lora_mm"], 1)
                af(work[0:64, 0, :], ps[0:64, 0, :], ACT.Tanh)
                act.wait_ge(S["lora_mm"], 2)
                nc.scalar.copy(work[64:128, 1, :], ps[64:128, 1, :])
                act.wait_ge(S["slab_mm"], n0 + 1)
                af(work[:, 2, :], ps[:, 2, :], ACT.Sigmoid).then_inc(banks_free[0], 1)
                hi_next(n0, 0, 1)
                act.wait_ge(S["lora_lo"], 1)
                for j in range(24):
                    kind, m = divmod(j, NT)
                    if j < 23:
                        act.wait_ge(S["lora_mm"], j + 3)
                    else:
                        act.wait_ge(S["slab_mm"], n0 + 2)
                    if kind < 2:
                        inst = af(work[:, j, :], ps[:, j % 4, :], ACT.Sigmoid, bias=vec(("w0", "a0")[kind], m))
                    else:
                        inst = nc.scalar.copy(work[:, j, :], ps[:, j % 4, :])
                    inst.then_inc(S["lora_out"] if j < 23 else banks_free[1], 1)
                act.wait_ge(banks_free[1], n0 // 2 + 1)
                for kind, row in enumerate((LW_, A_, G_)):
                    act.dma_start(spill[row], work[:, 8 * kind:8 * kind + 8, :]).then_inc(S["spilled"], 16)
                mix(3, lambda: act.wait_ge(S["slab_mm"], n0 + 1))
                mix(4, lambda: act.wait_ge(S["slab_mm"], n0 + 2))
                act.wait_ge(S["spilled"], 48)
                for j, (name, row) in enumerate((("r", R_), ("k", K_), ("v", V_))):
                    def keep(i, s):
                        nc.scalar.copy(pairs(work)[:, i * 2 + (4 * j + s)], banks(2 * s)).then_inc(banks_free[s], 1)
                    if j == 1:
                        mix(5, lambda: act.wait_ge(S["slab_mm"], FIRST["k"]))
                    slabs(FIRST[name], 4, keep)
                    evacuated(FIRST[name] + 4)
                    act.dma_start(spill[row], work[:, 8 * j:8 * j + 8, :]).then_inc(S["spilled"], 16)
                act.dma_start(spread[0:16, :], spread_in).then_inc(S["spread_loaded"], 16)
                act.dma_start(restart, restart_in).then_inc(S["spread_loaded"], 16)
                act.wait_ge(S["spilled"], 96)
                with act.Fori(0, 4) as g:
                    duo_act(g)
                act.wait_ge(S["spilled"], 96 + 32 * 4)
                for n, row in enumerate((Y_, BON_, G_)):
                    act.dma_start(work[:, 8 * n:8 * n + 8, :], spill[row]).then_inc(S["gn_loaded"], 16)
                for m in range(NT):
                    act.wait_ge(S["gn_d"], m + 1)
                    if m >= 2:
                        act.wait_ge(S["gn_sum"], m - 1)
                    af(scratch[:, m % 2, :], work[:, m, :], ACT.Square).then_inc(S["gn_sq"], 1)
                act.wait_ge(S["gn_var"], 1)
                af(rows16b, rows16, ACT.Sqrt).then_inc(S["gn_root"], 1)
                for m in range(NT + 1):
                    if m < NT:
                        act.wait_ge(S["gn_scaled"], m + 1)
                        af(work[:, m, :], work[:, m, :], ACT.Identity, scale=vec("gn_g", m), bias=vec("gn_b", m)).then_inc(S["gn_affine"], 1)
                    if m:
                        act.wait_ge(S["gn_gated"], m)
                        nc.scalar.copy(act_hi[:, m - 1, :], work[:, m - 1, :]).then_inc(S["gn_hi"], 1)
                slabs(FIRST["rwkv_o"], 4)
                evacuated(FIRST["rwkv_o"] + 4)
                norm("mixer0_post", y_of)

            def duo_act(g):
                act.wait_ge(S["dve_free"], g + 1)
                for tile, row in ((IN_LW, LW_), (IN_A, A_), (IN_K, K_), (IN_R, R_), (IN_V, V_)):
                    act.dma_start(tile, pairs(spill[row])[:, g]).then_inc(S["duo_loaded"], 16)
                act.wait_ge(S["duo_vec"], g + 1)
                act.wait_ge(S["duo_loaded"], g * 80 + 80)
                for q in range(2):
                    nc.scalar.activation(scratch[:, q, :], IN_K[:, q, :], ACT.Square, scale=duo_vec[:, q:q + 1]).then_inc(S["kk_sq"], 1)
                for q in range(2):
                    af(TMP["kk"][q], IN_K[:, q, :], ACT.Copy, scale=duo_vec[:, q:q + 1])
                for q in range(2):
                    inst = af(TMP["k"][q], IN_A[:, q, :], ACT.Identity, scale=duo_vec[:, 2 + q:3 + q], bias=duo_vec[:, 6 + q:7 + q])
                inst.then_inc(S["act_prep"], 1)
                act.wait_ge(S["kk_max"], g + 1)
                af(rows16b_duo, rows16, ACT.Sqrt).then_inc(S["kk_root"], 1)
                act.wait_ge(S["dve_prep"], g * 2 + 1)
                for q in range(2):
                    run_sum = TMP["Y"][q].rearrange("p (n t) -> p n t", t=CH)
                    af(grown[q][:, :, 1:65], run_sum, ACT.Exp, scale=-DECAY)
                    inst = af(TMP["X"][q], TMP["Y"][q], ACT.Exp, scale=DECAY)
                inst.then_inc(S["act_prep"], 1)
                for n in range(NCH):
                    act.wait_ge(S["sa_mm"], g * NCH + (n + 1))
                    af(sa_sb, ps[:, 1, 0:128], ACT.Copy, scale=-1.0).then_inc(S["sa_out"], 1)
                    act.wait_ge(S["st_mm"], g * NCH + (n + 1))
                    af(state[:, (n + 1) % 2, 64:128], ps[:, 2, 64:128], ACT.Copy, scale=grown[1][:, n, 64:65]).then_inc(S["st_out1"], 1)
                    act.wait_ge(S["y_mm"], g * NCH + (n + 1))
                    nc.scalar.copy(y_sb[:, :, 64 * n:64 * n + 64], ps[:, 3 + n % 2, 0:128].rearrange("p (q t) -> p q t", q=2)).then_inc(S["y_out"], 1)
                act.wait_ge(S["y_out"], (g + 1) * NCH)
                act.dma_start(pairs(spill[Y_])[:, g], y_sb).then_inc(S["spilled"], 16)
                act.dma_start(pairs(spill[BON_])[:, g], bonus_sb).then_inc(S["spilled"], 16)

            act.wait_ge(S["consts_loaded"], 32)
            act.wait_ge(raw_loaded[0], 16)
            nc.scalar.copy(w_hi[:, 0, :], w_raw[:, 0, :]).then_inc(S["hi_made"], 1)
            act.wait_ge(S["x_loaded"], 16)
            pre("first", x_of)

            def qkv(i, s):
                nc.scalar.copy(pairs(work)[:, i * 2 + s], banks(2 * s)).then_inc(banks_free[s], 1)
            slabs(0, 6, qkv)

            def cb(i, s):
                nc.scalar.copy(pairs(ybuf)[:, i * 2 + s], banks(2 * s)).then_inc(banks_free[s], 1)
            slabs(6, 2, cb)

            def cc(i, s):
                nc.scalar.copy(ybuf[:, 4 + 2 * s:6 + 2 * s, 1:T + 1], banks(2 * s)).then_inc(banks_free[s], 1)
            slabs(8, 2, cc)
            slabs(10, 2)
            for j in range(8):
                if j >= 2:
                    act.wait_ge(S["qk_sum"], j - 1)
                else:
                    act.wait_ge(S["rstd_mm"], 1)
                af(scratch[:, j % 2, :], work[:, j, :], ACT.Square).then_inc(S["qk_sq"], 1)
            act.wait_ge(S["qk_mean"], 1)
            af(rows16b, rows16, ACT.Sqrt).then_inc(S["qk_root"], 1)
            act.wait_ge(S["conv_done"], 1)
            act.dma_start(spread[0:16, :], spread_in).then_inc(S["spread_loaded"], 16)
            attention(0, None)
            act.wait_ge(S["branch_made"], 1)

            def branch(i, s, dst):
                nc.scalar.copy(dst[:, 4 * s:4 * s + 4], ps[:, 4 * s:4 * s + 4, :]).then_inc(banks_free[s], 1)
            slabs(FIRST["attn_branch"], 2, lambda i, s: branch(i, s, ybuf[:, :, 0:T]))
            slabs(FIRST["conv_branch"], 2, lambda i, s: branch(i, s, work))

            def gates(i, s):
                act.wait_ge(S["gate_made2"], i * 2 + (s + 1))
                af(scratch[:, 0:2, :], banks(2 * s), ACT.Sigmoid).then_inc(banks_free[s], 1)
            slabs(FIRST["gates"], 8, gates)
            for k in range(NT):
                act.wait_ge(S["tile_made"], k + 1)
                nc.scalar.copy(act_hi[:, k, :], ybuf[:, k, 0:T]).then_inc(S["merged_hi"], 1)
            slabs(FIRST["w_o"], 4)
            evacuated(FIRST["w_o"] + 4)
            pre("mlp", x_of)
            for cn in range(4):
                def relu(i, s):
                    act.wait_ge(S["hid_made"], i * 2 + (PAIR_STEPS[f"mlp{cn}"] + s))
                    af(work[:, 8:10, :], banks(2 * s), ACT.Relu).then_inc(S["gate_made"], 1)
                slabs(FIRST[f"mlp_in{cn}"], 4, relu)
                slabs(FIRST[f"mlp_out{cn}"], 4)
            evacuated(FIRST["mlp_out3"] + 4)
            ffn(0)
            rwkv_act()
            ffn(1)
            pre("kv", x_of)

            def kv(i, s):
                for m in range(2):
                    inst = af(work[:, 20 + 2 * s + m, :], ps[:, 2 * s + m, :], ACT.Identity, bias=vec("b_kv", 2 * s + m))
                inst.then_inc(banks_free[s], 1)
            slabs(FIRST["kv"], 2, kv)
            ffn(2)
            pre("mixer1_pre", x_of)

            act.dma_start(scratch[:, 3, :].rearrange("p (b k) -> p b k", b=2), swa_in).then_inc(S["swa_loaded"], 16)
            slabs(FIRST["q2"], 4)
            act.wait_ge(S["vtok_mm"], 1)
            nc.scalar.copy(work[:, 16:18, :], ps[:, 4:6, :]).then_inc(S["vtok_out"], 1)
            attention(1, None)
            for k in range(NT):
                act.wait_ge(S["at_osb"], STEPS[0] + STEPS[1])
                nc.scalar.copy(act_hi[:, k, :], work[:, k, :]).then_inc(S["merged_hi"], 1)
            slabs(FIRST["o2"], 4)
            evacuated(FIRST["o2"] + 4)
            norm("mixer1_post", y_of)
            ffn(3)
            act.wait_ge(S["post_done"], 6)
            act.dma_start(x_out, x[:]).then_inc(S["out_stored"], 16)
            act.wait_ge(S["out_stored"], 16)

        @block.vector
        def _(dve):
            tt = nc.vector.tensor_tensor
            stt = nc.vector.scalar_tensor_tensor
            ts = nc.vector.tensor_scalar
            copy = nc.vector.tensor_copy

            def norm(name):
                r = NORM[name]
                dve.wait_ge(S["sum_mm"], NT * (r + 1))
                ts(small[:, 0:4], ps[:, 4, 0:4], EPS, None, ALU.add).then_inc(S["mean_made"], 1)
                dve.wait_ge(S["root_made"], r + 1)
                nc.vector.reciprocal(small[:, 8:12], small[:, 4:8])
                dve.drain()
                for t in range(4):
                    inst = ts(scratch[:, 2, 128 * t:128 * t + 128], c("ident"), small[:, 8 + t:9 + t], None, ALU.mult)
                inst.then_inc(S["diag_made"], 1)
                dve.wait_ge(S["rstd_mm"], r + 1)

            def pre(name, src, dst=None, split=True):
                norm(name)
                for k in range(NT):
                    stt(out=work[:, k, :] if dst is None else dst(k), in0=src(k), scalar=vec(GAIN[name], k), in1=ps[:, 5, :],
                        op0=ALU.mult, op1=ALU.mult).then_inc(S["u_made"], 1)
                if split:
                    for k in range(NT):
                        dve.wait_ge(S["uhi_made"], NT * SPLIT_NO[name] + k + 1)
                        tt(act_lo[:, k, :], work[:, k, :], act_hi[:, k, :].bitcast(F32), ALU.subtract).then_inc(S["ulo_made"], 1)

            def post(name, factor):
                norm(name)
                for k in range(NT):
                    stt(out=work[:, k, :], in0=ybuf[:, k, 0:T], scalar=vec(GAIN[name], k), in1=ps[:, 5, :],
                        op0=ALU.mult, op1=ALU.mult)
                dve.drain()
                for k in range(NT):
                    inst = stt(out=x[:, k, :], in0=work[:, k, :], scalar=factor, in1=x[:, k, :], op0=ALU.mult, op1=ALU.add)
                inst.then_inc(S["post_done"], 1)

            def x_of(k):
                return x[:, k, :]

            def slabs(first, count, body):
                with dve.Fori(0, count // 2) as i:
                    for s in range(2):
                        dve.wait_ge(S["slab_mm"], i * 2 + (first + s + 1))
                        body(i, s)

            def hidden_pair(dst, s):
                tt(work[:, 10:12, :], banks(2 * s), work[:, 8:10, :], ALU.mult)
                tt(pairs(hid_hi)[:, dst], banks(2 * s), work[:, 8:10, :], ALU.mult).then_inc(banks_free[s], 1)
                dve.drain()
                tt(pairs(hid_lo)[:, dst], work[:, 10:12, :], pairs(hid_hi)[:, dst].bitcast(F32), ALU.subtract).then_inc(S["hid_made"], 1)

            def add_to(acc):
                def body(i, s):
                    a = pairs(acc)[:, i * 2 + s]
                    tt(a, banks(2 * s), a, ALU.add).then_inc(banks_free[s], 1)
                return body

            def ffn(f):
                pre(f"ffn{f}_pre", x_of)
                for cn, n in enumerate(FFN_CHUNKS):
                    first = FIRST[f"ffn{f}_in{cn}"]
                    with dve.Fori(0, n // 2) as i:
                        dve.wait_ge(S["slab_mm"], i * 2 + (first + 2))
                        dve.wait_ge(banks_free[0], i + (first // 2 + 1))
                        hidden_pair(i, 1)
                    first += n
                    if cn == 0:
                        slabs(first, 4, lambda i, s: copy(pairs(ybuf)[:, i * 2 + s], banks(2 * s)).then_inc(banks_free[s], 1))
                    else:
                        slabs(first, 4, add_to(ybuf))
                post(f"ffn{f}_post", 0.5)

            def attention(a, heads_bias):
                g0, steps = 16 * a, STEPS[a]
                for t in range(steps + 1):
                    if t < steps:
                        g, b = g0 + t, t % 2
                        dve.wait_ge(S["at_s"], g + 1)
                        if t >= 2:
                            dve.wait_ge(S["at_pt"], g - 1)
                        tt(p_buf[:, b, :, :], ps[:, 6:8, 0:256], heads_bias(t), ALU.add)
                        dve.drain()
                        nc.vector.tensor_reduce(small[:, 20 + 2 * b:22 + 2 * b], p_buf[:, b, :, :], AX_X, ALU.max)
                        dve.drain()
                        if a == 1:
                            tt(small[:, 20 + 2 * b:22 + 2 * b], small[:, 20 + 2 * b:22 + 2 * b], sinks[:, 2 * (t // 4):2 * (t // 4) + 2], ALU.max)
                            dve.drain()
                        ts(small[:, 12 + 2 * b:14 + 2 * b], small[:, 20 + 2 * b:22 + 2 * b], -1.0, None, ALU.mult).then_inc(S["at_max"], 1)
                    if t >= 1:
                        g, b = g0 + t - 1, (t - 1) % 2
                        dve.wait_ge(S["at_exp"], g + 1)
                        if a == 1:
                            tt(small[:, 16 + 2 * b:18 + 2 * b], small[:, 16 + 2 * b:18 + 2 * b], small[:, 24 + 2 * b:26 + 2 * b], ALU.add)
                            dve.drain()
                        nc.vector.reciprocal(small[:, 28 + 2 * b:30 + 2 * b], small[:, 16 + 2 * b:18 + 2 * b])
                        dve.drain()
                        for h in range(2):
                            inst = ts(p_buf[:, b, h, :], p_buf[:, b, h, :], small[:, 28 + 2 * b + h:29 + 2 * b + h], None, ALU.mult)
                        inst.then_inc(S["at_p"], 1)

            def rwkv_dve():
                dve.drain()
                ts(omu[:], vecs[:, VEC["mu0"]:VEC["mu0"] + 48], -1.0, 1.0, ALU.mult, ALU.add)
                ts(oma[:], vecs[:, VEC["k_a"]:VEC["k_a"] + 8], -1.0, 1.0, ALU.mult, ALU.add)
                nc.vector.memset(ybuf[:, :, 0:1], 0.0)
                nc.vector.memset(work[64:128, 0, :], 0.0)
                nc.vector.memset(work[0:64, 1, :], 0.0)
                dve.drain()
                pre("mixer0_pre", x_of, dst=u_now, split=False)
                dve.drain()
                for j in range(6):
                    hi, lo = (hid_hi, hid_lo) if j in (1, 4) else (act_hi, act_lo)
                    if j == 3:
                        dve.wait_ge(banks_free[0], FIRST["lora"] // 2 + 1)
                        copy(hid_hi[:, 0:3, :], work[:, 0:3, :])
                        dve.drain()
                        tt(hid_lo[:, 0:3, :], work[:, 0:3, :], hid_hi[:, 0:3, :].bitcast(F32), ALU.subtract).then_inc(S["lora_lo"], 1)
                    for k in range(NT + 1):
                        e = NT * j + k
                        if k < NT:
                            dve.wait_ge(S["t_made"], e + 1)
                            if e >= 2:
                                dve.wait_ge(S["mix_hi"], e - 1)
                                dve.wait_ge(S["mix_lo"], e - 1)
                            stt(out=scratch[:, 2 + k % 2, :], in0=ybuf[:, k, 0:T], scalar=vec(f"mu{MIX[j]}", k), in1=scratch[:, k % 2, :],
                                op0=ALU.mult, op1=ALU.add).then_inc(S["mix_made"], 1)
                        if k:
                            dve.wait_ge(S["mix_hi"], e)
                            dve.wait_ge(S["mix_made"], e)
                            tt(lo[:, k - 1, :], scratch[:, 2 + (k - 1) % 2, :], hi[:, k - 1, :].bitcast(F32), ALU.subtract).then_inc(S["mix_lo"], 1)
                for s in range(2):
                    dve.wait_ge(banks_free[s], FIRST["rwkv_o"] // 2)
                for q in range(2):
                    nc.vector.memset(grown[q][:, :, 0:1], 1.0)
                dve.wait_ge(S["spread_loaded"], 48)
                dve.wait_ge(S["spilled"], 96)
                nc.vector.memset(small[:, 30:31], 0.0).then_inc(S["dve_free"], 1)
                with dve.Fori(0, 4) as g:
                    duo_dve(g)
                for m in range(NT):
                    dve.wait_ge(S["gn_mean"], m + 1)
                    tt(work[:, m, :], work[:, m, :], ps[:, 4 + m % 2, :], ALU.subtract).then_inc(S["gn_d"], 1)
                dve.wait_ge(S["gn_sum"], NT)
                ts(rows16, ps[0:16, 6, :], 1 / 64, GN_EPS, ALU.mult, ALU.add).then_inc(S["gn_var"], 1)
                dve.wait_ge(S["gn_root"], 1)
                nc.vector.reciprocal(rows16, rows16b).then_inc(S["gn_recip"], 1)
                for m in range(NT + 1):
                    if m < NT:
                        dve.wait_ge(S["gn_bcast"], m + 1)
                        tt(work[:, m, :], work[:, m, :], ps[:, 4 + m % 2, :], ALU.mult).then_inc(S["gn_scaled"], 1)
                    if m:
                        w = work[:, m - 1, :]
                        dve.wait_ge(S["gn_affine"], m)
                        tt(w, w, work[:, 8 + m - 1, :], ALU.add)
                        dve.drain()
                        tt(w, w, work[:, 16 + m - 1, :], ALU.mult).then_inc(S["gn_gated"], 1)
                        dve.wait_ge(S["gn_hi"], m)
                        tt(act_lo[:, m - 1, :], w, act_hi[:, m - 1, :].bitcast(F32), ALU.subtract).then_inc(S["gn_lo"], 1)
                slabs(FIRST["rwkv_o"], 4, lambda i, s: copy(pairs(ybuf)[:, i * 2 + s], banks(2 * s)).then_inc(banks_free[s], 1))
                post("mixer0_post", 1.0)

            def chunks(tile):
                return tile.rearrange("p (n t) -> p n t", t=CH)

            def mask(name):
                return c(name).unsqueeze(1).broadcast_to([P, NCH, 64])

            def duo_dve(g):
                for n, tab in enumerate((vecs[:, VEC["k_k"]:VEC["k_k"] + 8], vecs[:, VEC["k_a"]:VEC["k_a"] + 8],
                                         vecs[:, VEC["r_k"]:VEC["r_k"] + 8], oma[:])):
                    inst = copy(duo_vec[:, 2 * n:2 * n + 2], tab.rearrange("p (a b) -> p a b", b=2)[:, g])
                inst.then_inc(S["duo_vec"], 1)
                dve.wait_ge(S["duo_loaded"], g * 80 + 80)
                for q in range(2):
                    inst = nc.vector.tensor_tensor_scan(TMP["Y"][q], restart, IN_LW[:, q, :], 0.0, ALU.mult, ALU.add)
                inst.then_inc(S["dve_prep"], 1)
                dve.wait_ge(S["kk_sum"], g + 1)
                ts(rows16, ps[0:16, 0, :], 1e-24, None, ALU.max).then_inc(S["kk_max"], 1)
                dve.wait_ge(S["act_prep"], g * 2 + 1)
                kb = work[:, 16:18, :]
                tt(kb, IN_K, kb, ALU.mult)
                dve.drain()
                for q in range(2):
                    stt(out=TMP["rk"][q], in0=IN_R[:, q, :], scalar=duo_vec[:, 4 + q:5 + q], in1=TMP["k"][q], op0=ALU.mult, op1=ALU.mult)
                dve.wait_ge(S["kk_root"], g + 1)
                nc.vector.reciprocal(rows16, rows16b_duo).then_inc(S["kk_recip"], 1)
                dve.drain()
                dve.wait_ge(S["act_prep"], g * 2 + 2)
                for q in range(2):
                    tt(chunks(TMP["R"][q]), chunks(IN_R[:, q, :]), grown[q][:, :, 1:65], ALU.mult)
                tt(kb, kb, work[:, 10:12, :], ALU.mult)
                for q in range(2):
                    dve.wait_ge(job_mm[q], g * len(JOBS) + 1)
                    tt(TMP["kk"][q], TMP["kk"][q], ps[:, 4 * q, :], ALU.mult).then_inc(job_out[q], 1)
                dve.drain()
                tt(work[:, 14:16, :], work[:, 12:14, :], IN_A, ALU.mult)
                for q in range(2):
                    tt(chunks(TMP["KK"][q]), chunks(TMP["kk"][q]), grown[q][:, :, 0:64], ALU.mult)
                dve.drain()
                tt(work[:, 14:16, :], work[:, 14:16, :], work[:, 10:12, :], ALU.mult).then_inc(S["dve_prep"], 1)
                dve.wait_ge(S["spilled"], g * 32 + 96)
                for j, (name, _, _, m) in enumerate(JOBS):
                    if j == 0:
                        continue
                    for q in range(2):
                        dve.wait_ge(job_mm[q], g * len(JOBS) + (j + 1))
                        p = ps[:, 4 * q + j % 4, :]
                        if name == "KabT":
                            tt(chunks(TMP["XT"][q]), chunks(p), mask("firstT"), ALU.mult)
                            inst = tt(chunks(TMP[name][q]), chunks(p), mask(m), ALU.mult)
                        elif name == "X":
                            tt(chunks(TMP["X"][q]), chunks(p), mask(m), ALU.mult)
                            dve.drain()
                            tt(chunks(TMP["X"][q]), chunks(TMP["X"][q]), mask("eye"), ALU.add)
                            inst = tt(chunks(TMP["XT"][q]), chunks(TMP["XT"][q]), mask("eye"), ALU.add)
                        elif name in ("X+", "XT+"):
                            dst = TMP[name[:-1]][q]
                            inst = tt(dst, p, dst, ALU.add)
                        elif name == "bonus":
                            inst = tt(bonus_sb[:, q, :], p, IN_V[:, q, :], ALU.mult)
                        elif m is None:
                            inst = copy(TMP[name][q], p)
                        else:
                            inst = tt(chunks(TMP[name][q]), chunks(p), mask(m), ALU.mult)
                        inst.then_inc(job_out[q], 1)
                nc.vector.memset(state[:, 0, 0:64], 0.0).then_inc(S["st_out"], 1)
                nc.vector.memset(state[:, 0, 64:128], 0.0).then_inc(S["st_out1"], 1)
                for n in range(NCH):
                    dve.wait_ge(S["rhs_mm"], g * NCH + (n + 1))
                    copy(rhs_sb, ps[:, 0, 0:128]).then_inc(S["rhs_out"], 1)
                    dve.wait_ge(S["st_mm"], g * NCH + (n + 1))
                    dve.wait_ge(S["st_out1"], g * (NCH + 1) + (n + 2))
                    ts(state[:, (n + 1) % 2, 0:64], ps[:, 2, 0:64], grown[0][:, n, 64:65], None, ALU.mult).then_inc(S["st_out"], 1)
                dve.wait_ge(S["y_mm"], (g + 1) * NCH)
                nc.vector.memset(small[:, 30:31], 0.0).then_inc(S["dve_free"], 1)

            dve.sem_inc(S["hid_made"], 1)
            dve.sem_inc(S["gate_made2"], 1)
            for q in range(2):
                nc.vector.memset(ybuf[:, 4:8, q * (T + 1):q * (T + 1) + 1], 0.0)
            dve.wait_ge(S["consts_loaded"], 32)
            dve.wait_ge(S["bias_loaded"], 32)
            ts(gains8[:, 0:1], vec("q_norm_g"), 0.125, None, ALU.mult)
            na_bias = work[:, 12:24, :].rearrange("p k t -> p (k t)").rearrange("p (h k) -> p h k", h=8)
            na_mask = area[:, 24:26, :].rearrange("p k t -> p (k t)")[:, 0:768]
            pre("first", x_of)
            tt(na_bias, na_bias, na_mask.unsqueeze(1).broadcast_to([P, 8, 768]), ALU.add)
            for s in range(2):
                dve.wait_ge(S["slab_mm"], 11 + s)
                z = ybuf[:, 4 + 2 * s:6 + 2 * s, 1:T + 1]
                tt(z, banks(2 * s), z, ALU.mult).then_inc(banks_free[s], 1)
            dve.drain()
            for j in range(4):
                z = ybuf[:, 4 + j, :]
                ts(area[:, 16 + j, :], z[:, 0:T], vec("conv_w", j), None, ALU.mult)
                dve.drain()
                for n in (1, 2):
                    stt(out=area[:, 16 + j, :], in0=z[:, n:n + T], scalar=vec("conv_w", 4 * n + j), in1=area[:, 16 + j, :],
                        op0=ALU.mult, op1=ALU.add)
                    dve.drain()
            dve.wait_ge(S["slab_mm"], 12)
            tt(area[:, 16:20, :], area[:, 16:20, :], ybuf[:, 0:4, 0:T], ALU.mult)
            dve.drain()
            copy(hid_hi[:, 4:8, :], area[:, 16:20, :])
            dve.drain()
            tt(hid_lo[:, 4:8, :], area[:, 16:20, :], hid_hi[:, 4:8, :].bitcast(F32), ALU.subtract).then_inc(S["conv_done"], 1)
            dve.wait_ge(S["qk_sum"], 8)
            ts(rows16, ps[0:16, 4, :], 1 / 64, EPS, ALU.mult, ALU.add).then_inc(S["qk_mean"], 1)
            dve.wait_ge(S["qk_root"], 1)
            nc.vector.reciprocal(rows16, rows16b).then_inc(S["qk_recip"], 1)
            for j in range(8):
                dve.wait_ge(S["qk_bcast"], j + 1)
                if j < 4:
                    tt(scratch[:, j % 2, :].rearrange("p (j r c) -> p j r c", j=4, r=8),
                       work[:, j, :].rearrange("p (r j c) -> p j r c", j=4, r=8),
                       ps[:, 6 + j % 2, :].rearrange("p (r j c) -> p j r c", j=4, r=8), ALU.mult)
                    dve.drain()
                    inst = ts(work[:, j, :], scratch[:, j % 2, :], gains8[:, 0:1], None, ALU.mult)
                else:
                    inst = stt(out=work[:, j, :], in0=work[:, j, :], scalar=vec("k_norm_g"), in1=ps[:, 6 + j % 2, :],
                               op0=ALU.mult, op1=ALU.mult)
                inst.then_inc(S["qk_done"], 1)

            def bias_of(t):
                tile, j = divmod(t, 4)
                return na_bias[:, 2 * tile:2 * tile + 2, 256 * NA_CLASS[j]:256 * NA_CLASS[j] + 256]
            attention(0, bias_of)
            dve.wait_ge(S["at_osb"], STEPS[0])
            for j in range(4):
                o = work[:, j, :].rearrange("p (j r c) -> p r j c", j=4, r=8)
                copy(hid_hi[:, j, :].rearrange("p (r j c) -> p r j c", j=4, r=8), o)
            dve.drain()
            for j in range(4):
                o = work[:, j, :].rearrange("p (j r c) -> p r j c", j=4, r=8)
                inst = tt(hid_lo[:, j, :].rearrange("p (r j c) -> p r j c", j=4, r=8), o,
                          hid_hi[:, j, :].rearrange("p (r j c) -> p r j c", j=4, r=8).bitcast(F32), ALU.subtract)
            inst.then_inc(S["branch_made"], 1)
            n0 = FIRST["gates"]

            def gated(acc):
                def body(i, s, off):
                    dve.wait_ge(banks_free[s], i + (n0 // 2 + 1 + off))
                    a = pairs(acc)[:, i * 2 + s]
                    return tt(a, scratch[:, 0:2, :], a, ALU.mult)
                return body
            with dve.Fori(0, 2) as i:
                for s in range(2):
                    gated(ybuf)(i, s, 0).then_inc(S["gate_made2"], 1)
            with dve.Fori(0, 2) as i:
                for s in range(2):
                    gated(work)(i, s, 2).then_inc(S["gate_made2"], 1)
            dve.drain()
            for k in range(NT):
                tt(ybuf[:, k, 0:T], ybuf[:, k, 0:T], work[:, k, :], ALU.add).then_inc(S["tile_made"], 1)
            for k in range(NT):
                dve.wait_ge(S["merged_hi"], k + 1)
                inst = tt(act_lo[:, k, :], ybuf[:, k, 0:T], act_hi[:, k, :].bitcast(F32), ALU.subtract)
            inst.then_inc(S["merged_made"], 1)
            slabs(FIRST["w_o"], 4, add_to(x))
            pre("mlp", x_of)
            for cn in range(4):
                def relu2(i, s):
                    dve.wait_ge(S["gate_made"], i * 2 + (PAIR_STEPS[f"mlp{cn}"] + s))
                    hidden_pair(i * 2 + s, s)
                slabs(FIRST[f"mlp_in{cn}"], 4, relu2)
                slabs(FIRST[f"mlp_out{cn}"], 4, add_to(x))
            ffn(0)
            rwkv_dve()
            ffn(1)
            pre("kv", x_of)
            ffn(2)
            pre("mixer1_pre", x_of)
            with dve.Fori(0, 2) as i:
                for s in range(2):
                    dve.wait_ge(S["slab_mm"], i * 2 + (FIRST["q2"] + s + 1))
                    b = vecs[:, VEC["b_q"]:VEC["b_q"] + 8].rearrange("p (a b) -> p a b", b=2)[:, i * 2 + s]
                    tt(pairs(work)[:, i * 2 + s], banks(2 * s), b.unsqueeze(2).broadcast_to([P, 2, T]), ALU.add)
                    dve.drain()
                    ts(pairs(work)[:, i * 2 + s], pairs(work)[:, i * 2 + s], 0.125, None, ALU.mult).then_inc(banks_free[s], 1)
            dve.wait_ge(S["swa_loaded"], 16)
            swa_mask = scratch[:, 3, :].rearrange("p (b k) -> p b k", b=2)
            attention(1, lambda t: swa_mask[:, min(t % 4, 1), :].unsqueeze(1).broadcast_to([P, 2, 256]))
            for k in range(NT):
                dve.wait_ge(S["merged_hi"], NT + k + 1)
                inst = tt(act_lo[:, k, :], work[:, k, :], act_hi[:, k, :].bitcast(F32), ALU.subtract)
            inst.then_inc(S["branch_made"], 1)
            with dve.Fori(0, 2) as i:
                for s in range(2):
                    dve.wait_ge(S["slab_mm"], i * 2 + (FIRST["o2"] + s + 1))
                    b = vecs[:, VEC["b_o"]:VEC["b_o"] + 8].rearrange("p (a b) -> p a b", b=2)[:, i * 2 + s]
                    tt(pairs(ybuf)[:, i * 2 + s], banks(2 * s), b.unsqueeze(2).broadcast_to([P, 2, T]), ALU.add).then_inc(banks_free[s], 1)
            post("mixer1_post", 1.0)
            ffn(3)


def stream_of(a):
    out = np.zeros((SLABS, P, SLAB), np.float32)

    def put(name, w, width=256, tiles=None):
        kt = w.shape[0] // P
        v = w.reshape(kt, P, w.shape[1] // width, width).transpose(2, 1, 0, 3)
        n = FIRST[name]
        out[n:n + v.shape[0], :, 0:kt * width] = v.reshape(v.shape[0], P, kt * width)

    w_in = a["w_in"][0]
    put("qkvconv", w_in[:, 0:3072])
    put("gates", w_in[:, 3072:5120])
    put("attn_branch", a["w_attn_branch"][0], 512)
    put("conv_branch", a["w_conv_branch"][0], 512)
    put("w_o", a["w_o"][0])
    for cn in range(4):
        put(f"mlp_in{cn}", a["w_mlp_in"][0][:, 1024 * cn:1024 * cn + 1024])
        put(f"mlp_out{cn}", a["w_mlp_out"][0][1024 * cn:1024 * cn + 1024])
    for f in range(4):
        wi, wo = a["ffn_w_in_2"][f // 2, f % 2], a["ffn_w_out_2"][f // 2, f % 2]
        t0 = 0
        for cn, n in enumerate(FFN_CHUNKS):
            g = wi[:, P * t0:P * (t0 + n)].reshape(D, n // 2, 256)
            u = wi[:, 2816 + P * t0:2816 + P * (t0 + n)].reshape(D, n // 2, 256)
            put(f"ffn{f}_in{cn}", np.stack([g, u], 2).reshape(D, n * 256))
            put(f"ffn{f}_out{cn}", wo[P * t0:P * (t0 + n)])
            t0 += n
    put("lora", np.concatenate([a["rwkv_w1_2"][0], a["rwkv_a1_2"][0], a["rwkv_g1_2"][0]], 1))
    n = FIRST["lora"] + 1
    out[n, 0:64, 0:1024], out[n, 64:128, 0:1024] = a["rwkv_w2_2"][0], a["rwkv_a2_2"][0]
    out[n, :, 1024:2048] = a["rwkv_g2_2"][0]
    for name, j in (("r", 0), ("k", 1), ("v", 2)):
        put(name, a["rwkv_w_rkv_2"][0, j])
    put("rwkv_o", a["rwkv_w_o_2"][0])
    put("kv", a["w_kv_2"])
    put("q2", a["attn_w_q_2"][0].reshape(D, 16, 64)[:, HEADS].reshape(D, D))
    put("o2", a["attn_w_o_2"][0].reshape(16, 64, D)[HEADS].reshape(D, D))
    return out


HEADS = [8 * (n // 8) + 4 * (n % 2) + (n % 8) // 2 for n in range(16)]


def vectors_of(a):
    rows = {"norm1_g": a["norm1_g"], "norm2_g": a["norm2_g"], "kv_norm_g": a["kv_norm_g_2"], "b_kv": a["b_kv_2"],
            "w0": a["rwkv_w0_2"], "a0": a["rwkv_a0_2"], "k_k": a["rwkv_k_k_2"], "k_a": a["rwkv_k_a_2"],
            "r_k": a["rwkv_r_k_2"], "gn_g": a["rwkv_gn_g_2"], "gn_b": a["rwkv_gn_b_2"], "b_o": a["attn_b_o_2"],
            "b_q": a["attn_b_q_2"].reshape(16, 64)[HEADS], "conv_w": a["conv_w"],
            "q_norm_g": np.concatenate([a["q_norm_g"]] * 2), "k_norm_g": np.concatenate([a["k_norm_g"]] * 2)}
    for i in range(12):
        rows[f"norm_g{i}"] = a["norm_g_2"][i // 6, i % 6]
    for i in range(6):
        rows[f"mu{i}"] = a["rwkv_mu_2"][0, i]
    return np.ascontiguousarray(np.concatenate([np.reshape(rows[n], (-1, P)) for n in VEC]).T)


def kernel(**inputs):
    import concourse.bacc as bacc
    from concourse.bass_utils import run_bass_kernel_spmd as run

    a = {k: np.asarray(v) for k, v in inputs.items()}
    mask, rel_r, rel_c = na_tables()
    rpb = a["rpb"][0]
    bias = np.stack([rpb[:, rel_r, rel_c[:, n, :]] for n in range(3)], 2).transpose(1, 0, 2, 3)
    consts = constants()
    consts[:, NCST - 16:] = a["attn_sinks_2"][0][HEADS][None, :]
    arrays = {
        "x_in": np.ascontiguousarray(a["x"][0].T.reshape(NT, P, T).transpose(1, 0, 2)),
        "stream": stream_of(a), "vec_in": vectors_of(a), "cst_in": consts, "spread_in": spread_rows(),
        "restart_in": scan_restart(), "bias_in": np.ascontiguousarray(bias.reshape(P, 12, T)), "mask_in": mask.reshape(P, 768),
        "swa_in": swa_masks(),
    }
    nc = bacc.Bacc("TRN2", target_bir_lowering=False, num_devices=1)
    aps = {n: nc.dram_tensor(n, v.shape, mybir.dt.from_np(v.dtype), kind="ExternalInput").ap() for n, v in arrays.items()}
    x_out = nc.dram_tensor("x_out", (P, NT, T), F32, kind="ExternalOutput").ap()
    build(nc, x_out=x_out, **aps)
    r = run(nc, [arrays], core_ids=[0])
    out = r.results[0]["x_out"]
    return np.ascontiguousarray(out.transpose(1, 0, 2).reshape(D, T).T)[None]
```

```python
from contextlib import ExitStack

import numpy as np
from concourse import mybir
from concourse.alu_op_type import AluOpType as ALU

F32 = mybir.dt.float32
F32R = mybir.dt.float32r
ACT = mybir.ActivationFunctionType
AX_X = mybir.AxisListType.X

P = 128
T = 512
D = 1024
NT = D // P
SLAB = 2048
EPS = 1e-6
GN_EPS = 64e-5
DECAY = float(np.exp(-0.5))
CH = 64
NCH = T // CH
FFN_TILES = 22
FFN_CHUNKS = (8, 8, 6)
MASKED = -1e30

_PARTS = [("qkvconv", 12), ("attn_branch", 2), ("conv_branch", 2), ("gates", 8), ("w_o", 4)]
for _c in range(4):
    _PARTS += [(f"mlp_in{_c}", 4), (f"mlp_out{_c}", 4)]


def _ffn_parts(f):
    out = []
    for c, n in enumerate(FFN_CHUNKS):
        out += [(f"ffn{f}_in{c}", n), (f"ffn{f}_out{c}", 4)]
    return out


_PARTS += _ffn_parts(0) + [("lora", 2), ("r", 4), ("k", 4), ("v", 4), ("rwkv_o", 4)] + _ffn_parts(1)
_PARTS += [("kv", 2)] + _ffn_parts(2) + [("q2", 4), ("o2", 4)] + _ffn_parts(3)
FIRST = {}
_n = 0
for _name, _k in _PARTS:
    FIRST[_name] = _n
    _n += _k
SLABS = _n

VEC = {}
_v = 0
for _name, _k in ([("norm1_g", 8), ("norm2_g", 8)] + [(f"norm_g{i}", 8) for i in range(12)]
                  + [(f"mu{i}", 8) for i in range(6)]
                  + [(n, 8) for n in ("w0", "a0", "k_k", "k_a", "r_k", "gn_g", "gn_b", "kv_norm_g", "b_q", "b_o")]
                  + [("b_kv", 4), ("q_norm_g", 1), ("k_norm_g", 1), ("conv_w", 12)]):
    VEC[_name] = _v
    _v += _k
NVEC = _v

CST = {}
_c0 = 0
for _name, _k in [("ident", 128), ("ones", 128), ("blk64", 128), ("blk1", 128), ("sel", 128), ("mean", 1),
                  ("strict", 64), ("incl", 64), ("eye", 64), ("first", 64), ("firstT", 64),
                  ("lev0", 64), ("lev1", 64), ("lev2", 64), ("lev3", 64), ("lev4", 64), ("sinks", 16)]:
    CST[_name] = _c0
    _c0 += _k
NCST = _c0


def constants():
    c = np.zeros((P, NCST), np.float32)
    i = np.arange(P)
    c[:, CST["ident"]:CST["ident"] + 128] = np.eye(P)
    c[:, CST["ones"]:CST["ones"] + 128] = 1
    blk = (i[:, None] // 64 == i[None, :] // 64)
    c[:, CST["blk64"]:CST["blk64"] + 128] = blk / 64
    c[:, CST["blk1"]:CST["blk1"] + 128] = blk
    for j in range(8):
        c[i, CST["sel"] + 16 * j + 2 * j + i // 64] = 1
    c[:, CST["mean"]] = 1 / D
    r, k = (i % 64)[:, None], np.arange(64)[None, :]
    c[:, CST["strict"]:CST["strict"] + 64] = r < k
    c[:, CST["incl"]:CST["incl"] + 64] = r <= k
    c[:, CST["eye"]:CST["eye"] + 64] = r == k
    c[:, CST["first"]:CST["first"] + 64] = -((r % 2 == 1) & (k == r - 1)).astype(np.float32)
    c[:, CST["firstT"]:CST["firstT"] + 64] = -((k % 2 == 1) & (r == k - 1)).astype(np.float32)
    for n, s in enumerate((2, 4, 8, 16, 32)):
        c[:, CST[f"lev{n}"]:CST[f"lev{n}"] + 64] = -(((r // s) % 2 == 1) & (k // s == r // s - 1)).astype(np.float32)
    return c


def spread_rows():
    return (np.arange(16)[:, None] == np.arange(1024)[None, :] // 64).astype(np.float32)


def scan_restart():
    return np.broadcast_to((np.arange(T) % CH != 0).astype(np.float32), (P, T)).copy()


NA_CLASS = (0, 1, 1, 2)
NA_KEY0 = (0, 8, 24, 32)


def na_tables():
    r, cc = np.divmod(np.arange(P), 16)
    kr, kc = np.divmod(np.arange(256), 32)
    mask = np.zeros((P, 3, 256), np.float32)
    rel_r = kr[None, :] - r[:, None] + 7
    rel_c = np.zeros((P, 3, 256), np.int64)
    for n, j in enumerate((0, 1, 3)):
        q = 16 * j + cc
        key = NA_KEY0[j] + kc
        start = np.clip(q - 8, 0, 48)
        ok = (key[None, :] >= start[:, None]) & (key[None, :] < start[:, None] + 16)
        mask[:, n, :] = np.where(ok, 0, MASKED)
        rel_c[:, n, :] = np.clip(key[None, :] - q[:, None] + 15, 0, 30)
    return mask, rel_r, rel_c


def swa_masks():
    q, s = np.arange(P)[:, None], np.arange(256)[None, :]
    ok = (s - 128 <= q) & (s > q)
    return np.stack([np.where(ok & (s >= 128), 0, MASKED), np.where(ok, 0, MASKED)], 1).astype(np.float32)


def build(nc, x_in, stream, vec_in, cst_in, spread_in, restart_in, bias_in, mask_in, swa_in,
          x_out):
    ctx = ExitStack()
    with ctx:
        def sb(name, shape, dt=F32):
            return ctx.enter_context(nc.sbuf_tensor(name, shape, dt))

        def sem(name):
            return ctx.enter_context(nc.semaphore(name))

        w_raw = sb("w_raw", [P, 2, SLAB])
        w_hi = sb("w_hi", [P, 2, SLAB], F32R)
        w_lo = sb("w_lo", [P, 2, SLAB], F32R)
        x = sb("x_res", [P, NT, T])
        ybuf = sb("ybuf", [P, NT, T + 2])
        work = sb("work", [P, 24, T])
        scratch = sb("scratch", [P, 4, T])
        vecs = sb("vecs", [P, NVEC])
        cst = sb("cst", [P, NCST])
        gains8 = sb("gains8", [P, 1])
        omu = sb("omu", [P, 48])
        oma = sb("oma", [P, 8])
        small = sb("small", [P, 32])
        area = sb("area", [P, 32, T])
        base = nc.sbuf_base - 32 * T * 4
        act_hi = nc.alloc_sbuf_tensor_at("act_hi", [P, NT, T], F32R, offset=base)
        act_lo = nc.alloc_sbuf_tensor_at("act_lo", [P, NT, T], F32R, offset=base + 8 * T * 4)
        hid_hi = nc.alloc_sbuf_tensor_at("hid_hi", [P, NT, T], F32R, offset=base + 16 * T * 4)
        hid_lo = nc.alloc_sbuf_tensor_at("hid_lo", [P, NT, T], F32R, offset=base + 24 * T * 4)
        ps = ctx.enter_context(nc.psum_tensor("ps", [P, 8, 512], F32))
        spill = nc.dram_tensor("spill", [8, P, NT, T], F32).ap()
        R_, K_, V_, LW_, A_, G_, Y_, BON_ = range(8)

        S = {n: sem(n) for n in (
            "consts_loaded", "x_loaded", "bias_loaded", "raw0_loaded", "raw1_loaded", "hi_made", "lo_made", "slab_mm",
            "banks0_free", "banks1_free",
            "sq_made", "sum_mm", "mean_made", "root_made", "diag_made", "rstd_mm", "u_made", "uhi_made", "ulo_made",
            "t_scaled", "x_made", "sig_made", "gdiag_made", "grstd_mm",
            "gate_made", "hid_made", "tile_made",
            "qk_sq", "qk_sum", "qk_mean", "qk_root", "qk_recip", "qk_bcast", "qk_done",
            "at_s", "at_vblk", "at_vt", "at_max", "at_exp", "at_vtok", "at_p", "at_pt", "at_ptsb", "at_o", "at_osb",
            "branch_made", "merged_made", "conv_done", "out_stored",
            "t_made", "mix_made", "mix_hi", "mix_lo", "lora_mm", "lora_lo", "lora_out", "spilled",
            "duo_loaded", "duo_vec", "kk_sq", "kk_sum", "kk_max", "kk_root", "kk_recip", "act_prep", 
            "dve_prep", "job0_mm", "job1_mm", "job0_out", "job1_out",
            "rhs_mm", "rhs_out", "sa_mm", "sa_out", "st_mm", "st_out", "st_out1", "y_mm", "y_out",
            "gn_loaded", "gn_mean", "gn_d", "gn_sq", "gn_sum", "gn_var", "gn_root", "gn_recip", "gn_bcast",
            "gn_scaled", "gn_affine", "gn_gated", "gn_hi", "gn_lo", "swa_loaded", "vtok_mm", "vtok_out",
            "pe_waited", "spread_loaded", "dve_free", "merged_hi",
        )}
        raw_loaded = (S["raw0_loaded"], S["raw1_loaded"])
        banks_free = (S["banks0_free"], S["banks1_free"])

        def c(name, a=0, n=None, p0=0, p1=P):
            n = n if n is not None else {"ident": 128, "ones": 128, "blk64": 128, "blk1": 128, "sel": 16}.get(name, 64)
            return cst[p0:p1, CST[name] + a:CST[name] + a + n]

        def vec(name, k=0):
            return vecs[:, VEC[name] + k:VEC[name] + k + 1]

        def pairs(t):
            return t[:, :, 0:T].rearrange("p (a b) t -> p a b t", b=2)

        def banks(a, n=2):
            return ps[:, a:a + n, :]

        yflat = ybuf[:].rearrange("p k t -> p (k t)")
        spread, rows16, restart = yflat[:, 0:1024], yflat[0:16, 1024:1536], yflat[:, 1536:2048]
        rows16b = scratch[0:16, 3, :]
        rows16b_duo = work[0:16, 22, :]
        MIX = (1, 4, 5, 0, 2, 3)

        def u_now(k):
            return ybuf[:, k, 1:T + 1]

        sinks = cst[:, NCST - 16:NCST]
        p_buf = yflat[:, 1536:3072].rearrange("p (b h k) -> p b h k", b=3, h=2)
        pt_buf = yflat[:, 3072:4096].rearrange("p (b h a k) -> p b h a k", b=2, h=2, a=2)
        vb_buf = scratch[:, 2, :].rearrange("p (b k) -> p b k", b=2)
        vt_buf = scratch[:, 3, :].rearrange("p (b a k) -> p b a k", b=2, a=2)

        NORMS = ["first", "mlp"]
        for f in range(4):
            NORMS += [f"ffn{f}_pre", f"ffn{f}_post"]
            if f == 0:
                NORMS += ["mixer0_pre", "mixer0_post"]
            if f == 1:
                NORMS += ["kv"]
            if f == 2:
                NORMS += ["mixer1_pre", "mixer1_post"]
        NORM = {n: i for i, n in enumerate(NORMS)}
        PRE = [n for n in NORMS if not n.endswith("post")]
        PRE_NO = {n: i for i, n in enumerate(PRE)}
        SPLIT_NO = {n: i for i, n in enumerate(n for n in PRE if n != "mixer0_pre")}
        POST_NO = {n: i for i, n in enumerate([n for n in NORMS if n.endswith("post")])}

        def squares(name):
            return work[:, 0:8, :] if name == "first" else work[:, 12:20, :]

        AFTER_POST = {"ffn0_post": "lora", "mixer0_post": "ffn1_in0", "ffn1_post": "kv", "ffn2_post": "q2",
                      "mixer1_post": "ffn3_in0"}
        GAIN = {"first": "norm1_g", "mlp": "norm2_g", "kv": "kv_norm_g",
                "ffn0_pre": "norm_g0", "ffn0_post": "norm_g1", "mixer0_pre": "norm_g2", "mixer0_post": "norm_g3",
                "ffn1_pre": "norm_g4", "ffn1_post": "norm_g5", "ffn2_pre": "norm_g6", "ffn2_post": "norm_g7",
                "mixer1_pre": "norm_g8", "mixer1_post": "norm_g9", "ffn3_pre": "norm_g10", "ffn3_post": "norm_g11"}

        PAIR_STEPS = {}
        _h = 0
        for cn in range(4):
            PAIR_STEPS[f"mlp{cn}"] = _h
            _h += 4
        for f in range(4):
            for cn, n in enumerate(FFN_CHUNKS):
                PAIR_STEPS[f"ffn{f}_{cn}"] = _h
                _h += n // 2
        SCORE_BANKS = (6, 0)
        STEPS = (16, 32)

        IN_R, IN_K, IN_V, IN_LW, IN_A = (work[:, 2 * n:2 * n + 2, :] for n in range(5))
        TMP = {}
        for n, name in enumerate(("X", "kk", "b", "k", "rk", "Y")):
            TMP[name] = [work[:, 10 + 2 * n + q, :] for q in range(2)]
        for n, name in enumerate(("R", "KK", "KabT", "KakT", "RkT", "RbT", "XT", "kT", "bT", "vT")):
            TMP[name] = [area[:, 2 * n + q, :] for q in range(2)]
        TMP["v"] = [work[:, 4 + q, :] for q in range(2)]
        y_sb, bonus_sb = work[:, 22:24, :], scratch[:, 2:4, :]
        aflat = area[:].rearrange("p k t -> p (k t)")
        at0 = 20 * T
        grown = [aflat[:, at0 + 520 * q:at0 + 520 * q + 520].rearrange("p (n t) -> p n t", t=65) for q in range(2)]
        state = aflat[:, at0 + 1056:at0 + 1056 + 256].rearrange("p (b k) -> p b k", b=2)
        rhs_sb = aflat[:, at0 + 1312:at0 + 1440]
        sa_sb = aflat[:, at0 + 1440:at0 + 1568]
        duo_vec = small[:, 12:20]
        JOBS = [("kk", None, None, None), ("KabT", "b", "KK", "strict"), ("X", "KK", "b", "first"),
                ("KakT", "k", "KK", "strict")]
        late = [("RkT", "k", "R", "incl"), ("RbT", "b", "R", "incl"), ("kT", "k", None, None), ("bT", "b", None, None),
                ("vT", "v", None, None), ("bonus", None, None, None)]
        for level in range(5):
            JOBS.append(("Y", "KabT", "X", f"lev{level}"))
            JOBS.append(late.pop(0))
            if level < 4:
                JOBS.append(("X+", "XT", "Y", None))
            JOBS.append(("XT+", "Y", "XT", None))
            if level == 0:
                JOBS.append(late.pop(0))
        at_job = {}
        JOB_NEEDS = []
        for j, (name, lhs, rhs, _) in enumerate(JOBS):
            needs = [at_job[w] for w in (lhs, rhs) if w in at_job]
            if name in ("Y", "X+", "XT+"):
                needs += [at_job[w] for w in ("Y", "X", "XT") if w in at_job and w in (lhs, rhs)]
            if j >= 4:
                needs.append(j - 4)
            JOB_NEEDS.append([max(needs)] if needs else [])
            at_job[{"X+": "X", "XT+": "XT", "X": "X"}.get(name, name)] = j
            if name == "X":
                at_job["XT"] = j
        job_mm, job_out = (S["job0_mm"], S["job1_mm"]), (S["job0_out"], S["job1_out"])

        def na_q(t, h):
            return work[64 * h:64 * h + 64, t // 4, 128 * (t % 4):128 * (t % 4) + 128]

        def na_k(t, h):
            k = work[64 * h:64 * h + 64, 4 + t // 4, :].rearrange("p (r c) -> p r c", c=64)
            return [k[:, :, NA_KEY0[t % 4]:NA_KEY0[t % 4] + 32]]

        def swa_q(t, h):
            return work[64 * h:64 * h + 64, t // 4, 128 * (t % 4):128 * (t % 4) + 128]

        def swa_k(t, h):
            b = t % 4
            return [work[64 * h:64 * h + 64, 20 + t // 16, 128 * n:128 * n + 128] for n in (max(b - 1, 0), b)]

        def swa_v(t, h, part):
            b = t % 4
            n = b if part else max(b - 1, 0)
            return work[:, 16 + n // 2, 256 * (n % 2) + 128 * (t // 16) + 64 * h:256 * (n % 2) + 128 * (t // 16) + 64 * h + 64]

        block = ctx.enter_context(nc.Block())

        @block.sync
        def _(sp):
            sp.dma_start(cst[:], cst_in).then_inc(S["consts_loaded"], 16)
            sp.dma_start(vecs[:], vec_in).then_inc(S["consts_loaded"], 16)
            sp.dma_start(x[:], x_in).then_inc(S["x_loaded"], 16)
            for s in range(2):
                sp.dma_start(w_raw[:, s, :], stream[s]).then_inc(raw_loaded[s], 16)
            sp.dma_start(work[:, 12:24, :], bias_in).then_inc(S["bias_loaded"], 16)
            sp.dma_start(area[:, 24:26, :].rearrange("p k t -> p (k t)")[:, 0:768], mask_in).then_inc(S["bias_loaded"], 16)
            with sp.Fori(1, SLABS // 2) as i:
                for s in range(2):
                    sp.wait_ge(S["lo_made"], i * 2 + (s - 1))
                    sp.dma_start(w_raw[:, s, :], stream[i * 2 + s]).then_inc(raw_loaded[s], 16)

        @block.gpsimd
        def _(pool):
            tt = nc.gpsimd.tensor_tensor

            def lo(n, s):
                pool.wait_ge(S["hi_made"], n + 1)
                tt(w_lo[:, s, :], w_raw[:, s, :], w_hi[:, s, :].bitcast(F32), ALU.subtract).then_inc(S["lo_made"], 1)

            def split(first, end):
                with pool.Fori(0, (end - first) // 2) as i:
                    lo(i * 2 + first, 1)
                    lo(i * 2 + (first + 1), 0)

            lo(0, 0)
            done = 1
            for name, n in POST_NO.items():
                end = FIRST[AFTER_POST[name]] + 1 if name in AFTER_POST else SLABS - 1
                split(done, end)
                done = end
                if name not in AFTER_POST:
                    lo(end, 1)
                for k in range(NT):
                    pool.wait_ge(S["t_scaled"], NT * n + k + 1)
                    tt(x[:, k, :], x[:, k, :], work[:, k, :], ALU.add).then_inc(S["x_made"], 1)

        @block.tensor
        def _(pe):
            mm = nc.tensor.matmul

            def slab_start(first, i, s):
                pe.wait_ge(S["lo_made"], i * 2 + (first + s + 1))
                if first or not isinstance(i, int):
                    pe.wait_ge(banks_free[s], i + first // 2)

            def slab(first, i, s, hi, lo, kt=8, middle=None):
                slab_start(first, i, s)
                for m in range(2):
                    for k in range(kt):
                        inst = product(s, m, k, hi, lo, k == kt - 1)
                    if m == 0 and middle is not None:
                        middle()
                inst.then_inc(S["slab_mm"], 1)

            def product(s, m, k, hi, lo, end):
                a = k * 256 + m * 128
                wh, wl = w_hi[:, s, a:a + 128], w_lo[:, s, a:a + 128]
                out = ps[:, 2 * s + m, :]
                mm(out, wh, hi[:, k, :], start=(k == 0), stop=False)
                mm(out, wh, lo[:, k, :], start=False, stop=False)
                return mm(out, wl, hi[:, k, :], start=False, stop=end)

            def slabs(first, count, hi, lo, kt=8, begin=0):
                with pe.Fori(begin, count // 2) as i:
                    for s in range(2):
                        slab(first, i, s, hi, lo, kt=kt)

            def eager_slab(first, hi, lo, kt, wait_tile):
                slab_start(first, 0, 0)
                for k in range(kt):
                    wait_tile(k)
                    for m in range(2):
                        inst = product(0, m, k, hi, lo, k == kt - 1)
                inst.then_inc(S["slab_mm"], 1)

            def out_slabs(key, first, kt):
                eager_out(key, first, kt)
                slab(first, 0, 1, hid_hi, hid_lo, kt=kt)
                slabs(first, 4, hid_hi, hid_lo, kt=kt, begin=1)

            def eager_out(key, first, kt):
                def pair_made(k):
                    if k % 2 == 0:
                        pe.wait_ge(S["hid_made"], PAIR_STEPS[key] + k // 2 + 1)
                eager_slab(first, hid_hi, hid_lo, kt, pair_made)

            def pre_slabs(name, first, count):
                eager_slab(first, act_hi, act_lo, NT, lambda k: pe.wait_ge(S["ulo_made"], NT * SPLIT_NO[name] + k + 1))
                for n in range(4):
                    sums(name, n)
                slab(first, 0, 1, act_hi, act_lo, middle=lambda: spread_rms(name))
                if count > 2:
                    slabs(first, count, act_hi, act_lo, begin=1)

            def post_slabs(name, first, hi, lo, kt=8, key=None):
                for i in range(2):
                    for s in range(2):
                        if i and s:
                            sums(name, 0)
                            sums(name, 1)
                        if key is not None and i + s == 0:
                            eager_out(key, first, kt)
                        else:
                            slab(first, i, s, hi, lo, kt=kt)
                sums(name, 2)
                sums(name, 3)
                spread_rms(name)

            def wide_slab(first, s, hi, lo, k0):
                slab_start(first, 0, s)
                for m in range(4):
                    for k in range(4):
                        a = k * 512 + m * 128
                        wh, wl = w_hi[:, s, a:a + 128], w_lo[:, s, a:a + 128]
                        out = ps[:, 4 * s + m, :]
                        mm(out, wh, hi[:, k0 + k, :], start=(k == 0), stop=False)
                        mm(out, wh, lo[:, k0 + k, :], start=False, stop=False)
                        inst = mm(out, wl, hi[:, k0 + k, :], start=False, stop=(k == 3))
                inst.then_inc(S["slab_mm"], 1)

            def sums(name, n):
                r = NORM[name]
                pe.wait_ge(S["sq_made"], 4 * r + n + 1)
                for k in (2 * n, 2 * n + 1):
                    for t in range(4):
                        inst = mm(ps[:, 4, t:t + 1], squares(name)[:, k, 128 * t:128 * t + 128], c("mean", n=1),
                                  start=(k == 0 and t == 0), stop=(k == NT - 1), skip_group_check=True)
                inst.then_inc(S["sum_mm"], 1)

            def spread_rms(name):
                pe.wait_ge(S["diag_made"], NORM[name] + 1)
                mm(ps[:, 5, :], c("ones"), scratch[:, 2, :], start=True, stop=True).then_inc(S["rstd_mm"], 1)

            def ffn(f):
                for cn, kt in enumerate(FFN_CHUNKS):
                    key, first = f"ffn{f}_{cn}", FIRST[f"ffn{f}_in{cn}"]
                    if cn == 0:
                        pre_slabs(f"ffn{f}_pre", first, kt)
                    else:
                        slabs(first, kt, act_hi, act_lo)
                    if cn < 2:
                        out_slabs(key, first + kt, kt)
                    else:
                        post_slabs(f"ffn{f}_post", first + kt, hid_hi, hid_lo, kt=kt, key=key)

            def attention(a, q_of, k_of, v_of):
                g0, steps = 16 * a, STEPS[a]
                for t in range(steps + 3):
                    if t < steps:
                        if t >= 2:
                            pe.wait_ge(S["at_max"], g0 + t - 1)
                        for h in range(2):
                            for part, keys in enumerate(k_of(t, h)):
                                n = 256 // len(k_of(t, h))
                                inst = mm(ps[:, SCORE_BANKS[t % 2] + h, n * part:n * part + n], q_of(t, h), keys, start=True, stop=True)
                        inst.then_inc(S["at_s"], 1)
                    if a == 0 and 1 <= t <= steps:
                        u = t - 1
                        if u:
                            pe.wait_ge(S["at_vtok"], u)
                        pe.wait_ge(S["at_vblk"], u + 1)
                        for part in range(2):
                            inst = nc.tensor.transpose(ps[:, 5, 128 * part:128 * part + 128],
                                                       vb_buf[:, u % 2, 128 * part:128 * part + 128], c("ident"))
                        inst.then_inc(S["at_vt"], 1)
                    if 2 <= t <= steps + 1:
                        u = t - 2
                        pe.wait_ge(S["at_p"], g0 + u + 1)
                        if u:
                            pe.wait_ge(S["at_ptsb"], g0 + u)
                        for h in range(2):
                            for part in range(2):
                                inst = nc.tensor.transpose(ps[:, 4, 256 * h + 128 * part:256 * h + 128 * part + 128],
                                                           p_buf[:, u % 3, h, 128 * part:128 * part + 128], c("ident"))
                        inst.then_inc(S["at_pt"], 1)
                    if t >= 3:
                        u = t - 3
                        pe.wait_ge(S["at_ptsb"], g0 + u + 1)
                        if u:
                            pe.wait_ge(S["at_osb"], g0 + u)
                        elif a == 0:
                            pe.wait_ge(S["at_vtok"], u + 1)
                        for h in range(2):
                            for part in range(2):
                                v = vt_buf[:, u % 2, part, 64 * h:64 * h + 64] if a == 0 else v_of(u, h, part)
                                inst = mm(ps[64 * h:64 * h + 64, 3, 0:128], v, pt_buf[:, u % 2, h, part, :],
                                          start=(part == 0), stop=(part == 1))
                        inst.then_inc(S["at_o"], 1)

            def heads_chunks(out, lhs, rhs):
                for n in range(NCH):
                    for h in range(2):
                        a, b = 64 * h, 64 * h + 64
                        inst = mm(out[a:b, 64 * n:64 * n + 64], lhs(a, b, n), rhs(a, b, n), start=True, stop=True)
                return inst

            def waited():
                pe.sem_inc(S["pe_waited"], 1)

            def chunk_of(tile):
                return lambda a, b, n: tile[a:b, 64 * n:64 * n + 64]

            def rwkv_duo(g):
                for q in range(2):
                    pe.wait_ge(S["kk_sq"], g * 2 + (q + 1))
                    inst = mm(ps[0:16, 0, :], c("sel", 16 * q), scratch[:, q, :], start=(q == 0), stop=(q == 1))
                inst.then_inc(S["kk_sum"], 1)
                for j, (name, lhs, rhs, _) in enumerate(JOBS):
                    for q in range(2):
                        if j == 0:
                            pe.wait_ge(S["kk_recip"], g + 1)
                        if j == 1:
                            pe.wait_ge(S["dve_prep"], g * 2 + 2)
                        for need in JOB_NEEDS[j]:
                            pe.wait_ge(job_out[q], g * len(JOBS) + (need + 1))
                        out = ps[:, 4 * q + j % 4, :]
                        waited()
                        if name == "kk":
                            inst = mm(out, spread[0:16, 128 * q:128 * q + 128], rows16, start=True, stop=True)
                        elif name == "bonus":
                            inst = mm(out, c("blk1"), TMP["rk"][q], start=True, stop=True)
                        elif rhs is None:
                            inst = heads_chunks(out, chunk_of(TMP[lhs][q]), lambda a, b, n: c("eye", p0=a, p1=b))
                        else:
                            inst = heads_chunks(out, chunk_of(TMP[lhs][q]), chunk_of(TMP[rhs][q]))
                        inst.then_inc(job_mm[q], 1)
                for n in range(NCH):
                    old = state[:, n % 2]

                    def part(bank, at, lhs, rhs, start, stop):
                        for q in range(2):
                            for h in range(2):
                                a, b = 64 * h, 64 * h + 64
                                inst = mm(ps[a:b, bank, at(q):at(q) + 64], lhs(a, b, q), rhs(a, b, q), start=start and q == 0,
                                          stop=stop, skip_group_check=True)
                        return inst

                    def ch(name):
                        return lambda a, b, q: TMP[name][q][a:b, 64 * n:64 * n + 64]

                    def st(a, b, q):
                        return old[a:b, 64 * q:64 * q + 64]

                    def at(q):
                        return 64 * q

                    if n == 0:
                        for q in range(2):
                            pe.wait_ge(job_out[q], (g + 1) * len(JOBS))
                    pe.wait_ge(S["st_out"], g * (NCH + 1) + (n + 1))
                    pe.wait_ge(S["st_out1"], g * (NCH + 1) + (n + 1))
                    waited()
                    part(0, at, ch("KK"), st, True, False)
                    part(0, at, ch("KakT"), ch("vT"), False, True).then_inc(S["rhs_mm"], 1)
                    if n >= 2:
                        pe.wait_ge(S["y_out"], g * NCH + (n - 1))
                        waited()
                    part(3 + n % 2, at, st, ch("R"), True, False)
                    part(3 + n % 2, at, ch("vT"), ch("RkT"), False, False)
                    part(2, at, lambda a, b, q: c("eye", p0=a, p1=b), st, True, False)
                    part(2, at, ch("kT"), ch("vT"), False, False)
                    pe.wait_ge(S["rhs_out"], g * NCH + (n + 1))
                    waited()
                    part(1, at, ch("XT"), lambda a, b, q: rhs_sb[a:b, 64 * q:64 * q + 64], True, True).then_inc(S["sa_mm"], 1)
                    pe.wait_ge(S["sa_out"], g * NCH + (n + 1))
                    waited()
                    part(2, at, ch("bT"), lambda a, b, q: sa_sb[a:b, 64 * q:64 * q + 64], False, True).then_inc(S["st_mm"], 1)
                    part(3 + n % 2, at, lambda a, b, q: sa_sb[a:b, 64 * q:64 * q + 64], ch("RbT"), False, True).then_inc(S["y_mm"], 1)

            pe.wait_ge(S["consts_loaded"], 32)
            pre_slabs("first", 0, 12)
            pe.wait_ge(S["conv_done"], 1)
            for j in range(8):
                pe.wait_ge(S["qk_sq"], j + 1)
                mm(ps[0:16, 4, :], c("sel", 16 * j), scratch[:, j % 2, :], start=(j == 0), stop=(j == 7)).then_inc(S["qk_sum"], 1)
            pe.wait_ge(S["qk_recip"], 1)
            pe.wait_ge(S["spread_loaded"], 16)
            for j in range(8):
                if j >= 2:
                    pe.wait_ge(S["qk_done"], j - 1)
                mm(ps[:, 6 + j % 2, :], spread[0:16, 128 * j:128 * j + 128], rows16, start=True, stop=True).then_inc(S["qk_bcast"], 1)
            pe.wait_ge(S["qk_done"], 8)
            attention(0, na_q, na_k, None)
            for s in range(2):
                pe.wait_ge(S["branch_made"], 1)
                wide_slab(FIRST["attn_branch"], s, hid_hi, hid_lo, 0)
            for s in range(2):
                wide_slab(FIRST["conv_branch"], s, hid_hi, hid_lo, 4)

            def spread_again():
                pe.wait_ge(banks_free[1], FIRST["gates"] // 2)
                pe.wait_ge(S["gdiag_made"], 1)
                mm(ps[:, 5, :], c("ones"), scratch[:, 2, :], start=True, stop=True).then_inc(S["grstd_mm"], 1)
            slab(FIRST["gates"], 0, 0, act_hi, act_lo, middle=spread_again)
            slab(FIRST["gates"], 0, 1, act_hi, act_lo)
            slabs(FIRST["gates"], 8, act_hi, act_lo, begin=1)
            pe.wait_ge(S["merged_made"], 1)
            slabs(FIRST["w_o"], 4, act_hi, act_lo)
            for cn in range(4):
                if cn == 0:
                    pre_slabs("mlp", FIRST["mlp_in0"], 4)
                else:
                    slabs(FIRST[f"mlp_in{cn}"], 4, act_hi, act_lo)
                out_slabs(f"mlp{cn}", FIRST[f"mlp_out{cn}"], 8)

            ffn(0)
            for n in range(4):
                sums("mixer0_pre", n)
            spread_rms("mixer0_pre")
            n = FIRST["lora"]
            pe.wait_ge(S["lo_made"], n + 1)
            for j, (col, hi, lo) in enumerate(((0, act_hi, act_lo), (0, hid_hi, hid_lo), (128, act_hi, act_lo))):
                pe.wait_ge(S["mix_lo"], NT * (j + 1))
                for k in range(NT):
                    a = k * 256 + col
                    wh, wl = w_hi[:, 0, a:a + 128], w_lo[:, 0, a:a + 128]
                    mm(ps[:, j, :], wh, hi[:, k, :], start=(k == 0), stop=False)
                    mm(ps[:, j, :], wh, lo[:, k, :], start=False, stop=False)
                    inst = mm(ps[:, j, :], wl, hi[:, k, :], start=False, stop=(k == NT - 1))
                inst.then_inc(S["lora_mm"] if j < 2 else S["slab_mm"], 1)
            pe.wait_ge(S["lora_lo"], 1)
            pe.wait_ge(S["lo_made"], n + 2)
            for j in range(24):
                kind, m = divmod(j, NT)
                if j >= 4:
                    pe.wait_ge(S["lora_out"], j - 3)
                a = 128 * m + (1024 if kind == 2 else 0)
                wh, wl = w_hi[:, 1, a:a + 128], w_lo[:, 1, a:a + 128]
                out = ps[:, j % 4, :]
                mm(out, wh, hid_hi[:, kind, :], start=True, stop=False)
                mm(out, wh, hid_lo[:, kind, :], start=False, stop=False)
                inst = mm(out, wl, hid_hi[:, kind, :], start=False, stop=True)
                inst.then_inc(S["lora_mm"] if j < 23 else S["slab_mm"], 1)
            pe.wait_ge(S["banks1_free"], FIRST["r"] // 2)
            pe.wait_ge(S["mix_lo"], NT * 4)
            slabs(FIRST["r"], 4, act_hi, act_lo)
            pe.wait_ge(S["mix_lo"], NT * 5)
            slabs(FIRST["k"], 4, hid_hi, hid_lo)
            pe.wait_ge(S["mix_lo"], NT * 6)
            slabs(FIRST["v"], 4, act_hi, act_lo)
            pe.wait_ge(banks_free[0], FIRST["rwkv_o"] // 2)
            pe.wait_ge(banks_free[1], FIRST["rwkv_o"] // 2)
            with pe.Fori(0, 4) as g:
                rwkv_duo(g)
            for m in range(NT):
                pe.wait_ge(S["gn_loaded"], 48)
                if m >= 2:
                    pe.wait_ge(S["gn_d"], m - 1)
                mm(ps[:, 4 + m % 2, :], c("blk64"), work[:, m, :], start=True, stop=True).then_inc(S["gn_mean"], 1)
                if m:
                    pe.wait_ge(S["gn_sq"], m)
                    mm(ps[0:16, 6, :], c("sel", 16 * (m - 1)), scratch[:, (m - 1) % 2, :], start=(m == 1), stop=False).then_inc(S["gn_sum"], 1)
            pe.wait_ge(S["gn_sq"], NT)
            mm(ps[0:16, 6, :], c("sel", 16 * 7), scratch[:, 1, :], start=False, stop=True).then_inc(S["gn_sum"], 1)
            pe.wait_ge(S["gn_recip"], 1)
            for m in range(NT):
                if m >= 2:
                    pe.wait_ge(S["gn_scaled"], m - 1)
                mm(ps[:, 4 + m % 2, :], spread[0:16, 128 * m:128 * m + 128], rows16, start=True, stop=True).then_inc(S["gn_bcast"], 1)
            pe.wait_ge(S["gn_lo"], NT)
            post_slabs("mixer0_post", FIRST["rwkv_o"], act_hi, act_lo)
            ffn(1)
            pre_slabs("kv", FIRST["kv"], 2)
            ffn(2)
            pre_slabs("mixer1_pre", FIRST["q2"], 4)
            for s in range(2):
                pe.wait_ge(banks_free[s], FIRST["o2"] // 2)
            for b in range(4):
                for a in range(2):
                    inst = nc.tensor.transpose(ps[:, 4 + b // 2, 256 * (b % 2) + 128 * a:256 * (b % 2) + 128 * a + 128],
                                               work[:, 22 + a, 128 * b:128 * b + 128], c("ident"))
            inst.then_inc(S["vtok_mm"], 1)
            pe.wait_ge(S["vtok_out"], 1)
            attention(1, swa_q, swa_k, swa_v)
            pe.wait_ge(S["branch_made"], 2)
            post_slabs("mixer1_post", FIRST["o2"], act_hi, act_lo)
            ffn(3)

        @block.scalar
        def _(act):
            af = nc.scalar.activation

            def hi_next(first, i, s):
                act.wait_ge(raw_loaded[1 - s], (i + (first // 2 + s + 1 if s else first // 2 + 1)) * 16)
                if first + s or not isinstance(i, int):
                    act.wait_ge(S["slab_mm"], i * 2 + (first + s))
                nc.scalar.copy(w_hi[:, 1 - s, :], w_raw[:, 1 - s, :]).then_inc(S["hi_made"], 1)

            def slabs(first, count, body=None, head=None):
                def one(i, s, more=True, head=None):
                    if more:
                        hi_next(first, i, s)
                    if head is not None:
                        head()
                    if body is not None:
                        act.wait_ge(S["slab_mm"], i * 2 + (first + s + 1))
                        body(i, s)
                begin = 1 if head is not None else 0
                end = first + count == SLABS
                if begin:
                    one(0, 0, head=head)
                    one(0, 1)
                if count // 2 - end > begin:
                    with act.Fori(begin, count // 2 - end) as i:
                        one(i, 0)
                        one(i, 1)
                if end:
                    one(count // 2 - 1, 0)
                    one(count // 2 - 1, 1, more=False)

            def evacuated(end):
                for s in range(2):
                    act.wait_ge(banks_free[s], end // 2)

            def root(name):
                act.wait_ge(S["mean_made"], NORM[name] + 1)
                af(small[:, 4:8], small[:, 0:4], ACT.Sqrt).then_inc(S["root_made"], 1)

            def norm_of_x(name):
                for n in range(4):
                    af(pairs(squares(name))[:, n], pairs(x)[:, n], ACT.Square).then_inc(S["sq_made"], 1)
                root(name)

            def pre(name, free, x_ready):
                act.wait_ge(S["slab_mm"], free)
                for k in range(NT):
                    x_ready(k)
                    af(act_hi[:, k, :], x[:, k, :], ACT.Copy, scale=vec(GAIN[name], k)).then_inc(S["uhi_made"], 1)

            def x_after(name):
                return lambda k: act.wait_ge(S["x_made"], NT * POST_NO[name] + k + 1)

            def x_after_slabs(first):
                return lambda k: act.wait_ge(banks_free[k // 2 % 2], first // 2 + k // 4 + 1)

            def post_slabs(name, first):
                def square(i, s):
                    act.wait_ge(banks_free[s], i + (first // 2 + 1))
                    af(pairs(squares(name))[:, i * 2 + s], pairs(ybuf)[:, i * 2 + s], ACT.Square).then_inc(S["sq_made"], 1)
                slabs(first, 4, square)
                root(name)

            def ffn(f, free, x_ready):
                pre(f"ffn{f}_pre", free, x_ready)
                for cn, n in enumerate(FFN_CHUNKS):
                    first = FIRST[f"ffn{f}_in{cn}"]

                    def silu(i):
                        act.wait_ge(banks_free[0], i + (first // 2 + 1))
                        af(work[:, 8:10, :], work[:, 8:10, :], ACT.Silu).then_inc(S["gate_made"], 1)
                    begin = 0
                    if cn == 0:
                        hi_next(first, 0, 0)
                        norm_of_x(f"ffn{f}_pre")
                        silu(0)
                        hi_next(first, 0, 1)
                        begin = 1
                    with act.Fori(begin, n // 2) as i:
                        hi_next(first, i, 0)
                        silu(i)
                        hi_next(first, i, 1)
                    if cn < 2:
                        slabs(first + n, 4)
                    else:
                        post_slabs(f"ffn{f}_post", first + n)

            def attention(a, exp_out):
                g0, steps = 16 * a, STEPS[a]
                for t in range(steps + 3):
                    if a == 0 and 1 <= t <= steps:
                        u = t - 1
                        tile, j = divmod(u, 4)
                        if u >= 2:
                            act.wait_ge(S["at_vt"], u - 1)
                        v = work[:, 8 + tile, :].rearrange("p (r c) -> p r c", c=64)[:, :, NA_KEY0[j]:NA_KEY0[j] + 32]
                        nc.scalar.copy(vb_buf[:, u % 2, :].rearrange("p (r c) -> p r c", c=32), v).then_inc(S["at_vblk"], 1)
                    if t < steps:
                        g, b, e = g0 + t, t % 3, t % 2
                        act.wait_ge(S["at_max"], g + 1)
                        for h in range(2):
                            inst = af(p_buf[:, b, h, :], p_buf[:, b, h, :], ACT.Exp,
                                      bias=small[:, 12 + 2 * e + h:13 + 2 * e + h],
                                      accum_out=small[:, 16 + 2 * e + h:17 + 2 * e + h])
                        if a == 1:
                            for h in range(2):
                                inst = af(small[:, 24 + 2 * e + h:25 + 2 * e + h],
                                          sinks[:, 2 * (t // 4) + h:2 * (t // 4) + h + 1], ACT.Exp,
                                          bias=small[:, 12 + 2 * e + h:13 + 2 * e + h])
                        inst.then_inc(S["at_exp"], 1)
                    if a == 0 and 1 <= t <= steps:
                        u = t - 1
                        act.wait_ge(S["at_vt"], u + 1)
                        if u >= 2:
                            act.wait_ge(S["at_o"], u - 1)
                        nc.scalar.copy(vt_buf[:, u % 2, :, :], ps[:, 5, 0:256].rearrange("p (a k) -> p a k", a=2)).then_inc(S["at_vtok"], 1)
                    if 2 <= t <= steps + 1:
                        u = t - 2
                        act.wait_ge(S["at_pt"], g0 + u + 1)
                        if u >= 2:
                            act.wait_ge(S["at_o"], g0 + u - 1)
                        nc.scalar.copy(pt_buf[:, u % 2, :, :, :],
                                       ps[:, 4, :].rearrange("p (h a k) -> p h a k", h=2, a=2)).then_inc(S["at_ptsb"], 1)
                    if t >= 3:
                        u = t - 3
                        act.wait_ge(S["at_o"], g0 + u + 1)
                        tile, j = divmod(u, 4)
                        nc.scalar.copy(work[:, tile, 128 * j:128 * j + 128], ps[:, 3, 0:128]).then_inc(S["at_osb"], 1)

            def mix(j, wait):
                dst = hid_hi if j in (1, 4) else act_hi
                for k in range(NT + 1):
                    if k < NT:
                        e = NT * j + k
                        if e >= 2:
                            act.wait_ge(S["mix_made"], e - 1)
                        af(scratch[:, k % 2, :], u_now(k), ACT.Copy, scale=omu[:, NT * MIX[j] + k:NT * MIX[j] + k + 1]).then_inc(S["t_made"], 1)
                    if k == 0:
                        wait()
                    if k:
                        e = NT * j + k - 1
                        act.wait_ge(S["mix_made"], e + 1)
                        nc.scalar.copy(dst[:, k - 1, :], scratch[:, 2 + (k - 1) % 2, :]).then_inc(S["mix_hi"], 1)

            def rwkv_act():
                act.wait_ge(S["x_made"], NT * (POST_NO["ffn0_post"] + 1))
                norm_of_x("mixer0_pre")
                n0 = FIRST["lora"]
                hi_next(n0, 0, 0)
                act.wait_ge(S["u_made"], NT)
                mix(0, lambda: None)
                mix(1, lambda: None)
                mix(2, lambda: act.wait_ge(S["lora_mm"], 1))
                act.wait_ge(S["lora_mm"], 1)
                af(work[0:64, 0, :], ps[0:64, 0, :], ACT.Tanh)
                act.wait_ge(S["lora_mm"], 2)
                nc.scalar.copy(work[64:128, 1, :], ps[64:128, 1, :])
                act.wait_ge(S["slab_mm"], n0 + 1)
                af(work[:, 2, :], ps[:, 2, :], ACT.Sigmoid).then_inc(banks_free[0], 1)
                hi_next(n0, 0, 1)
                act.wait_ge(S["lora_lo"], 1)
                for j in range(24):
                    kind, m = divmod(j, NT)
                    if j < 23:
                        act.wait_ge(S["lora_mm"], j + 3)
                    else:
                        act.wait_ge(S["slab_mm"], n0 + 2)
                    if kind < 2:
                        inst = af(work[:, j, :], ps[:, j % 4, :], ACT.Sigmoid, bias=vec(("w0", "a0")[kind], m))
                    else:
                        inst = nc.scalar.copy(work[:, j, :], ps[:, j % 4, :])
                    inst.then_inc(S["lora_out"] if j < 23 else banks_free[1], 1)
                act.wait_ge(banks_free[1], n0 // 2 + 1)
                for kind, row in enumerate((LW_, A_, G_)):
                    act.dma_start(spill[row], work[:, 8 * kind:8 * kind + 8, :]).then_inc(S["spilled"], 16)
                mix(3, lambda: act.wait_ge(S["slab_mm"], n0 + 1))
                mix(4, lambda: act.wait_ge(S["slab_mm"], n0 + 2))
                act.wait_ge(S["spilled"], 48)
                for j, (name, row) in enumerate((("r", R_), ("k", K_), ("v", V_))):
                    def keep(i, s):
                        nc.scalar.copy(pairs(work)[:, i * 2 + (4 * j + s)], banks(2 * s)).then_inc(banks_free[s], 1)
                    if j == 1:
                        mix(5, lambda: act.wait_ge(S["slab_mm"], FIRST["k"]))
                    slabs(FIRST[name], 4, keep)
                    evacuated(FIRST[name] + 4)
                    act.dma_start(spill[row], work[:, 8 * j:8 * j + 8, :]).then_inc(S["spilled"], 16)
                act.dma_start(spread[0:16, :], spread_in).then_inc(S["spread_loaded"], 16)
                act.dma_start(restart, restart_in).then_inc(S["spread_loaded"], 16)
                act.wait_ge(S["spilled"], 96)
                with act.Fori(0, 4) as g:
                    duo_act(g)
                act.wait_ge(S["spilled"], 96 + 32 * 4)
                for n, row in enumerate((Y_, BON_, G_)):
                    act.dma_start(work[:, 8 * n:8 * n + 8, :], spill[row]).then_inc(S["gn_loaded"], 16)
                for m in range(NT):
                    act.wait_ge(S["gn_d"], m + 1)
                    if m >= 2:
                        act.wait_ge(S["gn_sum"], m - 1)
                    af(scratch[:, m % 2, :], work[:, m, :], ACT.Square).then_inc(S["gn_sq"], 1)
                act.wait_ge(S["gn_var"], 1)
                af(rows16b, rows16, ACT.Sqrt).then_inc(S["gn_root"], 1)
                for m in range(NT + 1):
                    if m < NT:
                        act.wait_ge(S["gn_scaled"], m + 1)
                        af(work[:, m, :], work[:, m, :], ACT.Identity, scale=vec("gn_g", m), bias=vec("gn_b", m)).then_inc(S["gn_affine"], 1)
                    if m:
                        act.wait_ge(S["gn_gated"], m)
                        nc.scalar.copy(act_hi[:, m - 1, :], work[:, m - 1, :]).then_inc(S["gn_hi"], 1)
                post_slabs("mixer0_post", FIRST["rwkv_o"])

            def duo_act(g):
                act.wait_ge(S["dve_free"], g + 1)
                for tile, row in ((IN_LW, LW_), (IN_A, A_), (IN_K, K_), (IN_R, R_), (IN_V, V_)):
                    act.dma_start(tile, pairs(spill[row])[:, g]).then_inc(S["duo_loaded"], 16)
                act.wait_ge(S["duo_vec"], g + 1)
                act.wait_ge(S["duo_loaded"], g * 80 + 80)
                for q in range(2):
                    nc.scalar.activation(scratch[:, q, :], IN_K[:, q, :], ACT.Square, scale=duo_vec[:, q:q + 1]).then_inc(S["kk_sq"], 1)
                for q in range(2):
                    af(TMP["kk"][q], IN_K[:, q, :], ACT.Copy, scale=duo_vec[:, q:q + 1])
                for q in range(2):
                    inst = af(TMP["k"][q], IN_A[:, q, :], ACT.Identity, scale=duo_vec[:, 2 + q:3 + q], bias=duo_vec[:, 6 + q:7 + q])
                inst.then_inc(S["act_prep"], 1)
                act.wait_ge(S["kk_max"], g + 1)
                af(rows16b_duo, rows16, ACT.Sqrt).then_inc(S["kk_root"], 1)
                act.wait_ge(S["dve_prep"], g * 2 + 1)
                for q in range(2):
                    run_sum = TMP["Y"][q].rearrange("p (n t) -> p n t", t=CH)
                    af(grown[q][:, :, 1:65], run_sum, ACT.Exp, scale=-DECAY)
                    inst = af(TMP["X"][q], TMP["Y"][q], ACT.Exp, scale=DECAY)
                inst.then_inc(S["act_prep"], 1)
                for n in range(NCH):
                    act.wait_ge(S["sa_mm"], g * NCH + (n + 1))
                    af(sa_sb, ps[:, 1, 0:128], ACT.Copy, scale=-1.0).then_inc(S["sa_out"], 1)
                    act.wait_ge(S["st_mm"], g * NCH + (n + 1))
                    af(state[:, (n + 1) % 2, 64:128], ps[:, 2, 64:128], ACT.Copy, scale=grown[1][:, n, 64:65]).then_inc(S["st_out1"], 1)
                    act.wait_ge(S["y_mm"], g * NCH + (n + 1))
                    nc.scalar.copy(y_sb[:, :, 64 * n:64 * n + 64], ps[:, 3 + n % 2, 0:128].rearrange("p (q t) -> p q t", q=2)).then_inc(S["y_out"], 1)
                act.wait_ge(S["y_out"], (g + 1) * NCH)
                act.dma_start(pairs(spill[Y_])[:, g], y_sb).then_inc(S["spilled"], 16)
                act.dma_start(pairs(spill[BON_])[:, g], bonus_sb).then_inc(S["spilled"], 16)

            act.wait_ge(S["consts_loaded"], 32)
            act.wait_ge(raw_loaded[0], 16)
            nc.scalar.copy(w_hi[:, 0, :], w_raw[:, 0, :]).then_inc(S["hi_made"], 1)
            act.wait_ge(S["x_loaded"], 16)
            for k in range(NT):
                af(act_hi[:, k, :], x[:, k, :], ACT.Copy, scale=vec(GAIN["first"], k)).then_inc(S["uhi_made"], 1)
            slabs(0, 12, head=lambda: norm_of_x("first"))
            evacuated(6)
            for j in range(8):
                if j >= 2:
                    act.wait_ge(S["qk_sum"], j - 1)
                else:
                    act.wait_ge(S["conv_done"], 1)
                af(scratch[:, j % 2, :], work[:, j, :], ACT.Square).then_inc(S["qk_sq"], 1)
            act.wait_ge(S["qk_mean"], 1)
            af(rows16b, rows16, ACT.Sqrt).then_inc(S["qk_root"], 1)
            act.wait_ge(S["conv_done"], 1)
            act.dma_start(spread[0:16, :], spread_in).then_inc(S["spread_loaded"], 16)
            attention(0, None)
            act.wait_ge(S["branch_made"], 1)

            def branch(i, s, dst):
                nc.scalar.copy(dst[:, 4 * s:4 * s + 4], ps[:, 4 * s:4 * s + 4, :]).then_inc(banks_free[s], 1)
            slabs(FIRST["attn_branch"], 2, lambda i, s: branch(i, s, ybuf[:, :, 0:T]))
            slabs(FIRST["conv_branch"], 2, lambda i, s: branch(i, s, work))

            def gates(i, s):
                act.wait_ge(banks_free[s], i + (FIRST["gates"] // 2 + 1))
                af(scratch[:, 0:2, :], scratch[:, 0:2, :], ACT.Sigmoid).then_inc(S["sig_made"], 1)
            slabs(FIRST["gates"], 8, gates)
            for k in range(NT):
                act.wait_ge(S["tile_made"], k + 1)
                nc.scalar.copy(act_hi[:, k, :], ybuf[:, k, 0:T]).then_inc(S["merged_hi"], 1)
            slabs(FIRST["w_o"], 4)
            pre("mlp", FIRST["mlp_in0"], x_after_slabs(FIRST["w_o"]))
            for cn in range(4):
                slabs(FIRST[f"mlp_in{cn}"], 4, head=(lambda: norm_of_x("mlp")) if cn == 0 else None)
                slabs(FIRST[f"mlp_out{cn}"], 4)
            ffn(0, FIRST["mlp_out3"], x_after_slabs(FIRST["mlp_out3"]))
            rwkv_act()
            ffn(1, FIRST["ffn1_in0"], x_after("mixer0_post"))
            pre("kv", FIRST["kv"], x_after("ffn1_post"))
            slabs(FIRST["kv"], 2, head=lambda: norm_of_x("kv"))
            ffn(2, FIRST["ffn2_in0"], lambda k: None)
            pre("mixer1_pre", FIRST["q2"], x_after("ffn2_post"))

            def q2_head():
                norm_of_x("mixer1_pre")
                act.dma_start(work[:, 18, :].rearrange("p (b k) -> p b k", b=2), swa_in).then_inc(S["swa_loaded"], 16)
            slabs(FIRST["q2"], 4, head=q2_head)
            act.wait_ge(S["vtok_mm"], 1)
            nc.scalar.copy(work[:, 16:18, :], ps[:, 4:6, :]).then_inc(S["vtok_out"], 1)
            attention(1, None)
            for k in range(NT):
                act.wait_ge(S["at_osb"], STEPS[0] + STEPS[1])
                nc.scalar.copy(act_hi[:, k, :], work[:, k, :]).then_inc(S["merged_hi"], 1)
            post_slabs("mixer1_post", FIRST["o2"])
            ffn(3, FIRST["ffn3_in0"], x_after("mixer1_post"))
            act.wait_ge(S["x_made"], NT * len(POST_NO))
            act.dma_start(x_out, x[:]).then_inc(S["out_stored"], 16)
            act.wait_ge(S["out_stored"], 16)

        @block.vector
        def _(dve):
            tt = nc.vector.tensor_tensor
            stt = nc.vector.scalar_tensor_tensor
            ts = nc.vector.tensor_scalar
            copy = nc.vector.tensor_copy

            def norm(name, factor=1.0):
                r = NORM[name]
                dve.wait_ge(S["sum_mm"], 4 * (r + 1))
                ts(small[:, 0:4], ps[:, 4, 0:4], EPS, None, ALU.add).then_inc(S["mean_made"], 1)
                dve.wait_ge(S["root_made"], r + 1)
                nc.vector.reciprocal(small[:, 8:12], small[:, 4:8])
                dve.drain()
                diagonal(factor).then_inc(S["diag_made"], 1)
                dve.wait_ge(S["rstd_mm"], r + 1)

            def diagonal(factor):
                for t in range(4):
                    inst = ts(scratch[:, 2, 128 * t:128 * t + 128], c("ident"), small[:, 8 + t:9 + t], factor, ALU.mult, ALU.mult)
                return inst

            def pre(name):
                for k in range(NT):
                    dve.wait_ge(S["uhi_made"], NT * SPLIT_NO[name] + k + 1)
                    stt(out=act_lo[:, k, :], in0=x[:, k, :], scalar=vec(GAIN[name], k), in1=act_hi[:, k, :].bitcast(F32),
                        op0=ALU.mult, op1=ALU.subtract).then_inc(S["ulo_made"], 1)
                norm(name)
                keep_rms()

            def keep_rms():
                copy(scratch[:, 3, :], ps[:, 5, :])
                dve.drain()

            def post(name, factor):
                norm(name, factor)
                for k in range(NT):
                    stt(out=work[:, k, :], in0=ybuf[:, k, 0:T], scalar=vec(GAIN[name], k), in1=ps[:, 5, :],
                        op0=ALU.mult, op1=ALU.mult).then_inc(S["t_scaled"], 1)

            rms2 = scratch[:, 3, :].unsqueeze(1).broadcast_to([P, 2, T])

            def slabs(first, count, body):
                with dve.Fori(0, count // 2) as i:
                    for s in range(2):
                        dve.wait_ge(S["slab_mm"], i * 2 + (first + s + 1))
                        body(i, s)

            def scaled(dst, s):
                return tt(dst, banks(2 * s), rms2, ALU.mult)

            def add_to(acc):
                def body(i, s):
                    a = pairs(acc)[:, i * 2 + s]
                    tt(a, banks(2 * s), a, ALU.add).then_inc(banks_free[s], 1)
                return body

            def ffn(f):
                pre(f"ffn{f}_pre")
                for cn, n in enumerate(FFN_CHUNKS):
                    first = FIRST[f"ffn{f}_in{cn}"]
                    g0 = 11 * f + sum(FFN_CHUNKS[:cn]) // 2
                    with dve.Fori(0, n // 2) as i:
                        dve.drain()
                        dve.wait_ge(S["slab_mm"], i * 2 + (first + 1))
                        scaled(work[:, 8:10, :], 0).then_inc(banks_free[0], 1)
                        dve.wait_ge(S["slab_mm"], i * 2 + (first + 2))
                        scaled(work[:, 10:12, :], 1).then_inc(banks_free[1], 1)
                        dve.drain()
                        dve.wait_ge(S["gate_made"], i + (g0 + 1))
                        tt(pairs(hid_hi)[:, i], work[:, 10:12, :], work[:, 8:10, :], ALU.mult)
                        tt(work[:, 10:12, :], work[:, 10:12, :], work[:, 8:10, :], ALU.mult)
                        dve.drain()
                        tt(pairs(hid_lo)[:, i], work[:, 10:12, :], pairs(hid_hi)[:, i].bitcast(F32), ALU.subtract).then_inc(S["hid_made"], 1)
                    first += n
                    if cn == 0:
                        slabs(first, 4, lambda i, s: copy(pairs(ybuf)[:, i * 2 + s], banks(2 * s)).then_inc(banks_free[s], 1))
                    else:
                        slabs(first, 4, add_to(ybuf))
                post(f"ffn{f}_post", 0.5)

            def attention(a, heads_bias):
                g0, steps = 16 * a, STEPS[a]
                for t in range(steps + 1):
                    if t < steps:
                        g, b = g0 + t, t % 2
                        dve.wait_ge(S["at_s"], g + 1)
                        if t >= 3:
                            dve.wait_ge(S["at_pt"], g - 2)
                        tt(p_buf[:, t % 3, :, :], ps[:, SCORE_BANKS[b]:SCORE_BANKS[b] + 2, 0:256], heads_bias(t), ALU.add)
                        dve.drain()
                        nc.vector.tensor_reduce(small[:, 20 + 2 * b:22 + 2 * b], p_buf[:, t % 3, :, :], AX_X, ALU.max)
                        dve.drain()
                        if a == 1:
                            tt(small[:, 20 + 2 * b:22 + 2 * b], small[:, 20 + 2 * b:22 + 2 * b], sinks[:, 2 * (t // 4):2 * (t // 4) + 2], ALU.max)
                            dve.drain()
                        ts(small[:, 12 + 2 * b:14 + 2 * b], small[:, 20 + 2 * b:22 + 2 * b], -1.0, None, ALU.mult).then_inc(S["at_max"], 1)
                    if t >= 1:
                        g, b = g0 + t - 1, (t - 1) % 2
                        dve.wait_ge(S["at_exp"], g + 1)
                        if a == 1:
                            tt(small[:, 16 + 2 * b:18 + 2 * b], small[:, 16 + 2 * b:18 + 2 * b], small[:, 24 + 2 * b:26 + 2 * b], ALU.add)
                            dve.drain()
                        nc.vector.reciprocal(small[:, 28 + 2 * b:30 + 2 * b], small[:, 16 + 2 * b:18 + 2 * b])
                        dve.drain()
                        for h in range(2):
                            inst = ts(p_buf[:, (t - 1) % 3, h, :], p_buf[:, (t - 1) % 3, h, :], small[:, 28 + 2 * b + h:29 + 2 * b + h], None, ALU.mult)
                        inst.then_inc(S["at_p"], 1)

            def rwkv_dve():
                dve.drain()
                ts(omu[:], vecs[:, VEC["mu0"]:VEC["mu0"] + 48], -1.0, 1.0, ALU.mult, ALU.add)
                ts(oma[:], vecs[:, VEC["k_a"]:VEC["k_a"] + 8], -1.0, 1.0, ALU.mult, ALU.add)
                norm("mixer0_pre")
                nc.vector.memset(ybuf[:, :, 0:1], 0.0)
                nc.vector.memset(work[64:128, 0, :], 0.0)
                nc.vector.memset(work[0:64, 1, :], 0.0)
                for k in range(NT):
                    stt(out=u_now(k), in0=x[:, k, :], scalar=vec(GAIN["mixer0_pre"], k), in1=ps[:, 5, :],
                        op0=ALU.mult, op1=ALU.mult).then_inc(S["u_made"], 1)
                dve.drain()
                for j in range(6):
                    hi, lo = (hid_hi, hid_lo) if j in (1, 4) else (act_hi, act_lo)
                    if j == 3:
                        dve.wait_ge(banks_free[0], FIRST["lora"] // 2 + 1)
                        copy(hid_hi[:, 0:3, :], work[:, 0:3, :])
                        dve.drain()
                        tt(hid_lo[:, 0:3, :], work[:, 0:3, :], hid_hi[:, 0:3, :].bitcast(F32), ALU.subtract).then_inc(S["lora_lo"], 1)
                    for k in range(NT + 1):
                        e = NT * j + k
                        if k < NT:
                            dve.wait_ge(S["t_made"], e + 1)
                            if e >= 2:
                                dve.wait_ge(S["mix_hi"], e - 1)
                                dve.wait_ge(S["mix_lo"], e - 1)
                            stt(out=scratch[:, 2 + k % 2, :], in0=ybuf[:, k, 0:T], scalar=vec(f"mu{MIX[j]}", k), in1=scratch[:, k % 2, :],
                                op0=ALU.mult, op1=ALU.add).then_inc(S["mix_made"], 1)
                        if k:
                            dve.wait_ge(S["mix_hi"], e)
                            dve.wait_ge(S["mix_made"], e)
                            tt(lo[:, k - 1, :], scratch[:, 2 + (k - 1) % 2, :], hi[:, k - 1, :].bitcast(F32), ALU.subtract).then_inc(S["mix_lo"], 1)
                for s in range(2):
                    dve.wait_ge(banks_free[s], FIRST["rwkv_o"] // 2)
                for q in range(2):
                    nc.vector.memset(grown[q][:, :, 0:1], 1.0)
                dve.wait_ge(S["spread_loaded"], 48)
                dve.wait_ge(S["spilled"], 96)
                nc.vector.memset(small[:, 30:31], 0.0).then_inc(S["dve_free"], 1)
                with dve.Fori(0, 4) as g:
                    duo_dve(g)
                for m in range(NT):
                    dve.wait_ge(S["gn_mean"], m + 1)
                    tt(work[:, m, :], work[:, m, :], ps[:, 4 + m % 2, :], ALU.subtract).then_inc(S["gn_d"], 1)
                dve.wait_ge(S["gn_sum"], NT)
                ts(rows16, ps[0:16, 6, :], 1 / 64, GN_EPS, ALU.mult, ALU.add).then_inc(S["gn_var"], 1)
                dve.wait_ge(S["gn_root"], 1)
                nc.vector.reciprocal(rows16, rows16b).then_inc(S["gn_recip"], 1)
                for m in range(NT + 1):
                    if m < NT:
                        dve.wait_ge(S["gn_bcast"], m + 1)
                        tt(work[:, m, :], work[:, m, :], ps[:, 4 + m % 2, :], ALU.mult).then_inc(S["gn_scaled"], 1)
                    if m:
                        w = work[:, m - 1, :]
                        dve.wait_ge(S["gn_affine"], m)
                        tt(w, w, work[:, 8 + m - 1, :], ALU.add)
                        dve.drain()
                        tt(w, w, work[:, 16 + m - 1, :], ALU.mult).then_inc(S["gn_gated"], 1)
                        dve.wait_ge(S["gn_hi"], m)
                        tt(act_lo[:, m - 1, :], w, act_hi[:, m - 1, :].bitcast(F32), ALU.subtract).then_inc(S["gn_lo"], 1)
                slabs(FIRST["rwkv_o"], 4, lambda i, s: copy(pairs(ybuf)[:, i * 2 + s], banks(2 * s)).then_inc(banks_free[s], 1))
                post("mixer0_post", 1.0)

            def chunks(tile):
                return tile.rearrange("p (n t) -> p n t", t=CH)

            def mask(name):
                return c(name).unsqueeze(1).broadcast_to([P, NCH, 64])

            def duo_dve(g):
                for n, tab in enumerate((vecs[:, VEC["k_k"]:VEC["k_k"] + 8], vecs[:, VEC["k_a"]:VEC["k_a"] + 8],
                                         vecs[:, VEC["r_k"]:VEC["r_k"] + 8], oma[:])):
                    inst = copy(duo_vec[:, 2 * n:2 * n + 2], tab.rearrange("p (a b) -> p a b", b=2)[:, g])
                inst.then_inc(S["duo_vec"], 1)
                dve.wait_ge(S["duo_loaded"], g * 80 + 80)
                for q in range(2):
                    inst = nc.vector.tensor_tensor_scan(TMP["Y"][q], restart, IN_LW[:, q, :], 0.0, ALU.mult, ALU.add)
                inst.then_inc(S["dve_prep"], 1)
                dve.wait_ge(S["kk_sum"], g + 1)
                ts(rows16, ps[0:16, 0, :], 1e-24, None, ALU.max).then_inc(S["kk_max"], 1)
                dve.wait_ge(S["act_prep"], g * 2 + 1)
                kb = work[:, 16:18, :]
                tt(kb, IN_K, kb, ALU.mult)
                dve.drain()
                for q in range(2):
                    stt(out=TMP["rk"][q], in0=IN_R[:, q, :], scalar=duo_vec[:, 4 + q:5 + q], in1=TMP["k"][q], op0=ALU.mult, op1=ALU.mult)
                dve.wait_ge(S["kk_root"], g + 1)
                nc.vector.reciprocal(rows16, rows16b_duo).then_inc(S["kk_recip"], 1)
                dve.drain()
                dve.wait_ge(S["act_prep"], g * 2 + 2)
                for q in range(2):
                    tt(chunks(TMP["R"][q]), chunks(IN_R[:, q, :]), grown[q][:, :, 1:65], ALU.mult)
                tt(kb, kb, work[:, 10:12, :], ALU.mult)
                for q in range(2):
                    dve.wait_ge(job_mm[q], g * len(JOBS) + 1)
                    tt(TMP["kk"][q], TMP["kk"][q], ps[:, 4 * q, :], ALU.mult).then_inc(job_out[q], 1)
                dve.drain()
                tt(work[:, 14:16, :], work[:, 12:14, :], IN_A, ALU.mult)
                for q in range(2):
                    tt(chunks(TMP["KK"][q]), chunks(TMP["kk"][q]), grown[q][:, :, 0:64], ALU.mult)
                dve.drain()
                tt(work[:, 14:16, :], work[:, 14:16, :], work[:, 10:12, :], ALU.mult).then_inc(S["dve_prep"], 1)
                dve.wait_ge(S["spilled"], g * 32 + 96)
                for j, (name, _, _, m) in enumerate(JOBS):
                    if j == 0:
                        continue
                    for q in range(2):
                        dve.wait_ge(job_mm[q], g * len(JOBS) + (j + 1))
                        p = ps[:, 4 * q + j % 4, :]
                        if name == "KabT":
                            tt(chunks(TMP["XT"][q]), chunks(p), mask("firstT"), ALU.mult)
                            inst = tt(chunks(TMP[name][q]), chunks(p), mask(m), ALU.mult)
                        elif name == "X":
                            tt(chunks(TMP["X"][q]), chunks(p), mask(m), ALU.mult)
                            dve.drain()
                            tt(chunks(TMP["X"][q]), chunks(TMP["X"][q]), mask("eye"), ALU.add)
                            inst = tt(chunks(TMP["XT"][q]), chunks(TMP["XT"][q]), mask("eye"), ALU.add)
                        elif name in ("X+", "XT+"):
                            dst = TMP[name[:-1]][q]
                            inst = tt(dst, p, dst, ALU.add)
                        elif name == "bonus":
                            inst = tt(bonus_sb[:, q, :], p, IN_V[:, q, :], ALU.mult)
                        elif m is None:
                            inst = copy(TMP[name][q], p)
                        else:
                            inst = tt(chunks(TMP[name][q]), chunks(p), mask(m), ALU.mult)
                        inst.then_inc(job_out[q], 1)
                nc.vector.memset(state[:, 0, 0:64], 0.0).then_inc(S["st_out"], 1)
                nc.vector.memset(state[:, 0, 64:128], 0.0).then_inc(S["st_out1"], 1)
                for n in range(NCH):
                    dve.wait_ge(S["rhs_mm"], g * NCH + (n + 1))
                    copy(rhs_sb, ps[:, 0, 0:128]).then_inc(S["rhs_out"], 1)
                    dve.wait_ge(S["st_mm"], g * NCH + (n + 1))
                    dve.wait_ge(S["st_out1"], g * (NCH + 1) + (n + 2))
                    ts(state[:, (n + 1) % 2, 0:64], ps[:, 2, 0:64], grown[0][:, n, 64:65], None, ALU.mult).then_inc(S["st_out"], 1)
                dve.wait_ge(S["y_mm"], (g + 1) * NCH)
                nc.vector.memset(small[:, 30:31], 0.0).then_inc(S["dve_free"], 1)

            for q in range(2):
                nc.vector.memset(ybuf[:, 4:8, q * (T + 1):q * (T + 1) + 1], 0.0)
            dve.wait_ge(S["consts_loaded"], 32)
            dve.wait_ge(S["bias_loaded"], 32)
            ts(gains8[:, 0:1], vec("q_norm_g"), 0.125, None, ALU.mult)
            na_bias = work[:, 12:24, :].rearrange("p k t -> p (k t)").rearrange("p (h k) -> p h k", h=8)
            na_mask = area[:, 24:26, :].rearrange("p k t -> p (k t)")[:, 0:768]
            pre("first")
            with dve.Fori(0, 3) as i:
                for s in range(2):
                    dve.wait_ge(S["slab_mm"], i * 2 + (s + 1))
                    scaled(pairs(work)[:, i * 2 + s], s).then_inc(banks_free[s], 1)
            for s in range(2):
                dve.wait_ge(S["slab_mm"], 7 + s)
                scaled(pairs(ybuf)[:, s], s).then_inc(banks_free[s], 1)
            for s in range(2):
                dve.wait_ge(S["slab_mm"], 9 + s)
                scaled(ybuf[:, 4 + 2 * s:6 + 2 * s, 1:T + 1], s).then_inc(banks_free[s], 1)
            tt(na_bias, na_bias, na_mask.unsqueeze(1).broadcast_to([P, 8, 768]), ALU.add)
            for s in range(2):
                dve.wait_ge(S["slab_mm"], 11 + s)
                z = ybuf[:, 4 + 2 * s:6 + 2 * s, 1:T + 1]
                scaled(scratch[:, 0:2, :], s).then_inc(banks_free[s], 1)
                dve.drain()
                tt(z, scratch[:, 0:2, :], z, ALU.mult)
                dve.drain()
            dve.drain()
            for j in range(4):
                z = ybuf[:, 4 + j, :]
                ts(area[:, 16 + j, :], z[:, 0:T], vec("conv_w", j), None, ALU.mult)
                dve.drain()
                for n in (1, 2):
                    stt(out=area[:, 16 + j, :], in0=z[:, n:n + T], scalar=vec("conv_w", 4 * n + j), in1=area[:, 16 + j, :],
                        op0=ALU.mult, op1=ALU.add)
                    dve.drain()
            dve.wait_ge(S["slab_mm"], 12)
            tt(area[:, 16:20, :], area[:, 16:20, :], ybuf[:, 0:4, 0:T], ALU.mult)
            dve.drain()
            copy(hid_hi[:, 4:8, :], area[:, 16:20, :])
            dve.drain()
            tt(hid_lo[:, 4:8, :], area[:, 16:20, :], hid_hi[:, 4:8, :].bitcast(F32), ALU.subtract).then_inc(S["conv_done"], 1)
            dve.wait_ge(S["qk_sum"], 8)
            ts(rows16, ps[0:16, 4, :], 1 / 64, EPS, ALU.mult, ALU.add).then_inc(S["qk_mean"], 1)
            dve.wait_ge(S["qk_root"], 1)
            nc.vector.reciprocal(rows16, rows16b).then_inc(S["qk_recip"], 1)
            for j in range(8):
                dve.wait_ge(S["qk_bcast"], j + 1)
                if j < 4:
                    tt(scratch[:, j % 2, :].rearrange("p (j r c) -> p j r c", j=4, r=8),
                       work[:, j, :].rearrange("p (r j c) -> p j r c", j=4, r=8),
                       ps[:, 6 + j % 2, :].rearrange("p (r j c) -> p j r c", j=4, r=8), ALU.mult)
                    dve.drain()
                    inst = ts(work[:, j, :], scratch[:, j % 2, :], gains8[:, 0:1], None, ALU.mult)
                else:
                    inst = stt(out=work[:, j, :], in0=work[:, j, :], scalar=vec("k_norm_g"), in1=ps[:, 6 + j % 2, :],
                               op0=ALU.mult, op1=ALU.mult)
                inst.then_inc(S["qk_done"], 1)

            def bias_of(t):
                tile, j = divmod(t, 4)
                return na_bias[:, 2 * tile:2 * tile + 2, 256 * NA_CLASS[j]:256 * NA_CLASS[j] + 256]
            attention(0, bias_of)
            dve.wait_ge(S["at_osb"], STEPS[0])
            for j in range(4):
                o = work[:, j, :].rearrange("p (j r c) -> p r j c", j=4, r=8)
                copy(hid_hi[:, j, :].rearrange("p (r j c) -> p r j c", j=4, r=8), o)
            dve.drain()
            for j in range(4):
                o = work[:, j, :].rearrange("p (j r c) -> p r j c", j=4, r=8)
                inst = tt(hid_lo[:, j, :].rearrange("p (r j c) -> p r j c", j=4, r=8), o,
                          hid_hi[:, j, :].rearrange("p (r j c) -> p r j c", j=4, r=8).bitcast(F32), ALU.subtract)
            inst.then_inc(S["branch_made"], 1)
            n0 = FIRST["gates"]

            diagonal(1.0).then_inc(S["gdiag_made"], 1)
            dve.wait_ge(S["grstd_mm"], 1)
            keep_rms()
            for n, acc in enumerate((ybuf, work)):
                with dve.Fori(0, 2) as i:
                    for s in range(2):
                        dve.drain()
                        dve.wait_ge(S["slab_mm"], i * 2 + (n0 + 4 * n + s + 1))
                        scaled(scratch[:, 0:2, :], s).then_inc(banks_free[s], 1)
                        dve.wait_ge(S["sig_made"], i * 2 + (4 * n + s + 1))
                        a = pairs(acc)[:, i * 2 + s]
                        tt(a, scratch[:, 0:2, :], a, ALU.mult)
            dve.drain()
            for k in range(NT):
                tt(ybuf[:, k, 0:T], ybuf[:, k, 0:T], work[:, k, :], ALU.add).then_inc(S["tile_made"], 1)
            for k in range(NT):
                dve.wait_ge(S["merged_hi"], k + 1)
                inst = tt(act_lo[:, k, :], ybuf[:, k, 0:T], act_hi[:, k, :].bitcast(F32), ALU.subtract)
            inst.then_inc(S["merged_made"], 1)
            slabs(FIRST["w_o"], 4, add_to(x))
            pre("mlp")
            for cn in range(4):
                def relu2(i, s):
                    scaled(work[:, 8:10, :], s).then_inc(banks_free[s], 1)
                    dve.drain()
                    for out in (pairs(hid_hi)[:, i * 2 + s], work[:, 10:12, :]):
                        stt(out=out, in0=work[:, 8:10, :], scalar=0.0, in1=work[:, 8:10, :], op0=ALU.max, op1=ALU.mult)
                    dve.drain()
                    tt(pairs(hid_lo)[:, i * 2 + s], work[:, 10:12, :], pairs(hid_hi)[:, i * 2 + s].bitcast(F32),
                       ALU.subtract).then_inc(S["hid_made"], 1)
                    dve.drain()
                slabs(FIRST[f"mlp_in{cn}"], 4, relu2)
                slabs(FIRST[f"mlp_out{cn}"], 4, add_to(x))
            ffn(0)
            rwkv_dve()
            ffn(1)
            pre("kv")

            def biased(dst, b, s):
                scaled(dst, s)
                dve.drain()
                return tt(dst, dst, b.unsqueeze(2).broadcast_to([P, 2, T]), ALU.add)
            for s in range(2):
                dve.wait_ge(S["slab_mm"], FIRST["kv"] + s + 1)
                at = VEC["b_kv"] + 2 * s
                biased(work[:, 20 + 2 * s:22 + 2 * s, :], vecs[:, at:at + 2], s).then_inc(banks_free[s], 1)
            ffn(2)
            pre("mixer1_pre")
            with dve.Fori(0, 2) as i:
                for s in range(2):
                    dve.wait_ge(S["slab_mm"], i * 2 + (FIRST["q2"] + s + 1))
                    q = pairs(work)[:, i * 2 + s]
                    biased(q, vecs[:, VEC["b_q"]:VEC["b_q"] + 8].rearrange("p (a b) -> p a b", b=2)[:, i * 2 + s], s)
                    dve.drain()
                    ts(q, q, 0.125, None, ALU.mult).then_inc(banks_free[s], 1)
            dve.wait_ge(S["swa_loaded"], 16)
            swa_mask = work[:, 18, :].rearrange("p (b k) -> p b k", b=2)
            attention(1, lambda t: swa_mask[:, min(t % 4, 1), :].unsqueeze(1).broadcast_to([P, 2, 256]))
            for k in range(NT):
                dve.wait_ge(S["merged_hi"], NT + k + 1)
                inst = tt(act_lo[:, k, :], work[:, k, :], act_hi[:, k, :].bitcast(F32), ALU.subtract)
            inst.then_inc(S["branch_made"], 1)
            with dve.Fori(0, 2) as i:
                for s in range(2):
                    dve.wait_ge(S["slab_mm"], i * 2 + (FIRST["o2"] + s + 1))
                    b = vecs[:, VEC["b_o"]:VEC["b_o"] + 8].rearrange("p (a b) -> p a b", b=2)[:, i * 2 + s]
                    tt(pairs(ybuf)[:, i * 2 + s], banks(2 * s), b.unsqueeze(2).broadcast_to([P, 2, T]), ALU.add).then_inc(banks_free[s], 1)
            post("mixer1_post", 1.0)
            ffn(3)


def stream_of(a):
    out = np.zeros((SLABS, P, SLAB), np.float32)

    def put(name, w, width=256, tiles=None):
        kt = w.shape[0] // P
        v = w.reshape(kt, P, w.shape[1] // width, width).transpose(2, 1, 0, 3)
        n = FIRST[name]
        out[n:n + v.shape[0], :, 0:kt * width] = v.reshape(v.shape[0], P, kt * width)

    w_in = a["w_in"][0]
    put("qkvconv", w_in[:, 0:3072])
    put("gates", w_in[:, 3072:5120])
    put("attn_branch", a["w_attn_branch"][0], 512)
    put("conv_branch", a["w_conv_branch"][0], 512)
    put("w_o", a["w_o"][0])
    for cn in range(4):
        put(f"mlp_in{cn}", a["w_mlp_in"][0][:, 1024 * cn:1024 * cn + 1024])
        put(f"mlp_out{cn}", a["w_mlp_out"][0][1024 * cn:1024 * cn + 1024])
    for f in range(4):
        wi, wo = a["ffn_w_in_2"][f // 2, f % 2], a["ffn_w_out_2"][f // 2, f % 2]
        t0 = 0
        for cn, n in enumerate(FFN_CHUNKS):
            g = wi[:, P * t0:P * (t0 + n)].reshape(D, n // 2, 256)
            u = wi[:, 2816 + P * t0:2816 + P * (t0 + n)].reshape(D, n // 2, 256)
            put(f"ffn{f}_in{cn}", np.stack([g, u], 2).reshape(D, n * 256))
            put(f"ffn{f}_out{cn}", wo[P * t0:P * (t0 + n)])
            t0 += n
    put("lora", np.concatenate([a["rwkv_w1_2"][0], a["rwkv_a1_2"][0], a["rwkv_g1_2"][0]], 1))
    n = FIRST["lora"] + 1
    out[n, 0:64, 0:1024], out[n, 64:128, 0:1024] = a["rwkv_w2_2"][0], a["rwkv_a2_2"][0]
    out[n, :, 1024:2048] = a["rwkv_g2_2"][0]
    for name, j in (("r", 0), ("k", 1), ("v", 2)):
        put(name, a["rwkv_w_rkv_2"][0, j])
    put("rwkv_o", a["rwkv_w_o_2"][0])
    put("kv", a["w_kv_2"])
    put("q2", a["attn_w_q_2"][0].reshape(D, 16, 64)[:, HEADS].reshape(D, D))
    put("o2", a["attn_w_o_2"][0].reshape(16, 64, D)[HEADS].reshape(D, D))
    return out


HEADS = [8 * (n // 8) + 4 * (n % 2) + (n % 8) // 2 for n in range(16)]


def vectors_of(a):
    rows = {"norm1_g": a["norm1_g"], "norm2_g": a["norm2_g"], "kv_norm_g": a["kv_norm_g_2"], "b_kv": a["b_kv_2"],
            "w0": a["rwkv_w0_2"], "a0": a["rwkv_a0_2"], "k_k": a["rwkv_k_k_2"], "k_a": a["rwkv_k_a_2"],
            "r_k": a["rwkv_r_k_2"], "gn_g": a["rwkv_gn_g_2"], "gn_b": a["rwkv_gn_b_2"], "b_o": a["attn_b_o_2"],
            "b_q": a["attn_b_q_2"].reshape(16, 64)[HEADS], "conv_w": a["conv_w"],
            "q_norm_g": np.concatenate([a["q_norm_g"]] * 2), "k_norm_g": np.concatenate([a["k_norm_g"]] * 2)}
    for i in range(12):
        rows[f"norm_g{i}"] = a["norm_g_2"][i // 6, i % 6]
    for i in range(6):
        rows[f"mu{i}"] = a["rwkv_mu_2"][0, i]
    return np.ascontiguousarray(np.concatenate([np.reshape(rows[n], (-1, P)) for n in VEC]).T)


def kernel(**inputs):
    import concourse.bacc as bacc
    from concourse.bass_utils import run_bass_kernel_spmd as run

    a = {k: np.asarray(v) for k, v in inputs.items()}
    mask, rel_r, rel_c = na_tables()
    rpb = a["rpb"][0]
    bias = np.stack([rpb[:, rel_r, rel_c[:, n, :]] for n in range(3)], 2).transpose(1, 0, 2, 3)
    consts = constants()
    consts[:, NCST - 16:] = a["attn_sinks_2"][0][HEADS][None, :]
    arrays = {
        "x_in": np.ascontiguousarray(a["x"][0].T.reshape(NT, P, T).transpose(1, 0, 2)),
        "stream": stream_of(a), "vec_in": vectors_of(a), "cst_in": consts, "spread_in": spread_rows(),
        "restart_in": scan_restart(), "bias_in": np.ascontiguousarray(bias.reshape(P, 12, T)), "mask_in": mask.reshape(P, 768),
        "swa_in": swa_masks(),
    }
    nc = bacc.Bacc("TRN2", target_bir_lowering=False, num_devices=1)
    aps = {n: nc.dram_tensor(n, v.shape, mybir.dt.from_np(v.dtype), kind="ExternalInput").ap() for n, v in arrays.items()}
    x_out = nc.dram_tensor("x_out", (P, NT, T), F32, kind="ExternalOutput").ap()
    build(nc, x_out=x_out, **aps)
    r = run(nc, [arrays], core_ids=[0])
    out = r.results[0]["x_out"]
    return np.ascontiguousarray(out.transpose(1, 0, 2).reshape(D, T).T)[None]
```

```python
from contextlib import ExitStack

import numpy as np
from concourse import mybir
from concourse.alu_op_type import AluOpType as ALU

F32 = mybir.dt.float32
F32R = mybir.dt.float32r
ACT = mybir.ActivationFunctionType
AX_X = mybir.AxisListType.X

P = 128
T = 512
D = 1024
NT = D // P
SLAB = 2048
EPS = 1e-6
GN_EPS = 64e-5
DECAY = float(np.exp(-0.5))
CH = 64
NCH = T // CH
FFN_TILES = 22
FFN_CHUNKS = (8, 8, 6)
MASKED = -1e30

_PARTS = [("convqkv", 12), ("conv_branch", 2), ("attn_branch", 2), ("gates", 8), ("w_o", 4)]
for _c in range(4):
    _PARTS += [(f"mlp_in{_c}", 4), (f"mlp_out{_c}", 4)]


def _ffn_parts(f):
    out = []
    for c, n in enumerate(FFN_CHUNKS):
        out += [(f"ffn{f}_in{c}", n), (f"ffn{f}_out{c}", 4)]
    return out


_PARTS += _ffn_parts(0) + [("lora", 2), ("r", 4), ("k", 4), ("v", 4), ("rwkv_o", 4)] + _ffn_parts(1)
_PARTS += [("kv", 2)] + _ffn_parts(2) + [("q2", 4), ("o2", 4)] + _ffn_parts(3)
FIRST = {}
_n = 0
for _name, _k in _PARTS:
    FIRST[_name] = _n
    _n += _k
SLABS = _n

VEC = {}
_v = 0
for _name, _k in ([("norm1_g", 8), ("norm2_g", 8)] + [(f"norm_g{i}", 8) for i in range(12)]
                  + [(f"mu{i}", 8) for i in range(6)]
                  + [(n, 8) for n in ("w0", "a0", "k_k", "k_a", "r_k", "gn_g", "gn_b", "kv_norm_g", "b_q", "b_o")]
                  + [("b_kv", 4), ("q_norm_g", 1), ("k_norm_g", 1), ("conv_w", 12)]):
    VEC[_name] = _v
    _v += _k
NVEC = _v

CST = {}
_c0 = 0
for _name, _k in [("ident", 128), ("ones", 128), ("blk64", 128), ("blk1", 128), ("sel", 128), ("mean", 1),
                  ("strict", 64), ("incl", 64), ("eye", 64), ("firstT", 64),
                  ("lev0", 64), ("lev1", 64), ("lev2", 64), ("lev3", 64), ("lev4", 64), ("sinks", 16)]:
    CST[_name] = _c0
    _c0 += _k
NCST = _c0


def constants():
    c = np.zeros((P, NCST), np.float32)
    i = np.arange(P)
    c[:, CST["ident"]:CST["ident"] + 128] = np.eye(P)
    c[:, CST["ones"]:CST["ones"] + 128] = 1
    blk = (i[:, None] // 64 == i[None, :] // 64)
    c[:, CST["blk64"]:CST["blk64"] + 128] = blk / 64
    c[:, CST["blk1"]:CST["blk1"] + 128] = blk
    for j in range(8):
        c[i, CST["sel"] + 16 * j + 2 * j + i // 64] = 1
    c[:, CST["mean"]] = 1 / D
    r, k = (i % 64)[:, None], np.arange(64)[None, :]
    c[:, CST["strict"]:CST["strict"] + 64] = r < k
    c[:, CST["incl"]:CST["incl"] + 64] = r <= k
    c[:, CST["eye"]:CST["eye"] + 64] = r == k
    c[:, CST["firstT"]:CST["firstT"] + 64] = -((k % 2 == 1) & (r == k - 1)).astype(np.float32)
    for n, s in enumerate((2, 4, 8, 16, 32)):
        c[:, CST[f"lev{n}"]:CST[f"lev{n}"] + 64] = -(((r // s) % 2 == 1) & (k // s == r // s - 1)).astype(np.float32)
    return c


def spread_rows():
    return (np.arange(16)[:, None] == np.arange(1024)[None, :] // 64).astype(np.float32)


def scan_restart():
    return np.broadcast_to((np.arange(T) % CH != 0).astype(np.float32), (P, T)).copy()


NA_CLASS = (0, 1, 1, 2)
NA_KEY0 = (0, 8, 24, 32)


def na_tables():
    r, cc = np.divmod(np.arange(P), 16)
    kr, kc = np.divmod(np.arange(256), 32)
    mask = np.zeros((P, 3, 256), np.float32)
    rel_r = kr[None, :] - r[:, None] + 7
    rel_c = np.zeros((P, 3, 256), np.int64)
    for n, j in enumerate((0, 1, 3)):
        q = 16 * j + cc
        key = NA_KEY0[j] + kc
        start = np.clip(q - 8, 0, 48)
        ok = (key[None, :] >= start[:, None]) & (key[None, :] < start[:, None] + 16)
        mask[:, n, :] = np.where(ok, 0, MASKED)
        rel_c[:, n, :] = np.clip(key[None, :] - q[:, None] + 15, 0, 30)
    return mask, rel_r, rel_c


def swa_masks():
    q, s = np.arange(P)[:, None], np.arange(256)[None, :]
    ok = (s - 128 <= q) & (s > q)
    return np.stack([np.where(ok & (s >= 128), 0, MASKED), np.where(ok, 0, MASKED)], 1).astype(np.float32)


def build(nc, x_in, stream, vec_in, cst_in, spread_in, restart_in, bias_in, mask_in, swa_in,
          x_out):
    ctx = ExitStack()
    with ctx:
        def sb(name, shape, dt=F32):
            return ctx.enter_context(nc.sbuf_tensor(name, shape, dt))

        def sem(name):
            return ctx.enter_context(nc.semaphore(name))

        w_raw = sb("w_raw", [P, 2, SLAB])
        w_hi = sb("w_hi", [P, 2, SLAB], F32R)
        w_lo = sb("w_lo", [P, 2, SLAB], F32R)
        x = sb("x_res", [P, NT, T])
        ybuf = sb("ybuf", [P, NT, T + 2])
        work = sb("work", [P, 24, T])
        scratch = sb("scratch", [P, 4, T])
        vecs = sb("vecs", [P, NVEC])
        cst = sb("cst", [P, NCST])
        gains8 = sb("gains8", [P, 1])
        b_q8 = sb("b_q8", [P, 8])
        omu = sb("omu", [P, 48])
        oma = sb("oma", [P, 8])
        small = sb("small", [P, 32])
        area = sb("area", [P, 32, T])
        base = nc.sbuf_base - 32 * T * 4
        act_hi = nc.alloc_sbuf_tensor_at("act_hi", [P, NT, T], F32R, offset=base)
        act_lo = nc.alloc_sbuf_tensor_at("act_lo", [P, NT, T], F32R, offset=base + 8 * T * 4)
        hid_hi = nc.alloc_sbuf_tensor_at("hid_hi", [P, NT, T], F32R, offset=base + 16 * T * 4)
        hid_lo = nc.alloc_sbuf_tensor_at("hid_lo", [P, NT, T], F32R, offset=base + 24 * T * 4)
        ps = ctx.enter_context(nc.psum_tensor("ps", [P, 8, 512], F32))
        spill = nc.dram_tensor("spill", [8, P, NT, T], F32).ap()
        R_, K_, V_, LW_, A_, G_, Y_, BON_ = range(8)

        S = {n: sem(n) for n in (
            "vecs_loaded", "consts_loaded", "x_loaded", "x2_loaded", "bias_loaded", "spread_loaded", "swa_loaded", "out_stored",
            "raw0_loaded", "raw1_loaded", "hi_made", "lo_made", "slab_mm", "banks0_free", "banks1_free",
            "sq_made", "sq_added", "sum_mm", "mean_made", "root_made", "diag_made", "rstd_mm", "gdiag_made", "grstd_mm",
            "u_made", "uhi_made", "ulo_made", "uhi2_made", "ulo2_made", "t_scaled", "x_made",
            "gate_made", "hid_made", "sig_made", "tile_made", "merged_hi", "merged_made", "branch_made", "conv_done",
            "qk_sq", "qk_sum", "qk_mean", "qk_root", "qk_recip", "qk_bcast", "qk_done",
            "at_s", "at_max", "at_exp", "at_p", "at_pt", "at_ptsb", "at_vblk", "at_vt", "at_vtok", "at_o", "at_osb", "vtok_mm", "vtok_out",
            "t_made", "mix_made", "mix_hi", "mix_lo", "lora_mm", "lora_lo", "lora_out", "lora_g_out", "spilled",
            "duo_loaded", "v_loaded", "duo_vec", "kk_sq", "kk_sum", "kk_max", "kk_root", "kk_recip", "kk_spread", "act_prep", "dve_prep",
            "dve_free",
            "job0_mm", "job1_mm", "job0_out", "job1_out", "rhs_mm", "rhs_out", "sa_mm", "sa_out", "st_mm", "st_out", "y_mm", "y_out",
            "pe_waited",
            "gn_loaded", "gn_mean", "gn_d", "gn_sq", "gn_sum", "gn_var", "gn_root", "gn_recip", "gn_bcast", "gn_scaled", "gn_affine",
            "gn_gated", "gn_hi", "gn_lo",
        )}
        raw_loaded = (S["raw0_loaded"], S["raw1_loaded"])
        banks_free = (S["banks0_free"], S["banks1_free"])

        def c(name, a=0, n=None, p0=0, p1=P):
            n = n if n is not None else {"ident": 128, "ones": 128, "blk64": 128, "blk1": 128, "sel": 16}.get(name, 64)
            return cst[p0:p1, CST[name] + a:CST[name] + a + n]

        def vec(name, k=0):
            return vecs[:, VEC[name] + k:VEC[name] + k + 1]

        def pairs(t):
            return t[:, :, 0:T].rearrange("p (a b) t -> p a b t", b=2)

        def banks(a, n=2):
            return ps[:, a:a + n, :]

        yflat = ybuf[:].rearrange("p k t -> p (k t)")
        def qk_squares(j):
            return area[:, (16 if j < 4 else 20) + j, :]
        spread, rows16, restart = yflat[:, 0:1024], yflat[0:16, 1024:1536], yflat[:, 1536:2048]
        rows16b = scratch[0:16, 2, :]
        MIX = (1, 4, 5, 0, 2, 3)

        def u_now(k):
            return ybuf[:, k, 1:T + 1]

        sinks = cst[:, NCST - 16:NCST]
        p_buf = yflat[:, 1536:3072].rearrange("p (b h k) -> p b h k", b=3, h=2)
        pt_buf = yflat[:, 3072:4096].rearrange("p (b h a k) -> p b h a k", b=2, h=2, a=2)
        vb_buf = scratch[:, 2, :].rearrange("p (b k) -> p b k", b=2)
        vt_buf = scratch[:, 3, :].rearrange("p (b a k) -> p b a k", b=2, a=2)

        NORMS = ["first", "mlp"]
        for f in range(4):
            NORMS += [f"ffn{f}_post"] if f == 2 else [f"ffn{f}_pre", f"ffn{f}_post"]
            if f == 0:
                NORMS += ["mixer0_pre", "mixer0_post"]
            if f == 1:
                NORMS += ["kv"]
            if f == 2:
                NORMS += ["mixer1_pre", "mixer1_post"]
        NORM = {n: i for i, n in enumerate(NORMS)}
        PRE = [n for n in NORMS if not n.endswith("post")]
        SPLIT_NO = {n: i for i, n in enumerate(n for n in PRE if n != "mixer0_pre")}
        POST_NO = {n: i for i, n in enumerate([n for n in NORMS if n.endswith("post")])}

        PRE_AFTER = {"mixer0_post": "ffn1_pre", "ffn1_post": "kv", "ffn2_post": "mixer1_pre", "mixer1_post": "ffn3_pre"}
        SPLIT_BY_POST = set(PRE_AFTER.values())

        def squares(name):
            return work[:, 0:8, :] if name == "first" else work[:, 12:20, :]

        AFTER_POST = {"ffn0_post": "lora", "mixer0_post": "ffn1_in0", "ffn1_post": "kv", "ffn2_post": "q2",
                      "mixer1_post": "ffn3_in0"}
        GAIN = {"first": "norm1_g", "mlp": "norm2_g", "kv": "kv_norm_g",
                "ffn0_pre": "norm_g0", "ffn0_post": "norm_g1", "mixer0_pre": "norm_g2", "mixer0_post": "norm_g3",
                "ffn1_pre": "norm_g4", "ffn1_post": "norm_g5", "ffn2_pre": "norm_g6", "ffn2_post": "norm_g7",
                "mixer1_pre": "norm_g8", "mixer1_post": "norm_g9", "ffn3_pre": "norm_g10", "ffn3_post": "norm_g11"}

        PAIR_STEPS = {}
        made = 0
        for cn in range(4):
            PAIR_STEPS[f"mlp{cn}"] = made
            made += 4
        for f in range(4):
            for cn, n in enumerate(FFN_CHUNKS):
                PAIR_STEPS[f"ffn{f}_{cn}"] = made
                made += n // 2
        SCORE_BANKS = (6, 0)
        TURN_BANKS = (4, 2)
        DUOS = NT // 2
        SPILLED = 16 * (5 + 4)
        STEPS = (16, 32)

        IN_R, IN_K, IN_V, IN_LW, IN_A = (work[:, 2 * n:2 * n + 2, :] for n in range(5))
        TMP = {}
        for n, name in enumerate(("X", "kk", "b", "k", "rk", "Y")):
            TMP[name] = [work[:, 10 + 2 * n + q, :] for q in range(2)]
        for n, name in enumerate(("R", "KK", "KabT", "KakT", "RkT", "RbT", "XT", "kT", "bT", "vT")):
            TMP[name] = [area[:, 2 * n + q, :] for q in range(2)]
        TMP["v"] = [work[:, 4 + q, :] for q in range(2)]
        v_tiles = area[:, 24:32, :]
        y_sb, bonus_sb = work[:, 22:24, :], scratch[:, 2:4, :]
        aflat = area[:].rearrange("p k t -> p (k t)")
        at0 = 20 * T
        grown = [aflat[:, at0 + 520 * q:at0 + 520 * q + 520].rearrange("p (n t) -> p n t", t=65) for q in range(2)]
        state = aflat[:, at0 + 1056:at0 + 1056 + 256].rearrange("p (b k) -> p b k", b=2)
        rhs_sb = aflat[:, at0 + 1312:at0 + 1440]
        sa_sb = aflat[:, at0 + 1440:at0 + 1568]
        old_sb = aflat[:, at0 + 1568:at0 + 1696]
        duo_vec = small[:, 12:20]
        JOBS = [("kT", "k", None, None), ("vT", "v", None, None), ("RkT", "k", "R", "incl"), ("bonus", None, None, None),
                ("KabT", "b", "KK", "strict"), ("KakT", "k", "KK", "strict"), ("X", "XT", None, None)]
        late = [("RbT", "b", "R", "incl"), ("bT", "b", None, None)]
        for level in range(5):
            JOBS.append(("Y", "KabT", "X", f"lev{level}"))
            if late:
                JOBS.append(late.pop(0))
            JOBS.append(("XT+", "Y", "XT", None))
            if level < 4:
                JOBS.append(("X", "XT", None, None))
        at_job = {}
        JOB_NEEDS = []
        for j, (name, lhs, rhs, _) in enumerate(JOBS):
            needs = [at_job[w] for w in (lhs, rhs) if w in at_job]
            if j >= 4:
                needs.append(j - 4)
            JOB_NEEDS.append([max(needs)] if needs else [])
            at_job[{"XT+": "XT"}.get(name, name)] = j
            if name == "KabT":
                at_job["XT"] = j
        job_mm, job_out = (S["job0_mm"], S["job1_mm"]), (S["job0_out"], S["job1_out"])

        def na_q(t, h):
            return work[64 * h:64 * h + 64, t // 4, 128 * (t % 4):128 * (t % 4) + 128]

        def na_k(t, h):
            k = work[64 * h:64 * h + 64, 4 + t // 4, :].rearrange("p (r c) -> p r c", c=64)
            return [k[:, :, NA_KEY0[t % 4]:NA_KEY0[t % 4] + 32]]

        def swa_q(t, h):
            return work[64 * h:64 * h + 64, t // 4, 128 * (t % 4):128 * (t % 4) + 128]

        def swa_k(t, h):
            b = t % 4
            return [work[64 * h:64 * h + 64, 20 + t // 16, 128 * n:128 * n + 128] for n in (max(b - 1, 0), b)]

        def swa_v(t, h, part):
            b = t % 4
            n = b if part else max(b - 1, 0)
            return work[:, 16 + n // 2, 256 * (n % 2) + 128 * (t // 16) + 64 * h:256 * (n % 2) + 128 * (t // 16) + 64 * h + 64]

        block = ctx.enter_context(nc.Block())

        @block.sync
        def _(sp):
            sp.dma_start(vecs[:], vec_in).then_inc(S["vecs_loaded"], 16)
            sp.dma_start(w_raw[:, 0, :], stream[0]).then_inc(raw_loaded[0], 16)
            sp.dma_start(x[:, 0:4, :], x_in[:, 0:4, :]).then_inc(S["x_loaded"], 16)
            sp.dma_start(x[:, 4:8, :], x_in[:, 4:8, :]).then_inc(S["x2_loaded"], 16)
            sp.dma_start(w_raw[:, 1, :], stream[1]).then_inc(raw_loaded[1], 16)
            sp.dma_start(cst[:], cst_in).then_inc(S["consts_loaded"], 16)
            sp.dma_start(work[:, 12:24, :], bias_in).then_inc(S["bias_loaded"], 16)
            sp.dma_start(area[:, 24:26, :].rearrange("p k t -> p (k t)")[:, 0:768], mask_in).then_inc(S["bias_loaded"], 16)
            with sp.Fori(1, SLABS // 2) as i:
                for s in range(2):
                    sp.wait_ge(S["lo_made"], i * 2 + (s - 1))
                    sp.dma_start(w_raw[:, s, :], stream[i * 2 + s]).then_inc(raw_loaded[s], 16)

        @block.gpsimd
        def _(pool):
            tt = nc.gpsimd.tensor_tensor

            def lo(n, s):
                pool.wait_ge(S["hi_made"], n + 1)
                tt(w_lo[:, s, :], w_raw[:, s, :], w_hi[:, s, :].bitcast(F32), ALU.subtract).then_inc(S["lo_made"], 1)

            def split(first, end):
                with pool.Fori(0, (end - first) // 2) as i:
                    lo(i * 2 + first, 1)
                    lo(i * 2 + (first + 1), 0)

            lo(0, 0)
            done = 1
            for name, n in POST_NO.items():
                end = FIRST[AFTER_POST[name]] + 1 if name in AFTER_POST else SLABS - 1
                split(done, end)
                done = end
                if name not in AFTER_POST:
                    lo(end, 1)
                for k in range(NT):
                    pool.wait_ge(S["t_scaled"], NT * n + k + 1)
                    tt(x[:, k, :], x[:, k, :], work[:, k, :], ALU.add).then_inc(S["x_made"], 1)

        @block.tensor
        def _(pe):
            mm = nc.tensor.matmul

            def slab_start(first, i, s):
                pe.wait_ge(S["lo_made"], i * 2 + (first + s + 1))
                if first or not isinstance(i, int):
                    pe.wait_ge(banks_free[s], i + first // 2)

            def slab(first, i, s, hi, lo, kt=8, middle=None):
                slab_start(first, i, s)
                for m in range(2):
                    for k in range(kt):
                        inst = product(s, m, k, hi, lo, k == kt - 1)
                    if m == 0 and middle is not None:
                        middle()
                inst.then_inc(S["slab_mm"], 1)

            def product(s, m, k, hi, lo, end):
                a = k * 256 + m * 128
                wh, wl = w_hi[:, s, a:a + 128], w_lo[:, s, a:a + 128]
                out = ps[:, 2 * s + m, :]
                mm(out, wh, hi[:, k, :], start=(k == 0), stop=False)
                mm(out, wh, lo[:, k, :], start=False, stop=False)
                return mm(out, wl, hi[:, k, :], start=False, stop=end)

            def slabs(first, count, hi, lo, kt=8, begin=0):
                with pe.Fori(begin, count // 2) as i:
                    for s in range(2):
                        slab(first, i, s, hi, lo, kt=kt)

            def eager_slab(first, hi, lo, kt, wait_tile):
                slab_start(first, 0, 0)
                for k in range(kt):
                    wait_tile(k)
                    for m in range(2):
                        inst = product(0, m, k, hi, lo, k == kt - 1)
                inst.then_inc(S["slab_mm"], 1)

            def out_slabs(key, first, kt):
                eager_out(key, first, kt)
                slab(first, 0, 1, hid_hi, hid_lo, kt=kt)
                slabs(first, 4, hid_hi, hid_lo, kt=kt, begin=1)

            def eager_out(key, first, kt):
                def pair_made(k):
                    if k % 2 == 0:
                        pe.wait_ge(S["hid_made"], PAIR_STEPS[key] + k // 2 + 1)
                eager_slab(first, hid_hi, hid_lo, kt, pair_made)

            def pre_slabs(name, first, count, hi=act_hi, lo=act_lo):
                eager_slab(first, hi, lo, NT, lambda k: pe.wait_ge(S["ulo_made"], NT * SPLIT_NO[name] + k + 1))
                if name == "first":
                    pe.wait_ge(S["consts_loaded"], 16)
                sums(name)
                slab(first, 0, 1, hi, lo, middle=lambda: spread_rms(name))
                if count > 2:
                    slabs(first, count, hi, lo, begin=1)

            def post_slabs(name, first, hi, lo, kt=8, eager=None):
                for i in range(2):
                    for s in range(2):
                        if eager is not None and i + s == 0:
                            eager()
                        else:
                            slab(first, i, s, hi, lo, kt=kt)
                stay_warm(3)
                sums(name)
                stay_warm(1)
                spread_rms(name)
                stay_warm(4)

            def stay_warm(n, bank=6):
                for _ in range(n):
                    mm(ps[:, bank, :], c("ones"), cst[:, 0:512], start=True, stop=True)

            def wide_slab(first, s, hi, lo, k0):
                slab_start(first, 0, s)
                for m in range(4):
                    for k in range(4):
                        a = k * 512 + m * 128
                        wh, wl = w_hi[:, s, a:a + 128], w_lo[:, s, a:a + 128]
                        out = ps[:, 4 * s + m, :]
                        mm(out, wh, hi[:, k0 + k, :], start=(k == 0), stop=False)
                        mm(out, wh, lo[:, k0 + k, :], start=False, stop=False)
                        inst = mm(out, wl, hi[:, k0 + k, :], start=False, stop=(k == 3))
                inst.then_inc(S["slab_mm"], 1)

            def sums(name):
                pe.wait_ge(S["sq_added"], NORM[name] + 1)
                for k in range(2):
                    for t in range(4):
                        inst = mm(ps[:, 4, t:t + 1], squares(name)[:, k, 128 * t:128 * t + 128], c("mean", n=1),
                                  start=(k == 0 and t == 0), stop=(k == 1), skip_group_check=True)
                inst.then_inc(S["sum_mm"], 1)

            def spread_rms(name):
                pe.wait_ge(S["diag_made"], NORM[name] + 1)
                mm(ps[:, 5, :], c("ones"), scratch[:, 2, :], start=True, stop=True).then_inc(S["rstd_mm"], 1)

            def ffn(f):
                for cn, kt in enumerate(FFN_CHUNKS):
                    key, first = f"ffn{f}_{cn}", FIRST[f"ffn{f}_in{cn}"]
                    if cn == 0 and f != 2:
                        pre_slabs(f"ffn{f}_pre", first, kt)
                    else:
                        if cn == 0:
                            pe.wait_ge(S["ulo2_made"], NT)
                        slabs(first, kt, act_hi, act_lo)
                    if cn < 2:
                        out_slabs(key, first + kt, kt)
                    else:
                        post_slabs(f"ffn{f}_post", first + kt, hid_hi, hid_lo, kt=kt,
                                   eager=lambda: eager_out(key, first + kt, kt))

            def attention(a, q_of, k_of, v_of):
                g0, steps = 16 * a, STEPS[a]
                for t in range(steps + 3):
                    if a == 1 and t == 2:
                        pe.wait_ge(banks_free[1], FIRST["o2"] // 2)
                    if t < steps:
                        if t >= 2:
                            pe.wait_ge(S["at_max"], g0 + t - 1)
                        for h in range(2):
                            for part, keys in enumerate(k_of(t, h)):
                                n = 256 // len(k_of(t, h))
                                inst = mm(ps[:, SCORE_BANKS[t % 2] + h, n * part:n * part + n], q_of(t, h), keys, start=True, stop=True)
                        inst.then_inc(S["at_s"], 1)
                        if a == 1 and t < 3:
                            stay_warm(1, bank=5)
                    if a == 0 and 1 <= t <= steps:
                        u = t - 1
                        if u:
                            pe.wait_ge(S["at_vtok"], u)
                        pe.wait_ge(S["at_vblk"], u + 1)
                        for part in range(2):
                            inst = nc.tensor.transpose(ps[:, 5, 128 * part:128 * part + 128],
                                                       vb_buf[:, u % 2, 128 * part:128 * part + 128], c("ident"))
                        inst.then_inc(S["at_vt"], 1)
                    if 2 <= t <= steps + 1:
                        u = t - 2
                        pe.wait_ge(S["at_p"], g0 + u + 1)
                        if u >= 2:
                            pe.wait_ge(S["at_ptsb"], g0 + u - 1)
                        for h in range(2):
                            for part in range(2):
                                inst = nc.tensor.transpose(ps[:, TURN_BANKS[u % 2], 256 * h + 128 * part:256 * h + 128 * part + 128],
                                                           p_buf[:, u % 3, h, 128 * part:128 * part + 128], c("ident"))
                        inst.then_inc(S["at_pt"], 1)
                    if t >= 3:
                        u = t - 3
                        pe.wait_ge(S["at_ptsb"], g0 + u + 1)
                        if u:
                            pe.wait_ge(S["at_osb"], g0 + u)
                        elif a == 0:
                            pe.wait_ge(S["at_vtok"], u + 1)
                        for h in range(2):
                            for part in range(2):
                                v = vt_buf[:, u % 2, part, 64 * h:64 * h + 64] if a == 0 else v_of(u, h, part)
                                inst = mm(ps[64 * h:64 * h + 64, 3, 0:128], v, pt_buf[:, u % 2, h, part, :],
                                          start=(part == 0), stop=(part == 1))
                        inst.then_inc(S["at_o"], 1)

            def heads_chunks(out, lhs, rhs):
                for n in range(NCH):
                    for h in range(2):
                        a, b = 64 * h, 64 * h + 64
                        inst = mm(out[a:b, 64 * n:64 * n + 64], lhs(a, b, n), rhs(a, b, n), start=True, stop=True)
                return inst

            def transposes(out, tile):
                for n in range(NCH):
                    at = slice(64 * n, 64 * n + 64)
                    nc.tensor.transpose(out[0:64, at], tile[0:64, at], c("eye", p1=64))
                    inst = mm(out[64:128, at], tile[64:128, at], c("eye", p0=64), start=True, stop=True)
                return inst

            def waited():
                pe.sem_inc(S["pe_waited"], 1)

            def chunk_of(tile):
                return lambda a, b, n: tile[a:b, 64 * n:64 * n + 64]

            def kk_sums(g):
                for q in range(2):
                    pe.wait_ge(S["kk_sq"], g * 2 + (q + 1))
                    inst = mm(ps[0:16, 5, :], c("sel", 16 * q), scratch[:, q, :], start=(q == 0), stop=(q == 1))
                inst.then_inc(S["kk_sum"], 1)

            def kk_spread(g):
                pe.wait_ge(S["kk_recip"], g + 1)
                for q in range(2):
                    inst = mm(ps[:, 6 + q, :], spread[0:16, 128 * q:128 * q + 128], rows16, start=True, stop=True)
                inst.then_inc(S["kk_spread"], 1)

            def rwkv_duo(g, more):
                for j, (name, lhs, rhs, _) in enumerate(JOBS):
                    for q in range(2):
                        if j == 0:
                            pe.wait_ge(S["dve_prep"], g * 3 + 2)
                            pe.wait_ge(S["v_loaded"], g * 16 + 16)
                        if name == "KabT":
                            pe.wait_ge(S["dve_prep"], g * 3 + 3)
                        for need in JOB_NEEDS[j]:
                            pe.wait_ge(job_out[q], g * len(JOBS) + (need + 1))
                        out = ps[:, 4 * q + j % 4, :]
                        waited()
                        if name == "bonus":
                            inst = mm(out, c("blk1"), TMP["rk"][q], start=True, stop=True)
                        elif rhs is None:
                            inst = transposes(out, TMP[lhs][q])
                        else:
                            inst = heads_chunks(out, chunk_of(TMP[lhs][q]), chunk_of(TMP[rhs][q]))
                        inst.then_inc(job_mm[q], 1)
                for q in range(2):
                    pe.wait_ge(job_out[q], (g + 1) * len(JOBS))
                for n in range(NCH):
                    old = state[:, n % 2]

                    def part(bank, lhs, rhs, start, stop):
                        for q in range(2):
                            for h in range(2):
                                a, b = 64 * h, 64 * h + 64
                                inst = mm(ps[a:b, bank, 64 * q:64 * q + 64], lhs(a, b, q), rhs(a, b, q), start=start and q == 0,
                                          stop=stop, skip_group_check=True)
                        return inst

                    def ch(name):
                        return lambda a, b, q: TMP[name][q][a:b, 64 * n:64 * n + 64]

                    def st(a, b, q):
                        return old[a:b, 64 * q:64 * q + 64]

                    def of(tile):
                        return lambda a, b, q: tile[a:b, 64 * q:64 * q + 64]

                    pe.wait_ge(S["st_out"], g * (NCH + 1) + (n + 1))
                    waited()
                    part(0, ch("KK"), st, True, False)
                    part(0, ch("KakT"), ch("vT"), False, True).then_inc(S["rhs_mm"], 1)
                    if n >= 2:
                        pe.wait_ge(S["y_out"], g * NCH + (n - 1))
                        waited()
                    part(3 + n % 2, st, ch("R"), True, False)
                    part(3 + n % 2, ch("vT"), ch("RkT"), False, False)
                    pe.wait_ge(S["rhs_out"], g * NCH + (n + 1))
                    waited()
                    part(1, ch("XT"), of(rhs_sb), True, True).then_inc(S["sa_mm"], 1)
                    part(2, ch("kT"), ch("vT"), True, False)
                    if more and n == 4:
                        kk_sums(g + 1)
                    pe.wait_ge(S["sa_out"], g * NCH + (n + 1))
                    waited()
                    part(2, ch("bT"), of(sa_sb), False, True).then_inc(S["st_mm"], 1)
                    part(3 + n % 2, of(sa_sb), ch("RbT"), False, True).then_inc(S["y_mm"], 1)
                if more:
                    kk_spread(g + 1)
                pe.wait_ge(S["st_out"], (g + 1) * (NCH + 1))
                pe.wait_ge(S["y_out"], (g + 1) * NCH)

            pre_slabs("first", 0, 6)
            slabs(6, 4, act_hi, act_lo)

            def qk_sums():
                for n, pair in enumerate((0, 2, 1, 3)):
                    pe.wait_ge(S["qk_sq"], n + 1)
                    for j in (2 * pair, 2 * pair + 1):
                        inst = mm(ps[0:16, 4, :], c("sel", 16 * j), qk_squares(j), start=(j == 0), stop=(j == 7))
                inst.then_inc(S["qk_sum"], 1)

            def qk_spread(j):
                if j >= 4:
                    pe.wait_ge(S["qk_done"], j - 3)
                mm(ps[:, 4 + j % 4, :], spread[0:16, 128 * j:128 * j + 128], rows16, start=True, stop=True).then_inc(S["qk_bcast"], 1)

            def qk_spread_q():
                pe.wait_ge(S["qk_recip"], 1)
                pe.wait_ge(S["spread_loaded"], 16)
                for j in range(4):
                    qk_spread(j)
            slab(10, 0, 0, act_hi, act_lo, middle=qk_sums)
            slab(10, 0, 1, act_hi, act_lo, middle=qk_spread_q)
            for j in range(4, 8):
                qk_spread(j)
            pe.wait_ge(S["qk_done"], 8)
            for s in range(2):
                pe.wait_ge(banks_free[s], 6)
            attention(0, na_q, na_k, None)
            pe.wait_ge(S["at_osb"], STEPS[0])
            pe.wait_ge(S["at_max"], STEPS[0])
            for s in range(2):
                wide_slab(FIRST["conv_branch"], s, hid_hi, hid_lo, 4)
            for s in range(2):
                pe.wait_ge(S["branch_made"], 1)
                wide_slab(FIRST["attn_branch"], s, hid_hi, hid_lo, 0)

            def spread_again():
                pe.wait_ge(banks_free[1], FIRST["gates"] // 2)
                pe.wait_ge(S["gdiag_made"], 1)
                mm(ps[:, 5, :], c("ones"), scratch[:, 2, :], start=True, stop=True).then_inc(S["grstd_mm"], 1)
            slab(FIRST["gates"], 0, 0, act_hi, act_lo, middle=spread_again)
            slab(FIRST["gates"], 0, 1, act_hi, act_lo)
            slabs(FIRST["gates"], 8, act_hi, act_lo, begin=1)
            eager_slab(FIRST["w_o"], hid_hi, hid_lo, NT, lambda k: pe.wait_ge(S["merged_made"], k // 2 + 1))
            slab(FIRST["w_o"], 0, 1, hid_hi, hid_lo)
            slabs(FIRST["w_o"], 4, hid_hi, hid_lo, begin=1)
            for cn in range(4):
                if cn == 0:
                    pre_slabs("mlp", FIRST["mlp_in0"], 4)
                else:
                    slabs(FIRST[f"mlp_in{cn}"], 4, act_hi, act_lo)
                out_slabs(f"mlp{cn}", FIRST[f"mlp_out{cn}"], 8)

            ffn(0)
            sums("mixer0_pre")
            spread_rms("mixer0_pre")
            n = FIRST["lora"]
            pe.wait_ge(S["lo_made"], n + 1)
            for j, (col, hi, lo) in enumerate(((0, act_hi, act_lo), (0, hid_hi, hid_lo), (128, act_hi, act_lo))):
                for k in range(NT):
                    pe.wait_ge(S["mix_lo"], NT * j + k + 1)
                    a = k * 256 + col
                    wh, wl = w_hi[:, 0, a:a + 128], w_lo[:, 0, a:a + 128]
                    mm(ps[:, j, :], wh, hi[:, k, :], start=(k == 0), stop=False)
                    mm(ps[:, j, :], wh, lo[:, k, :], start=False, stop=False)
                    inst = mm(ps[:, j, :], wl, hi[:, k, :], start=False, stop=(k == NT - 1))
                inst.then_inc(S["lora_mm"] if j < 2 else S["slab_mm"], 1)
            pe.wait_ge(S["lora_lo"], 1)
            pe.wait_ge(S["lo_made"], n + 2)
            for j in range(24):
                kind, m = divmod(j, NT)
                if 4 <= j < 20:
                    pe.wait_ge(S["lora_out"], j - 3)
                elif j >= 20:
                    pe.wait_ge(S["lora_g_out"], j - 19)
                a = 128 * m + (1024 if kind == 2 else 0)
                wh, wl = w_hi[:, 1, a:a + 128], w_lo[:, 1, a:a + 128]
                out = ps[:, j % 4, :]
                mm(out, wh, hid_hi[:, kind, :], start=True, stop=False)
                mm(out, wh, hid_lo[:, kind, :], start=False, stop=False)
                inst = mm(out, wl, hid_hi[:, kind, :], start=False, stop=True)
                inst.then_inc(S["lora_mm"] if j < 23 else S["slab_mm"], 1)
            pe.wait_ge(S["banks1_free"], FIRST["r"] // 2)
            for name, j, hi, lo in (("r", 3, act_hi, act_lo), ("k", 4, hid_hi, hid_lo), ("v", 5, act_hi, act_lo)):
                eager_slab(FIRST[name], hi, lo, NT, lambda k: pe.wait_ge(S["mix_lo"], NT * j + k + 1))
                slab(FIRST[name], 0, 1, hi, lo)
                if name != "v":
                    slabs(FIRST[name], 4, hi, lo, begin=1)
            slab(FIRST["v"], 1, 0, act_hi, act_lo)
            slab(FIRST["v"], 1, 1, act_hi, act_lo, middle=lambda: kk_sums(0))
            kk_spread(0)
            pe.wait_ge(banks_free[0], FIRST["rwkv_o"] // 2)
            pe.wait_ge(banks_free[1], FIRST["rwkv_o"] // 2)
            with pe.Fori(0, DUOS - 1) as g:
                rwkv_duo(g, True)
            rwkv_duo(DUOS - 1, False)
            for m in range(NT):
                pe.wait_ge(S["gn_loaded"], 48)
                if m >= 2:
                    pe.wait_ge(S["gn_d"], m - 1)
                mm(ps[:, 4 + m % 2, :], c("blk64"), work[:, m, :], start=True, stop=True).then_inc(S["gn_mean"], 1)
                if m:
                    pe.wait_ge(S["gn_sq"], m)
                    mm(ps[0:16, 6, :], c("sel", 16 * (m - 1)), scratch[:, (m - 1) % 2, :], start=(m == 1), stop=False).then_inc(S["gn_sum"], 1)
            pe.wait_ge(S["gn_sq"], NT)
            mm(ps[0:16, 6, :], c("sel", 16 * 7), scratch[:, 1, :], start=False, stop=True).then_inc(S["gn_sum"], 1)
            pe.wait_ge(S["gn_recip"], 1)
            for m in range(NT):
                if m >= 2:
                    pe.wait_ge(S["gn_scaled"], m - 1)
                mm(ps[:, 4 + m % 2, :], spread[0:16, 128 * m:128 * m + 128], rows16, start=True, stop=True).then_inc(S["gn_bcast"], 1)
            post_slabs("mixer0_post", FIRST["rwkv_o"], act_hi, act_lo,
                       eager=lambda: eager_slab(FIRST["rwkv_o"], act_hi, act_lo, NT, lambda k: pe.wait_ge(S["gn_lo"], k + 1)))
            ffn(1)
            pre_slabs("kv", FIRST["kv"], 2, hid_hi, hid_lo)
            ffn(2)
            pre_slabs("mixer1_pre", FIRST["q2"], 4)
            for b in range(4):
                for a in range(2):
                    inst = nc.tensor.transpose(ps[:, 4 + b // 2, 256 * (b % 2) + 128 * a:256 * (b % 2) + 128 * a + 128],
                                               work[:, 22 + a, 128 * b:128 * b + 128], c("ident"))
            inst.then_inc(S["vtok_mm"], 1)
            pe.wait_ge(banks_free[0], FIRST["o2"] // 2)
            pe.wait_ge(S["vtok_out"], 1)
            attention(1, swa_q, swa_k, swa_v)
            post_slabs("mixer1_post", FIRST["o2"], act_hi, act_lo,
                       eager=lambda: eager_slab(FIRST["o2"], act_hi, act_lo, NT, lambda k: pe.wait_ge(S["branch_made"], k + 2)))
            ffn(3)

        @block.scalar
        def _(act):
            af = nc.scalar.activation

            def hi_next(first, i, s):
                act.wait_ge(raw_loaded[1 - s], (i + (first // 2 + s + 1 if s else first // 2 + 1)) * 16)
                if first + s or not isinstance(i, int):
                    act.wait_ge(S["slab_mm"], i * 2 + (first + s))
                nc.scalar.copy(w_hi[:, 1 - s, :], w_raw[:, 1 - s, :]).then_inc(S["hi_made"], 1)

            def slabs(first, count, body=None, head=None):
                def one(i, s, more=True, head=None):
                    if more:
                        hi_next(first, i, s)
                    if head is not None:
                        head()
                    if body is not None:
                        act.wait_ge(S["slab_mm"], i * 2 + (first + s + 1))
                        body(i, s)
                begin = 1 if head is not None else 0
                end = first + count == SLABS
                if begin:
                    one(0, 0, head=head)
                    one(0, 1)
                if count // 2 - end > begin:
                    with act.Fori(begin, count // 2 - end) as i:
                        one(i, 0)
                        one(i, 1)
                if end:
                    one(count // 2 - 1, 0)
                    one(count // 2 - 1, 1, more=False)

            def evacuated(end):
                for s in range(2):
                    act.wait_ge(banks_free[s], end // 2)

            def root(name):
                act.wait_ge(S["mean_made"], NORM[name] + 1)
                af(small[:, 4:8], small[:, 0:4], ACT.Sqrt).then_inc(S["root_made"], 1)

            def norm_of_x(name, x_ready=None):
                for n in range(4):
                    if x_ready is not None:
                        x_ready(2 * n + 1)
                    af(pairs(squares(name))[:, n], pairs(x)[:, n], ACT.Square).then_inc(S["sq_made"], 1)
                root(name)

            def pre(name, free, x_ready):
                act.wait_ge(S["slab_mm"], free)
                for k in range(NT):
                    x_ready(k)
                    dst = hid_hi if name == "kv" else act_hi
                    af(dst[:, k, :], x[:, k, :], ACT.Copy, scale=vec(GAIN[name], k)).then_inc(S["uhi_made"], 1)
                    if name == "kv":
                        af(act_hi[:, k, :], x[:, k, :], ACT.Copy, scale=vec(GAIN["ffn2_pre"], k)).then_inc(S["uhi2_made"], 1)

            def x_after(name):
                return lambda k: act.wait_ge(S["x_made"], NT * POST_NO[name] + k + 1)

            def x_after_slabs(first):
                return lambda k: act.wait_ge(banks_free[k // 2 % 2], first // 2 + k // 4 + 1)

            def post_slabs(name, first):
                def square(i, s):
                    act.wait_ge(banks_free[s], i + (first // 2 + 1))
                    af(pairs(squares(name))[:, i * 2 + s], pairs(ybuf)[:, i * 2 + s], ACT.Square).then_inc(S["sq_made"], 1)
                slabs(first, 4, square)
                root(name)

            def ffn(f, free=None, x_ready=None):
                if f != 2:
                    pre(f"ffn{f}_pre", free, x_ready)
                for cn, n in enumerate(FFN_CHUNKS):
                    first = FIRST[f"ffn{f}_in{cn}"]

                    def silu(i):
                        act.wait_ge(banks_free[0], i + (first // 2 + 1))
                        af(work[:, 8:10, :], work[:, 8:10, :], ACT.Silu).then_inc(S["gate_made"], 1)
                    begin = 0
                    if cn == 0 and f != 2:
                        hi_next(first, 0, 0)
                        norm_of_x(f"ffn{f}_pre")
                        hi_next(first, 0, 1)
                        silu(0)
                        begin = 1
                    with act.Fori(begin, n // 2) as i:
                        hi_next(first, i, 0)
                        silu(i)
                        hi_next(first, i, 1)
                    if cn < 2:
                        slabs(first + n, 4)
                    else:
                        post_slabs(f"ffn{f}_post", first + n)

            def attention(a):
                g0, steps = 16 * a, STEPS[a]
                for t in range(steps + 3):
                    if a == 0 and 1 <= t <= steps:
                        u = t - 1
                        tile, j = divmod(u, 4)
                        if u >= 2:
                            act.wait_ge(S["at_vt"], u - 1)
                        v = work[:, 8 + tile, :].rearrange("p (r c) -> p r c", c=64)[:, :, NA_KEY0[j]:NA_KEY0[j] + 32]
                        nc.scalar.copy(vb_buf[:, u % 2, :].rearrange("p (r c) -> p r c", c=32), v).then_inc(S["at_vblk"], 1)
                    if t < steps:
                        g, b, e = g0 + t, t % 3, t % 2
                        act.wait_ge(S["at_max"], g + 1)
                        for h in range(2):
                            inst = af(p_buf[:, b, h, :], p_buf[:, b, h, :], ACT.Exp,
                                      bias=small[:, 12 + 2 * e + h:13 + 2 * e + h],
                                      accum_out=small[:, 16 + 2 * e + h:17 + 2 * e + h])
                        if a == 1:
                            for h in range(2):
                                inst = af(small[:, 24 + 2 * e + h:25 + 2 * e + h],
                                          sinks[:, 2 * (t // 4) + h:2 * (t // 4) + h + 1], ACT.Exp,
                                          bias=small[:, 12 + 2 * e + h:13 + 2 * e + h])
                        inst.then_inc(S["at_exp"], 1)
                    if a == 0 and 1 <= t <= steps:
                        u = t - 1
                        act.wait_ge(S["at_vt"], u + 1)
                        if u >= 2:
                            act.wait_ge(S["at_o"], u - 1)
                        nc.scalar.copy(vt_buf[:, u % 2, :, :], ps[:, 5, 0:256].rearrange("p (a k) -> p a k", a=2)).then_inc(S["at_vtok"], 1)
                    if 2 <= t <= steps + 1:
                        u = t - 2
                        act.wait_ge(S["at_pt"], g0 + u + 1)
                        if u >= 2:
                            act.wait_ge(S["at_o"], g0 + u - 1)
                        nc.scalar.copy(pt_buf[:, u % 2, :, :, :],
                                       ps[:, TURN_BANKS[u % 2], :].rearrange("p (h a k) -> p h a k", h=2, a=2)).then_inc(S["at_ptsb"], 1)
                    if t >= 3:
                        u = t - 3
                        act.wait_ge(S["at_o"], g0 + u + 1)
                        tile, j = divmod(u, 4)
                        nc.scalar.copy(work[:, tile, 128 * j:128 * j + 128], ps[:, 3, 0:128]).then_inc(S["at_osb"], 1)

            def mix(j, wait):
                dst = hid_hi if j in (1, 4) else act_hi
                for k in range(NT + 1):
                    if k < NT:
                        e = NT * j + k
                        if e >= 2:
                            act.wait_ge(S["mix_made"], e - 1)
                        af(scratch[:, k % 2, :], u_now(k), ACT.Copy, scale=omu[:, NT * MIX[j] + k:NT * MIX[j] + k + 1]).then_inc(S["t_made"], 1)
                    if k == 0:
                        wait()
                    if k:
                        e = NT * j + k - 1
                        act.wait_ge(S["mix_made"], e + 1)
                        nc.scalar.copy(dst[:, k - 1, :], scratch[:, 2 + (k - 1) % 2, :]).then_inc(S["mix_hi"], 1)

            def rwkv_act():
                norm_of_x("mixer0_pre", x_after("ffn0_post"))
                n0 = FIRST["lora"]
                hi_next(n0, 0, 0)
                act.wait_ge(S["u_made"], NT)
                mix(0, lambda: None)
                mix(1, lambda: None)
                mix(2, lambda: act.wait_ge(S["lora_mm"], 1))
                act.wait_ge(S["lora_mm"], 1)
                af(work[0:64, 0, :], ps[0:64, 0, :], ACT.Tanh)
                act.wait_ge(S["lora_mm"], 2)
                nc.scalar.copy(work[64:128, 1, :], ps[64:128, 1, :])
                act.wait_ge(S["slab_mm"], n0 + 1)
                af(work[:, 2, :], ps[:, 2, :], ACT.Sigmoid).then_inc(banks_free[0], 1)
                hi_next(n0, 0, 1)
                act.wait_ge(S["lora_lo"], 1)
                for j in range(16):
                    kind, m = divmod(j, NT)
                    act.wait_ge(S["lora_mm"], j + 3)
                    af(work[:, j, :], ps[:, j % 4, :], ACT.Sigmoid, bias=vec(("w0", "a0")[kind], m)).then_inc(S["lora_out"], 1)
                act.wait_ge(S["lora_out"], 16)
                for kind, row in enumerate((LW_, A_)):
                    act.dma_start(spill[row], work[:, 8 * kind:8 * kind + 8, :]).then_inc(S["spilled"], 16)
                mix(3, lambda: act.wait_ge(S["slab_mm"], n0 + 1))
                act.wait_ge(banks_free[1], n0 // 2 + 1)
                act.dma_start(spill[G_], work[:, 16:24, :]).then_inc(S["spilled"], 16)

                def keep(tiles):
                    def body(i, s):
                        nc.scalar.copy(pairs(tiles)[:, i * 2 + s], banks(2 * s)).then_inc(banks_free[s], 1)
                    return body

                def before_r():
                    mix(4, lambda: act.wait_ge(S["slab_mm"], n0 + 2))
                    act.wait_ge(S["spilled"], 48)
                slabs(FIRST["r"], 4, keep(work), head=before_r)
                evacuated(FIRST["r"] + 4)
                act.dma_start(spill[R_], work[:, 0:8, :]).then_inc(S["spilled"], 16)
                slabs(FIRST["k"], 4, keep(work[:, 8:16, :]), head=lambda: mix(5, lambda: act.wait_ge(S["slab_mm"], FIRST["k"])))
                evacuated(FIRST["k"] + 4)
                act.dma_start(spill[K_], work[:, 8:16, :]).then_inc(S["spilled"], 16)
                act.dma_start(spread[0:16, :], spread_in).then_inc(S["spread_loaded"], 16)
                act.dma_start(restart, restart_in).then_inc(S["spread_loaded"], 16)
                steps = prep_act(0)
                for n in range(4):
                    i, s = divmod(n, 2)
                    hi_next(FIRST["v"], i, s)
                    act.wait_ge(S["slab_mm"], FIRST["v"] + n + 1)
                    nc.scalar.copy(pairs(v_tiles)[:, n], banks(2 * s)).then_inc(banks_free[s], 1)
                    act.wait_ge(banks_free[s], FIRST["v"] // 2 + i + 1)
                    act.dma_start(pairs(spill[V_])[:, n], pairs(v_tiles)[:, n]).then_inc(S["spilled"], 16)
                    if n == 1:
                        act.wait_ge(S["spilled"], 16 * (5 + 2))
                        steps[0]()
                    if n == 2:
                        steps[3]()
                        steps[4]()
                steps[5]()
                steps[6]()
                act.wait_ge(S["spilled"], SPILLED)
                load_v(0)
                with act.Fori(0, DUOS - 1) as g:
                    duo_act(g, True)
                duo_act(DUOS - 1, False)
                for m in range(NT):
                    act.wait_ge(S["gn_d"], m + 1)
                    if m >= 2:
                        act.wait_ge(S["gn_sum"], m - 1)
                    af(scratch[:, m % 2, :], work[:, m, :], ACT.Square).then_inc(S["gn_sq"], 1)
                act.wait_ge(S["gn_var"], 1)
                af(rows16b, rows16, ACT.Sqrt).then_inc(S["gn_root"], 1)
                for m in range(NT + 1):
                    if m < NT:
                        act.wait_ge(S["gn_scaled"], m + 1)
                        af(work[:, m, :], work[:, m, :], ACT.Identity, scale=vec("gn_g", m), bias=vec("gn_b", m)).then_inc(S["gn_affine"], 1)
                    if m:
                        act.wait_ge(S["gn_gated"], m)
                        nc.scalar.copy(act_hi[:, m - 1, :], work[:, m - 1, :]).then_inc(S["gn_hi"], 1)
                post_slabs("mixer0_post", FIRST["rwkv_o"])

            def load_v(g):
                act.dma_start(IN_V, pairs(spill[V_])[:, g]).then_inc(S["v_loaded"], 16)

            def prep_act(g):
                def load():
                    act.wait_ge(S["dve_free"], g + 1)
                    for tile, row in ((IN_LW, LW_), (IN_K, K_), (IN_A, A_), (IN_R, R_)):
                        act.dma_start(tile, pairs(spill[row])[:, g]).then_inc(S["duo_loaded"], 16)

                def kk():
                    act.wait_ge(S["duo_vec"], g + 1)
                    act.wait_ge(S["duo_loaded"], g * 64 + 64)
                    for q in range(2):
                        af(scratch[:, q, :], IN_K[:, q, :], ACT.Square, scale=duo_vec[:, q:q + 1]).then_inc(S["kk_sq"], 1)
                    for q in range(2):
                        af(TMP["kk"][q], IN_K[:, q, :], ACT.Copy, scale=duo_vec[:, q:q + 1])

                def a_part():
                    for q in range(2):
                        inst = af(TMP["k"][q], IN_A[:, q, :], ACT.Identity, scale=duo_vec[:, 2 + q:3 + q], bias=duo_vec[:, 6 + q:7 + q])
                    inst.then_inc(S["act_prep"], 1)

                def kk_norm():
                    act.wait_ge(S["kk_max"], g + 1)
                    af(rows16, rows16, ACT.Sqrt).then_inc(S["kk_root"], 1)

                def inverse_decay():
                    act.wait_ge(S["dve_prep"], g * 3 + 1)
                    inst = af(work[:, 10:12, :], work[:, 20:22, :], ACT.Exp, scale=DECAY)
                    inst.then_inc(S["act_prep"], 1)
                return {0: load, 3: kk, 4: a_part, 5: kk_norm, 6: inverse_decay}

            def load_gn():
                act.wait_ge(S["spilled"], SPILLED + 32 * DUOS - 16)
                act.dma_start(work[:, 0:6, :], spill[Y_][:, 0:6]).then_inc(S["gn_loaded"], 16)
                act.dma_start(work[:, 8:16, :], spill[BON_]).then_inc(S["gn_loaded"], 16)
                act.dma_start(work[:, 16:24, :], spill[G_]).then_inc(S["gn_loaded"], 16)

            def duo_act(g, more):
                for q in range(2):
                    inst = af(grown[q][:, :, 1:65], TMP["Y"][q].rearrange("p (n t) -> p n t", t=CH), ACT.Exp, scale=-DECAY)
                inst.then_inc(S["act_prep"], 1)
                for q in range(2):
                    act.wait_ge(job_out[q], (g + 1) * len(JOBS))
                act.dma_start(pairs(spill[BON_])[:, g], bonus_sb).then_inc(S["spilled"], 16)
                steps = {2: load_gn}
                if more:
                    steps = {**prep_act(g + 1), 1: lambda: load_v(g + 1)}
                y_to = y_sb if more else work[:, 6:8, :]
                for n in range(NCH):
                    act.wait_ge(S["sa_mm"], g * NCH + (n + 1))
                    af(sa_sb, ps[:, 1, 0:128], ACT.Copy, scale=-1.0).then_inc(S["sa_out"], 1)
                    if n in steps:
                        steps[n]()
                    act.wait_ge(S["y_mm"], g * NCH + (n + 1))
                    nc.scalar.copy(y_to[:, :, 64 * n:64 * n + 64], ps[:, 3 + n % 2, 0:128].rearrange("p (q t) -> p q t", q=2)).then_inc(S["y_out"], 1)
                if more:
                    act.wait_ge(S["y_out"], (g + 1) * NCH)
                    act.dma_start(pairs(spill[Y_])[:, g], y_sb).then_inc(S["spilled"], 16)
                    act.wait_ge(S["st_out"], (g + 1) * (NCH + 1))
                    act.wait_ge(S["spilled"], g * 32 + (SPILLED + 32))

            act.wait_ge(S["vecs_loaded"], 16)
            act.wait_ge(raw_loaded[0], 16)
            nc.scalar.copy(w_hi[:, 0, :], w_raw[:, 0, :]).then_inc(S["hi_made"], 1)
            for k in range(NT):
                if k % 4 == 0:
                    act.wait_ge(S["x2_loaded"] if k else S["x_loaded"], 16)
                af(act_hi[:, k, :], x[:, k, :], ACT.Copy, scale=vec(GAIN["first"], k)).then_inc(S["uhi_made"], 1)
            slabs(0, 6, head=lambda: norm_of_x("first"))
            slabs(6, 2)
            act.wait_ge(S["conv_done"], 1)
            act.dma_start(spread[0:16, :], spread_in).then_inc(S["spread_loaded"], 16)

            def square_qk(i, s):
                for n in (s, 2 + s):
                    act.wait_ge(banks_free[s], 4 + n // 2)
                    af(pairs(area)[:, 8 + n // 2 * 4 + s], pairs(work)[:, n], ACT.Square).then_inc(S["qk_sq"], 1)
            slabs(8, 2, square_qk)
            hi_next(10, 0, 0)
            act.wait_ge(S["qk_mean"], 1)
            af(rows16b, rows16, ACT.Sqrt).then_inc(S["qk_root"], 1)
            hi_next(10, 0, 1)
            evacuated(12)
            attention(0)
            act.wait_ge(S["branch_made"], 1)

            def branch(i, s, dst):
                nc.scalar.copy(dst[:, 4 * s:4 * s + 4], ps[:, 4 * s:4 * s + 4, :]).then_inc(banks_free[s], 1)
            slabs(FIRST["conv_branch"], 2, lambda i, s: branch(i, s, work))
            slabs(FIRST["attn_branch"], 2, lambda i, s: branch(i, s, ybuf[:, :, 0:T]))

            def gates(i, s):
                act.wait_ge(banks_free[s], i + (FIRST["gates"] // 2 + 1))
                af(scratch[:, 0:2, :], scratch[:, 0:2, :], ACT.Sigmoid).then_inc(S["sig_made"], 1)

            def gates_and_hi(i, s):
                gates(i + 2, s)
                act.wait_ge(S["tile_made"], i * 2 + (s + 1))
                nc.scalar.copy(pairs(hid_hi)[:, i * 2 + s], pairs(ybuf)[:, i * 2 + s]).then_inc(S["merged_hi"], 1)
            slabs(FIRST["gates"], 4, gates)
            slabs(FIRST["gates"] + 4, 4, gates_and_hi)
            slabs(FIRST["w_o"], 4)
            pre("mlp", FIRST["w_o"], x_after_slabs(FIRST["w_o"]))
            for cn in range(4):
                slabs(FIRST[f"mlp_in{cn}"], 4, head=(lambda: norm_of_x("mlp")) if cn == 0 else None)
                slabs(FIRST[f"mlp_out{cn}"], 4)
            ffn(0, FIRST["mlp_out3"], x_after_slabs(FIRST["mlp_out3"]))
            rwkv_act()
            ffn(1, FIRST["ffn1_in0"], x_after("mixer0_post"))
            pre("kv", FIRST["kv"], x_after("ffn1_post"))
            slabs(FIRST["kv"], 2, head=lambda: norm_of_x("kv"))
            ffn(2)
            pre("mixer1_pre", FIRST["q2"], x_after("ffn2_post"))

            def q2_head():
                norm_of_x("mixer1_pre")
                act.dma_start(work[:, 18, :].rearrange("p (b k) -> p b k", b=2), swa_in).then_inc(S["swa_loaded"], 16)
            slabs(FIRST["q2"], 4, head=q2_head)
            act.wait_ge(S["vtok_mm"], 1)
            nc.scalar.copy(work[:, 16:18, :], ps[:, 4:6, :]).then_inc(S["vtok_out"], 1)
            attention(1)
            for k in range(NT):
                act.wait_ge(S["at_osb"], STEPS[0] + STEPS[1])
                nc.scalar.copy(act_hi[:, k, :], work[:, k, :]).then_inc(S["merged_hi"], 1)
            post_slabs("mixer1_post", FIRST["o2"])
            ffn(3, FIRST["ffn3_in0"], x_after("mixer1_post"))
            act.wait_ge(S["x_made"], NT * len(POST_NO))
            act.dma_start(x_out, x[:]).then_inc(S["out_stored"], 16)
            act.wait_ge(S["out_stored"], 16)

        @block.vector
        def _(dve):
            tt = nc.vector.tensor_tensor
            stt = nc.vector.scalar_tensor_tensor
            ts = nc.vector.tensor_scalar
            copy = nc.vector.tensor_copy

            def norm(name, factor=1.0):
                r = NORM[name]
                sq = pairs(squares(name))
                for n in range(1, 4):
                    dve.drain()
                    dve.wait_ge(S["sq_made"], 4 * r + n + 1)
                    inst = tt(sq[:, 0], sq[:, 0], sq[:, n], ALU.add)
                inst.then_inc(S["sq_added"], 1)
                dve.wait_ge(S["sum_mm"], r + 1)
                ts(small[:, 0:4], ps[:, 4, 0:4], EPS, None, ALU.add).then_inc(S["mean_made"], 1)
                dve.wait_ge(S["root_made"], r + 1)
                nc.vector.reciprocal(small[:, 8:12], small[:, 4:8])
                dve.drain()
                diagonal(factor).then_inc(S["diag_made"], 1)
                dve.wait_ge(S["rstd_mm"], r + 1)

            def diagonal(factor):
                for t in range(4):
                    inst = ts(scratch[:, 2, 128 * t:128 * t + 128], c("ident"), small[:, 8 + t:9 + t], factor, ALU.mult, ALU.mult)
                return inst

            def lo_of_x(name, k):
                dve.wait_ge(S["uhi_made"], NT * SPLIT_NO[name] + k + 1)
                hi, lo = (hid_hi, hid_lo) if name == "kv" else (act_hi, act_lo)
                stt(out=lo[:, k, :], in0=x[:, k, :], scalar=vec(GAIN[name], k), in1=hi[:, k, :].bitcast(F32),
                    op0=ALU.mult, op1=ALU.subtract).then_inc(S["ulo_made"], 1)

            def pre(name):
                if name not in SPLIT_BY_POST:
                    for k in range(NT):
                        lo_of_x(name, k)
                if name == "kv":
                    for k in range(NT):
                        dve.wait_ge(S["uhi2_made"], k + 1)
                        stt(out=act_lo[:, k, :], in0=x[:, k, :], scalar=vec(GAIN["ffn2_pre"], k), in1=act_hi[:, k, :].bitcast(F32),
                            op0=ALU.mult, op1=ALU.subtract).then_inc(S["ulo2_made"], 1)
                norm(name)
                keep_rms()

            def keep_rms():
                copy(scratch[:, 3, :], ps[:, 5, :])
                dve.drain()

            def post(name, factor):
                norm(name, factor)
                for k in range(NT + 3):
                    if k < NT:
                        stt(out=work[:, k, :], in0=ybuf[:, k, 0:T], scalar=vec(GAIN[name], k), in1=ps[:, 5, :],
                            op0=ALU.mult, op1=ALU.mult).then_inc(S["t_scaled"], 1)
                    if k >= 3 and name in PRE_AFTER:
                        lo_of_x(PRE_AFTER[name], k - 3)

            rms2 = scratch[:, 3, :].unsqueeze(1).broadcast_to([P, 2, T])

            def slabs(first, count, body):
                with dve.Fori(0, count // 2) as i:
                    for s in range(2):
                        dve.wait_ge(S["slab_mm"], i * 2 + (first + s + 1))
                        body(i, s)

            def scaled(dst, s):
                return tt(dst, banks(2 * s), rms2, ALU.mult)

            def add_to(acc):
                def body(i, s):
                    a = pairs(acc)[:, i * 2 + s]
                    tt(a, banks(2 * s), a, ALU.add).then_inc(banks_free[s], 1)
                return body

            def ffn(f):
                if f != 2:
                    pre(f"ffn{f}_pre")
                for cn, n in enumerate(FFN_CHUNKS):
                    first = FIRST[f"ffn{f}_in{cn}"]
                    g0 = 11 * f + sum(FFN_CHUNKS[:cn]) // 2
                    with dve.Fori(0, n // 2) as i:
                        dve.drain()
                        dve.wait_ge(S["slab_mm"], i * 2 + (first + 1))
                        scaled(work[:, 8:10, :], 0).then_inc(banks_free[0], 1)
                        dve.wait_ge(S["slab_mm"], i * 2 + (first + 2))
                        scaled(work[:, 10:12, :], 1).then_inc(banks_free[1], 1)
                        dve.drain()
                        dve.wait_ge(S["gate_made"], i + (g0 + 1))
                        tt(pairs(hid_hi)[:, i], work[:, 10:12, :], work[:, 8:10, :], ALU.mult)
                        tt(work[:, 10:12, :], work[:, 10:12, :], work[:, 8:10, :], ALU.mult)
                        dve.drain()
                        tt(pairs(hid_lo)[:, i], work[:, 10:12, :], pairs(hid_hi)[:, i].bitcast(F32), ALU.subtract).then_inc(S["hid_made"], 1)
                    first += n
                    if cn == 0:
                        slabs(first, 4, lambda i, s: copy(pairs(ybuf)[:, i * 2 + s], banks(2 * s)).then_inc(banks_free[s], 1))
                    else:
                        slabs(first, 4, add_to(ybuf))
                post(f"ffn{f}_post", 0.5)

            def attention(a, heads_bias):
                g0, steps = 16 * a, STEPS[a]
                for t in range(steps + 1):
                    if t < steps:
                        g, b = g0 + t, t % 2
                        dve.wait_ge(S["at_s"], g + 1)
                        if t >= 3:
                            dve.wait_ge(S["at_pt"], g - 2)
                        tt(p_buf[:, t % 3, :, :], ps[:, SCORE_BANKS[b]:SCORE_BANKS[b] + 2, 0:256], heads_bias(t), ALU.add)
                        dve.drain()
                        nc.vector.tensor_reduce(small[:, 20 + 2 * b:22 + 2 * b], p_buf[:, t % 3, :, :], AX_X, ALU.max)
                        dve.drain()
                        if a == 1:
                            tt(small[:, 20 + 2 * b:22 + 2 * b], small[:, 20 + 2 * b:22 + 2 * b], sinks[:, 2 * (t // 4):2 * (t // 4) + 2], ALU.max)
                            dve.drain()
                        ts(small[:, 12 + 2 * b:14 + 2 * b], small[:, 20 + 2 * b:22 + 2 * b], -1.0, None, ALU.mult).then_inc(S["at_max"], 1)
                    if t >= 1:
                        g, b = g0 + t - 1, (t - 1) % 2
                        dve.wait_ge(S["at_exp"], g + 1)
                        if a == 1:
                            tt(small[:, 16 + 2 * b:18 + 2 * b], small[:, 16 + 2 * b:18 + 2 * b], small[:, 24 + 2 * b:26 + 2 * b], ALU.add)
                            dve.drain()
                        nc.vector.reciprocal(small[:, 28 + 2 * b:30 + 2 * b], small[:, 16 + 2 * b:18 + 2 * b])
                        dve.drain()
                        for h in range(2):
                            inst = ts(p_buf[:, (t - 1) % 3, h, :], p_buf[:, (t - 1) % 3, h, :], small[:, 28 + 2 * b + h:29 + 2 * b + h], None, ALU.mult)
                        inst.then_inc(S["at_p"], 1)

            def rwkv_dve():
                dve.drain()
                ts(omu[:], vecs[:, VEC["mu0"]:VEC["mu0"] + 48], -1.0, 1.0, ALU.mult, ALU.add)
                ts(oma[:], vecs[:, VEC["k_a"]:VEC["k_a"] + 8], -1.0, 1.0, ALU.mult, ALU.add)
                norm("mixer0_pre")
                nc.vector.memset(ybuf[:, :, 0:1], 0.0)
                nc.vector.memset(work[64:128, 0, :], 0.0)
                nc.vector.memset(work[0:64, 1, :], 0.0)
                for k in range(NT):
                    stt(out=u_now(k), in0=x[:, k, :], scalar=vec(GAIN["mixer0_pre"], k), in1=ps[:, 5, :],
                        op0=ALU.mult, op1=ALU.mult).then_inc(S["u_made"], 1)
                dve.drain()
                for j in range(6):
                    hi, lo = (hid_hi, hid_lo) if j in (1, 4) else (act_hi, act_lo)
                    if j == 3:
                        dve.wait_ge(banks_free[0], FIRST["lora"] // 2 + 1)
                        copy(hid_hi[:, 0:3, :], work[:, 0:3, :])
                        dve.drain()
                        tt(hid_lo[:, 0:3, :], work[:, 0:3, :], hid_hi[:, 0:3, :].bitcast(F32), ALU.subtract).then_inc(S["lora_lo"], 1)
                        for m in range(NT):
                            if m < NT - 1:
                                dve.wait_ge(S["lora_mm"], 16 + m + 3)
                            else:
                                dve.wait_ge(S["slab_mm"], FIRST["lora"] + 2)
                            copy(work[:, 16 + m, :], ps[:, m % 4, :]).then_inc(S["lora_g_out"] if m < NT - 1 else banks_free[1], 1)
                    for k in range(NT + 1):
                        e = NT * j + k
                        if k < NT:
                            dve.wait_ge(S["t_made"], e + 1)
                            if e >= 2:
                                dve.wait_ge(S["mix_hi"], e - 1)
                                dve.wait_ge(S["mix_lo"], e - 1)
                            stt(out=scratch[:, 2 + k % 2, :], in0=ybuf[:, k, 0:T], scalar=vec(f"mu{MIX[j]}", k), in1=scratch[:, k % 2, :],
                                op0=ALU.mult, op1=ALU.add).then_inc(S["mix_made"], 1)
                        if k:
                            dve.wait_ge(S["mix_hi"], e)
                            dve.wait_ge(S["mix_made"], e)
                            tt(lo[:, k - 1, :], scratch[:, 2 + (k - 1) % 2, :], hi[:, k - 1, :].bitcast(F32), ALU.subtract).then_inc(S["mix_lo"], 1)
                dve.wait_ge(S["slab_mm"], FIRST["v"])
                for q in range(2):
                    nc.vector.memset(grown[q][:, :, 0:1], 1.0)
                dve.wait_ge(S["spread_loaded"], 48)
                nc.vector.memset(small[:, 30:31], 0.0).then_inc(S["dve_free"], 1)
                for step in prep_dve(0).values():
                    step()
                dve.wait_ge(S["slab_mm"], FIRST["rwkv_o"])
                with dve.Fori(0, DUOS - 1) as g:
                    duo_dve(g, True)
                duo_dve(DUOS - 1, False)
                for m in range(NT):
                    dve.wait_ge(S["gn_mean"], m + 1)
                    tt(work[:, m, :], work[:, m, :], ps[:, 4 + m % 2, :], ALU.subtract).then_inc(S["gn_d"], 1)
                dve.wait_ge(S["gn_sum"], NT)
                ts(rows16, ps[0:16, 6, :], 1 / 64, GN_EPS, ALU.mult, ALU.add).then_inc(S["gn_var"], 1)
                dve.wait_ge(S["gn_root"], 1)
                nc.vector.reciprocal(rows16, rows16b).then_inc(S["gn_recip"], 1)
                for m in range(NT + 1):
                    if m < NT:
                        dve.wait_ge(S["gn_bcast"], m + 1)
                        tt(work[:, m, :], work[:, m, :], ps[:, 4 + m % 2, :], ALU.mult).then_inc(S["gn_scaled"], 1)
                    if m:
                        w = work[:, m - 1, :]
                        dve.wait_ge(S["gn_affine"], m)
                        tt(w, w, work[:, 8 + m - 1, :], ALU.add)
                        dve.drain()
                        tt(w, w, work[:, 16 + m - 1, :], ALU.mult).then_inc(S["gn_gated"], 1)
                        dve.wait_ge(S["gn_hi"], m)
                        tt(act_lo[:, m - 1, :], w, act_hi[:, m - 1, :].bitcast(F32), ALU.subtract).then_inc(S["gn_lo"], 1)
                slabs(FIRST["rwkv_o"], 4, lambda i, s: copy(pairs(ybuf)[:, i * 2 + s], banks(2 * s)).then_inc(banks_free[s], 1))
                post("mixer0_post", 1.0)

            def chunks(tile):
                return tile.rearrange("p (n t) -> p n t", t=CH)

            def mask(name):
                return c(name).unsqueeze(1).broadcast_to([P, NCH, 64])

            def prep_dve(g):
                kb, inv = work[:, 16:18, :], work[:, 10:12, :]

                def vectors():
                    for n, tab in enumerate((vecs[:, VEC["k_k"]:VEC["k_k"] + 8], vecs[:, VEC["k_a"]:VEC["k_a"] + 8],
                                             vecs[:, VEC["r_k"]:VEC["r_k"] + 8], oma[:])):
                        inst = copy(duo_vec[:, 2 * n:2 * n + 2], tab.rearrange("p (a b) -> p a b", b=2)[:, g])
                    inst.then_inc(S["duo_vec"], 1)

                def sums():
                    dve.wait_ge(S["duo_loaded"], g * 64 + 64)
                    for q in range(2):
                        inst = nc.vector.tensor_tensor_scan(TMP["Y"][q], restart, IN_LW[:, q, :], 0.0, ALU.mult, ALU.add)
                    inst.then_inc(S["dve_prep"], 1)

                def kk_max():
                    dve.wait_ge(S["kk_sum"], g + 1)
                    ts(rows16, ps[0:16, 5, :], 1e-24, None, ALU.max).then_inc(S["kk_max"], 1)
                    dve.wait_ge(S["act_prep"], g * 3 + 1)
                    tt(kb, IN_K, kb, ALU.mult)

                def recip():
                    dve.wait_ge(S["kk_root"], g + 1)
                    nc.vector.reciprocal(rows16, rows16).then_inc(S["kk_recip"], 1)

                def products():
                    dve.drain()
                    for q in range(2):
                        stt(out=TMP["rk"][q], in0=IN_R[:, q, :], scalar=duo_vec[:, 4 + q:5 + q], in1=TMP["k"][q], op0=ALU.mult, op1=ALU.mult)
                    dve.drain()
                    dve.wait_ge(S["act_prep"], g * 3 + 2)
                    tt(kb, kb, inv, ALU.mult)
                return {0: vectors, 3: sums, 5: kk_max, 6: recip, 7: products}

            def duo_dve(g, more):
                inv = work[:, 10:12, :]
                dve.wait_ge(S["kk_spread"], g + 1)
                tt(work[:, 12:14, :], work[:, 12:14, :], ps[:, 6:8, :], ALU.mult)
                dve.wait_ge(S["act_prep"], g * 3 + 3)
                for q in range(2):
                    inst = tt(chunks(TMP["R"][q]), chunks(IN_R[:, q, :]), grown[q][:, :, 1:65], ALU.mult)
                inst.then_inc(S["dve_prep"], 1)
                dve.drain()
                tt(work[:, 14:16, :], work[:, 12:14, :], IN_A, ALU.mult)
                for q in range(2):
                    tt(chunks(TMP["KK"][q]), chunks(TMP["kk"][q]), grown[q][:, :, 0:64], ALU.mult)
                dve.drain()
                tt(work[:, 14:16, :], work[:, 14:16, :], inv, ALU.mult).then_inc(S["dve_prep"], 1)
                dve.drain()
                dve.wait_ge(S["spilled"], g * 32 + SPILLED)
                for j, (name, _, _, m) in enumerate(JOBS):
                    for q in range(2):
                        dve.wait_ge(job_mm[q], g * len(JOBS) + (j + 1))
                        p = ps[:, 4 * q + j % 4, :]
                        if name == "KabT":
                            tt(chunks(TMP["XT"][q]), chunks(p), mask("firstT"), ALU.mult)
                            tt(chunks(TMP[name][q]), chunks(p), mask(m), ALU.mult)
                            dve.drain()
                            inst = tt(chunks(TMP["XT"][q]), chunks(TMP["XT"][q]), mask("eye"), ALU.add)
                        elif name == "XT+":
                            inst = tt(TMP["XT"][q], p, TMP["XT"][q], ALU.add)
                        elif name == "bonus":
                            inst = tt(bonus_sb[:, q, :], p, IN_V[:, q, :], ALU.mult)
                        elif m is None:
                            inst = copy(TMP[name][q], p)
                        else:
                            inst = tt(chunks(TMP[name][q]), chunks(p), mask(m), ALU.mult)
                        inst.then_inc(job_out[q], 1)
                dve.drain()
                nc.vector.memset(small[:, 30:31], 0.0).then_inc(S["dve_free"], 1)
                nc.vector.memset(state[:, 0, :], 0.0).then_inc(S["st_out"], 1)
                steps = prep_dve(g + 1) if more else {}
                for n in range(NCH):
                    dve.wait_ge(S["rhs_mm"], g * NCH + (n + 1))
                    copy(rhs_sb, ps[:, 0, 0:128]).then_inc(S["rhs_out"], 1)
                    dve.drain()
                    for q in range(2):
                        ts(old_sb[:, 64 * q:64 * q + 64], state[:, n % 2, 64 * q:64 * q + 64], grown[q][:, n, 64:65], None, ALU.mult)
                    if n in steps:
                        steps[n]()
                    dve.drain()
                    dve.wait_ge(S["st_mm"], g * NCH + (n + 1))
                    for q in range(2):
                        inst = stt(out=state[:, (n + 1) % 2, 64 * q:64 * q + 64], in0=ps[:, 2, 64 * q:64 * q + 64],
                                   scalar=grown[q][:, n, 64:65], in1=old_sb[:, 64 * q:64 * q + 64], op0=ALU.mult, op1=ALU.add)
                    inst.then_inc(S["st_out"], 1)
                dve.wait_ge(S["y_mm"], (g + 1) * NCH)

            for q in range(2):
                nc.vector.memset(ybuf[:, 4:8, q * (T + 1):q * (T + 1) + 1], 0.0)
            dve.wait_ge(S["vecs_loaded"], 16)
            ts(b_q8[:], vecs[:, VEC["b_q"]:VEC["b_q"] + 8], 0.125, None, ALU.mult)
            ts(gains8[:, 0:1], vec("q_norm_g"), 0.125, None, ALU.mult)
            na_bias = work[:, 12:24, :].rearrange("p k t -> p (k t)").rearrange("p (h k) -> p h k", h=8)
            na_mask = area[:, 24:26, :].rearrange("p k t -> p (k t)")[:, 0:768]
            pre("first")
            for s in range(2):
                dve.wait_ge(S["slab_mm"], 1 + s)
                scaled(pairs(ybuf)[:, s], s).then_inc(banks_free[s], 1)
            for s in range(2):
                dve.wait_ge(S["slab_mm"], 3 + s)
                scaled(ybuf[:, 4 + 2 * s:6 + 2 * s, 1:T + 1], s).then_inc(banks_free[s], 1)
            dve.wait_ge(S["bias_loaded"], 32)
            tt(na_bias, na_bias, na_mask.unsqueeze(1).broadcast_to([P, 8, 768]), ALU.add)
            for s in range(2):
                dve.wait_ge(S["slab_mm"], 5 + s)
                z = ybuf[:, 4 + 2 * s:6 + 2 * s, 1:T + 1]
                scaled(scratch[:, 0:2, :], s).then_inc(banks_free[s], 1)
                dve.drain()
                tt(z, scratch[:, 0:2, :], z, ALU.mult)
                dve.drain()

            def conv(j):
                z = ybuf[:, 4 + j, :]
                ts(area[:, 16 + j, :], z[:, 0:T], vec("conv_w", j), None, ALU.mult)
                dve.drain()
                for n in (1, 2):
                    stt(out=area[:, 16 + j, :], in0=z[:, n:n + T], scalar=vec("conv_w", 4 * n + j), in1=area[:, 16 + j, :],
                        op0=ALU.mult, op1=ALU.add)
                    dve.drain()

            def qk_pair(n):
                dve.wait_ge(S["slab_mm"], 7 + n)
                scaled(pairs(work)[:, n], n % 2).then_inc(banks_free[n % 2], 1)
            conv(0)
            conv(1)
            conv(2)
            qk_pair(0)
            conv(3)
            tt(area[:, 16:20, :], area[:, 16:20, :], ybuf[:, 0:4, 0:T], ALU.mult)
            dve.drain()
            copy(hid_hi[:, 4:8, :], area[:, 16:20, :])
            dve.drain()
            qk_pair(1)
            tt(hid_lo[:, 4:8, :], area[:, 16:20, :], hid_hi[:, 4:8, :].bitcast(F32), ALU.subtract).then_inc(S["conv_done"], 1)
            qk_pair(2)
            qk_pair(3)

            def v_pair(s):
                dve.wait_ge(S["slab_mm"], 11 + s)
                scaled(pairs(work)[:, 4 + s], s).then_inc(banks_free[s], 1)
            dve.wait_ge(S["qk_sum"], 1)
            dve.drain()
            ts(rows16, ps[0:16, 4, :], 1 / 64, EPS, ALU.mult, ALU.add).then_inc(S["qk_mean"], 1)
            dve.wait_ge(S["qk_root"], 1)
            nc.vector.reciprocal(rows16, rows16b).then_inc(S["qk_recip"], 1)
            v_pair(0)
            for j in range(8):
                if j == 4:
                    v_pair(1)
                dve.wait_ge(S["qk_bcast"], j + 1)
                if j < 4:
                    tt(scratch[:, j % 2, :].rearrange("p (j r c) -> p j r c", j=4, r=8),
                       work[:, j, :].rearrange("p (r j c) -> p j r c", j=4, r=8),
                       ps[:, 4 + j % 4, :].rearrange("p (r j c) -> p j r c", j=4, r=8), ALU.mult)
                    dve.drain()
                    inst = ts(work[:, j, :], scratch[:, j % 2, :], gains8[:, 0:1], None, ALU.mult)
                else:
                    inst = stt(out=work[:, j, :], in0=work[:, j, :], scalar=vec("k_norm_g"), in1=ps[:, 4 + j % 4, :],
                               op0=ALU.mult, op1=ALU.mult)
                inst.then_inc(S["qk_done"], 1)

            def bias_of(t):
                tile, j = divmod(t, 4)
                return na_bias[:, 2 * tile:2 * tile + 2, 256 * NA_CLASS[j]:256 * NA_CLASS[j] + 256]
            attention(0, bias_of)
            dve.wait_ge(S["at_osb"], STEPS[0])
            for j in range(4):
                o = work[:, j, :].rearrange("p (j r c) -> p r j c", j=4, r=8)
                copy(hid_hi[:, j, :].rearrange("p (r j c) -> p r j c", j=4, r=8), o)
            dve.drain()
            for j in range(4):
                o = work[:, j, :].rearrange("p (j r c) -> p r j c", j=4, r=8)
                inst = tt(hid_lo[:, j, :].rearrange("p (r j c) -> p r j c", j=4, r=8), o,
                          hid_hi[:, j, :].rearrange("p (r j c) -> p r j c", j=4, r=8).bitcast(F32), ALU.subtract)
            inst.then_inc(S["branch_made"], 1)
            n0 = FIRST["gates"]

            diagonal(1.0).then_inc(S["gdiag_made"], 1)
            dve.wait_ge(S["grstd_mm"], 1)
            keep_rms()
            for n, acc in enumerate((ybuf, work)):
                with dve.Fori(0, 2) as i:
                    for s in range(2):
                        dve.drain()
                        dve.wait_ge(S["slab_mm"], i * 2 + (n0 + 4 * n + s + 1))
                        scaled(scratch[:, 0:2, :], s).then_inc(banks_free[s], 1)
                        dve.wait_ge(S["sig_made"], i * 2 + (4 * n + s + 1))
                        a, y = pairs(acc)[:, i * 2 + s], pairs(ybuf)[:, i * 2 + s]
                        tt(a, scratch[:, 0:2, :], a, ALU.mult)
                        if n == 1:
                            dve.drain()
                            tt(y, y, a, ALU.add).then_inc(S["tile_made"], 1)
                            dve.wait_ge(S["merged_hi"], i * 2 + (s + 1))
                            tt(pairs(hid_lo)[:, i * 2 + s], y, pairs(hid_hi)[:, i * 2 + s].bitcast(F32), ALU.subtract).then_inc(S["merged_made"], 1)
            slabs(FIRST["w_o"], 4, add_to(x))
            pre("mlp")
            for cn in range(4):
                def relu2(i, s):
                    scaled(work[:, 8:10, :], s).then_inc(banks_free[s], 1)
                    dve.drain()
                    for out in (pairs(hid_hi)[:, i * 2 + s], work[:, 10:12, :]):
                        stt(out=out, in0=work[:, 8:10, :], scalar=0.0, in1=work[:, 8:10, :], op0=ALU.max, op1=ALU.mult)
                    dve.drain()
                    tt(pairs(hid_lo)[:, i * 2 + s], work[:, 10:12, :], pairs(hid_hi)[:, i * 2 + s].bitcast(F32),
                       ALU.subtract).then_inc(S["hid_made"], 1)
                    dve.drain()
                slabs(FIRST[f"mlp_in{cn}"], 4, relu2)
                slabs(FIRST[f"mlp_out{cn}"], 4, add_to(x))
            ffn(0)
            rwkv_dve()
            ffn(1)
            pre("kv")

            def biased(dst, b, s):
                scaled(dst, s)
                dve.drain()
                return tt(dst, dst, b.unsqueeze(2).broadcast_to([P, 2, T]), ALU.add)
            for s in range(2):
                dve.wait_ge(S["slab_mm"], FIRST["kv"] + s + 1)
                at = VEC["b_kv"] + 2 * s
                biased(work[:, 20 + 2 * s:22 + 2 * s, :], vecs[:, at:at + 2], s).then_inc(banks_free[s], 1)
            ffn(2)
            pre("mixer1_pre")
            with dve.Fori(0, 2) as i:
                for s in range(2):
                    dve.wait_ge(S["slab_mm"], i * 2 + (FIRST["q2"] + s + 1))
                    q = pairs(work)[:, i * 2 + s]
                    stt(out=q, in0=banks(2 * s), scalar=0.125, in1=rms2, op0=ALU.mult, op1=ALU.mult)
                    dve.drain()
                    b = b_q8[:].rearrange("p (a b) -> p a b", b=2)[:, i * 2 + s]
                    tt(q, q, b.unsqueeze(2).broadcast_to([P, 2, T]), ALU.add).then_inc(banks_free[s], 1)
            dve.wait_ge(S["swa_loaded"], 16)
            swa_mask = work[:, 18, :].rearrange("p (b k) -> p b k", b=2)
            attention(1, lambda t: swa_mask[:, min(t % 4, 1), :].unsqueeze(1).broadcast_to([P, 2, 256]))
            for k in range(NT):
                dve.wait_ge(S["merged_hi"], 4 + k + 1)
                tt(act_lo[:, k, :], work[:, k, :], act_hi[:, k, :].bitcast(F32), ALU.subtract).then_inc(S["branch_made"], 1)
            with dve.Fori(0, 2) as i:
                for s in range(2):
                    dve.wait_ge(S["slab_mm"], i * 2 + (FIRST["o2"] + s + 1))
                    b = vecs[:, VEC["b_o"]:VEC["b_o"] + 8].rearrange("p (a b) -> p a b", b=2)[:, i * 2 + s]
                    tt(pairs(ybuf)[:, i * 2 + s], banks(2 * s), b.unsqueeze(2).broadcast_to([P, 2, T]), ALU.add).then_inc(banks_free[s], 1)
            post("mixer1_post", 1.0)
            ffn(3)


def stream_of(a):
    out = np.zeros((SLABS, P, SLAB), np.float32)

    def put(name, w, width=256, tiles=None):
        kt = w.shape[0] // P
        v = w.reshape(kt, P, w.shape[1] // width, width).transpose(2, 1, 0, 3)
        n = FIRST[name]
        out[n:n + v.shape[0], :, 0:kt * width] = v.reshape(v.shape[0], P, kt * width)

    w_in = a["w_in"][0]
    put("convqkv", np.concatenate([w_in[:, 1536:3072], w_in[:, 0:1536]], 1))
    put("gates", w_in[:, 3072:5120])
    put("attn_branch", a["w_attn_branch"][0], 512)
    put("conv_branch", a["w_conv_branch"][0], 512)
    put("w_o", a["w_o"][0])
    for cn in range(4):
        put(f"mlp_in{cn}", a["w_mlp_in"][0][:, 1024 * cn:1024 * cn + 1024])
        put(f"mlp_out{cn}", a["w_mlp_out"][0][1024 * cn:1024 * cn + 1024])
    for f in range(4):
        wi, wo = a["ffn_w_in_2"][f // 2, f % 2], a["ffn_w_out_2"][f // 2, f % 2]
        t0 = 0
        for cn, n in enumerate(FFN_CHUNKS):
            g = wi[:, P * t0:P * (t0 + n)].reshape(D, n // 2, 256)
            u = wi[:, 2816 + P * t0:2816 + P * (t0 + n)].reshape(D, n // 2, 256)
            put(f"ffn{f}_in{cn}", np.stack([g, u], 2).reshape(D, n * 256))
            put(f"ffn{f}_out{cn}", wo[P * t0:P * (t0 + n)])
            t0 += n
    put("lora", np.concatenate([a["rwkv_w1_2"][0], a["rwkv_a1_2"][0], a["rwkv_g1_2"][0]], 1))
    n = FIRST["lora"] + 1
    out[n, 0:64, 0:1024], out[n, 64:128, 0:1024] = a["rwkv_w2_2"][0], a["rwkv_a2_2"][0]
    out[n, :, 1024:2048] = a["rwkv_g2_2"][0]
    for name, j in (("r", 0), ("k", 1), ("v", 2)):
        put(name, a["rwkv_w_rkv_2"][0, j])
    put("rwkv_o", a["rwkv_w_o_2"][0])
    put("kv", a["w_kv_2"])
    put("q2", a["attn_w_q_2"][0].reshape(D, 16, 64)[:, HEADS].reshape(D, D))
    put("o2", a["attn_w_o_2"][0].reshape(16, 64, D)[HEADS].reshape(D, D))
    return out


HEADS = [8 * (n // 8) + 4 * (n % 2) + (n % 8) // 2 for n in range(16)]


def vectors_of(a):
    rows = {"norm1_g": a["norm1_g"], "norm2_g": a["norm2_g"], "kv_norm_g": a["kv_norm_g_2"], "b_kv": a["b_kv_2"],
            "w0": a["rwkv_w0_2"], "a0": a["rwkv_a0_2"], "k_k": a["rwkv_k_k_2"], "k_a": a["rwkv_k_a_2"],
            "r_k": a["rwkv_r_k_2"], "gn_g": a["rwkv_gn_g_2"], "gn_b": a["rwkv_gn_b_2"], "b_o": a["attn_b_o_2"],
            "b_q": a["attn_b_q_2"].reshape(16, 64)[HEADS], "conv_w": a["conv_w"],
            "q_norm_g": np.concatenate([a["q_norm_g"]] * 2), "k_norm_g": np.concatenate([a["k_norm_g"]] * 2)}
    for i in range(12):
        rows[f"norm_g{i}"] = a["norm_g_2"][i // 6, i % 6]
    for i in range(6):
        rows[f"mu{i}"] = a["rwkv_mu_2"][0, i]
    return np.ascontiguousarray(np.concatenate([np.reshape(rows[n], (-1, P)) for n in VEC]).T)


def kernel(**inputs):
    import concourse.bacc as bacc
    from concourse.bass_utils import run_bass_kernel_spmd as run

    a = {k: np.asarray(v) for k, v in inputs.items()}
    mask, rel_r, rel_c = na_tables()
    rpb = a["rpb"][0]
    bias = np.stack([rpb[:, rel_r, rel_c[:, n, :]] for n in range(3)], 2).transpose(1, 0, 2, 3)
    consts = constants()
    consts[:, NCST - 16:] = a["attn_sinks_2"][0][HEADS][None, :]
    arrays = {
        "x_in": np.ascontiguousarray(a["x"][0].T.reshape(NT, P, T).transpose(1, 0, 2)),
        "stream": stream_of(a), "vec_in": vectors_of(a), "cst_in": consts, "spread_in": spread_rows(),
        "restart_in": scan_restart(), "bias_in": np.ascontiguousarray(bias.reshape(P, 12, T)), "mask_in": mask.reshape(P, 768),
        "swa_in": swa_masks(),
    }
    nc = bacc.Bacc("TRN2", target_bir_lowering=False, num_devices=1)
    aps = {n: nc.dram_tensor(n, v.shape, mybir.dt.from_np(v.dtype), kind="ExternalInput").ap() for n, v in arrays.items()}
    x_out = nc.dram_tensor("x_out", (P, NT, T), F32, kind="ExternalOutput").ap()
    build(nc, x_out=x_out, **aps)
    r = run(nc, [arrays], core_ids=[0])
    out = r.results[0]["x_out"]
    return np.ascontiguousarray(out.transpose(1, 0, 2).reshape(D, T).T)[None]
```
